# Optimizing a Trainium2 kernel written in Bass

```python
import math
import jax, jax.numpy as jnp
from jax import lax
import numpy as np

D_MODEL = 1024
BATCH = 1
SEQ = 256
DEPTH = 1

PLE_DIM = 256
HEAD_DIM = 64
NSA_HEADS = 8
NSA_KV_GROUPS = 2
NSA_GROUP_SIZE = NSA_HEADS // NSA_KV_GROUPS
NSA_CMP_LEN = 32
NSA_CMP_STRIDE = 16
NSA_SLC_BLOCK = 64
NSA_SLC_TOPK = 16
NSA_LOCAL_BLOCKS = 2
NSA_WINDOW = 512
DSA_HEADS = 8
IDX_HEADS = 8
IDX_DIM = 32
DSA_TOPK_MAX = 256
Q_BLOCK = 128
REL_BUCKETS = 32
REL_MAX_EXACT = 16
REL_MAX_DIST = 128
N_EXPERTS = 32
TOP_K = 4
D_FF = 1024
SWIGLU_LIMIT = 7.0
SWIGLU_ALPHA = 1.702
MOE_ROWS = 256
EPS = 1e-6
NEG_INF = -1e30

NSA_W = NSA_HEADS * HEAD_DIM
DSA_W = DSA_HEADS * HEAD_DIM
IN_SPLITS = (NSA_W, 6 * NSA_KV_GROUPS * HEAD_DIM, 3 * NSA_HEADS, DSA_W, DSA_W, DSA_W,
             IDX_HEADS * IDX_DIM, IDX_DIM, IDX_HEADS, D_MODEL, D_MODEL)
D_IN = sum(IN_SPLITS)

kernel_name = "hybrid_nsa_dsa_moe_block"

def rmsnorm(x, g):
    xf = x.astype(jnp.float32)
    y = xf * lax.rsqrt(jnp.mean(xf * xf, axis=-1, keepdims=True) + EPS)
    return (y * g.astype(jnp.float32)).astype(x.dtype)

def rel_bucket(dist):
    n = jnp.maximum(dist, 0)
    nf = jnp.maximum(n, 1).astype(jnp.float32)
    large = REL_MAX_EXACT + (jnp.log(nf / REL_MAX_EXACT) / math.log(REL_MAX_DIST / REL_MAX_EXACT)
                             * (REL_BUCKETS - REL_MAX_EXACT)).astype(jnp.int32)
    large = jnp.minimum(large, REL_BUCKETS - 1)
    return jnp.where(n < REL_MAX_EXACT, n, large)

def masked_softmax(logits, mask):
    logits = jnp.where(mask, logits.astype(jnp.float32), NEG_INF)
    m = jnp.max(logits, axis=-1, keepdims=True)
    e = jnp.where(mask, jnp.exp(logits - m), 0.0)
    return e / jnp.maximum(jnp.sum(e, axis=-1, keepdims=True), 1e-30)

def split_cols(z, sizes):
    out, o = [], 0
    for s in sizes:
        out.append(z[..., o:o + s])
        o += s
    return out

def nsa_mixer(q, kv, gate_logits, pe_ck, w_ck1, w_ck2, pe_cv, w_cv1, w_cv2, g_q, g_k, rel_tab):
    B, S, _ = q.shape
    G, R, dh = NSA_KV_GROUPS, NSA_GROUP_SIZE, HEAD_DIM
    q = rmsnorm(q.reshape(B, S, G, R, dh), g_q) * (dh ** -0.5)
    kv = kv.reshape(B, S, 6, G, dh)
    k_cmp_raw, v_cmp_raw, k_slc, v_slc, k_win, v_win = [kv[:, :, j] for j in range(6)]

    n_cmp = (S - NSA_CMP_LEN) // NSA_CMP_STRIDE + 1
    cmp_start = jnp.arange(n_cmp) * NSA_CMP_STRIDE
    cmp_tok = cmp_start[:, None] + jnp.arange(NSA_CMP_LEN)[None, :]
    cmp_end = cmp_start + NSA_CMP_LEN - 1

    def compress(z, pe, w1, w2):
        zb = z[:, cmp_tok] + pe[None, None, :, None, :]
        hdn = jax.nn.silu(jnp.einsum('bclgd,lde->bcge', zb, w1))
        return jnp.einsum('bcge,ed->bcgd', hdn, w2)

    k_cmp = rmsnorm(compress(k_cmp_raw, pe_ck, w_ck1, w_ck2), g_k)
    v_cmp = compress(v_cmp_raw, pe_cv, w_cv1, w_cv2)

    n_slc = S // NSA_SLC_BLOCK
    slc_start = jnp.arange(n_slc) * NSA_SLC_BLOCK
    overlap = jnp.maximum(
        jnp.minimum(cmp_start[:, None] + NSA_CMP_LEN, slc_start[None, :] + NSA_SLC_BLOCK)
        - jnp.maximum(cmp_start[:, None], slc_start[None, :]), 0).astype(jnp.float32) / NSA_CMP_LEN
    n_sel = min(NSA_SLC_TOPK, n_slc)
    n_ar = jnp.arange(n_slc)

    k_slc = rmsnorm(k_slc, g_k).transpose(0, 2, 1, 3)
    v_slc = v_slc.transpose(0, 2, 1, 3)
    pad = ((0, 0), (0, 0), (NSA_WINDOW, 0), (0, 0))
    k_win = jnp.pad(rmsnorm(k_win, g_k).transpose(0, 2, 1, 3), pad)
    v_win = jnp.pad(v_win.transpose(0, 2, 1, 3), pad)
    gates = jax.nn.sigmoid(gate_logits.astype(jnp.float32)).astype(q.dtype).reshape(B, S, G, R, 3)

    tab = rel_tab.reshape(REL_BUCKETS, G, R).transpose(1, 2, 0)
    b_ix = jnp.arange(B)[:, None, None, None]
    g_ix = jnp.arange(G)[None, :, None, None]
    g5 = jnp.arange(G)[None, :, None, None, None]
    r5 = jnp.arange(R)[None, None, :, None, None]

    def block(blk):
        t0 = blk * Q_BLOCK
        t = t0 + jnp.arange(Q_BLOCK)
        qb = lax.dynamic_slice_in_dim(q, t0, Q_BLOCK, axis=1)
        gb = lax.dynamic_slice_in_dim(gates, t0, Q_BLOCK, axis=1)

        mask_c = cmp_end[None, :] <= t[:, None]
        lc = (jnp.einsum('btgrd,bcgd->bgrtc', qb, k_cmp).astype(jnp.float32)
              + tab[:, :, rel_bucket(t[:, None] - cmp_end[None, :])])
        pc = masked_softmax(lc, mask_c)
        o_c = jnp.einsum('bgrtc,bcgd->btgrd', pc.astype(v_cmp.dtype), v_cmp)

        imp = jnp.einsum('bgrtc,cn->bgtn', pc, overlap)
        cur = t // NSA_SLC_BLOCK
        valid = slc_start[None, :] <= t[:, None]
        forced = valid & ((n_ar[None, :] == 0) | (n_ar[None, :] > cur[:, None] - NSA_LOCAL_BLOCKS))
        score = jnp.where(forced, jnp.inf, jnp.where(valid, imp, -jnp.inf))
        _, sel = lax.top_k(score, n_sel)
        tok = (sel[..., None] * NSA_SLC_BLOCK + jnp.arange(NSA_SLC_BLOCK)).reshape(
            B, G, Q_BLOCK, n_sel * NSA_SLC_BLOCK)
        ks = k_slc[b_ix, g_ix, tok]
        vs = v_slc[b_ix, g_ix, tok]
        ls = (jnp.einsum('btgrd,bgtkd->bgrtk', qb, ks).astype(jnp.float32)
              + tab[g5, r5, rel_bucket(t[:, None] - tok)[:, :, None]])
        ps = masked_softmax(ls, (tok <= t[:, None])[:, :, None])
        o_s = jnp.einsum('bgrtk,bgtkd->btgrd', ps.astype(vs.dtype), vs)

        kw = lax.dynamic_slice_in_dim(k_win, t0, Q_BLOCK + NSA_WINDOW, axis=2)
        vw = lax.dynamic_slice_in_dim(v_win, t0, Q_BLOCK + NSA_WINDOW, axis=2)
        s = t0 - NSA_WINDOW + jnp.arange(Q_BLOCK + NSA_WINDOW)
        d = t[:, None] - s[None, :]
        mask_w = (d >= 0) & (d < NSA_WINDOW) & (s[None, :] >= 0)
        lw = jnp.einsum('btgrd,bgsd->bgrts', qb, kw).astype(jnp.float32) + tab[:, :, rel_bucket(d)]
        pw = masked_softmax(lw, mask_w)
        o_w = jnp.einsum('bgrts,bgsd->btgrd', pw.astype(vw.dtype), vw)

        o = gb[..., 0:1] * o_c + gb[..., 1:2] * o_s + gb[..., 2:3] * o_w
        return o.reshape(B, Q_BLOCK, NSA_W)

    out = lax.map(block, jnp.arange(S // Q_BLOCK))
    return out.transpose(1, 0, 2, 3).reshape(B, S, NSA_W)

def dsa_mixer(q, k, v, iq, ik, iw, g_q, g_k, rel_tab):
    B, S, _ = q.shape
    H, dh = DSA_HEADS, HEAD_DIM
    q = rmsnorm(q.reshape(B, S, H, dh), g_q) * (dh ** -0.5)
    k = rmsnorm(k.reshape(B, S, H, dh), g_k)
    v = v.reshape(B, S, H, dh)
    iq = iq.reshape(B, S, IDX_HEADS, IDX_DIM) * (IDX_DIM ** -0.5)
    iw = iw * (IDX_HEADS ** -0.5)
    n_keep = min(DSA_TOPK_MAX, S // 4)
    s_ar = jnp.arange(S)
    b_ix = jnp.arange(B)[:, None, None]

    def block(blk):
        t0 = blk * Q_BLOCK
        t = t0 + jnp.arange(Q_BLOCK)
        qi = lax.dynamic_slice_in_dim(iq, t0, Q_BLOCK, axis=1)
        wi = lax.dynamic_slice_in_dim(iw, t0, Q_BLOCK, axis=1)
        idx_score = jnp.einsum('bth,bths->bts', wi.astype(jnp.float32),
                               jax.nn.relu(jnp.einsum('bthd,bsd->bths', qi, ik).astype(jnp.float32)))
        idx_score = jnp.where(s_ar[None, :] <= t[:, None], idx_score, -jnp.inf)
        _, sel = lax.top_k(idx_score, n_keep)
        kg = k[b_ix, sel]
        vg = v[b_ix, sel]
        qb = lax.dynamic_slice_in_dim(q, t0, Q_BLOCK, axis=1)
        dist = t[:, None] - sel
        logits = (jnp.einsum('bthd,btkhd->bhtk', qb, kg).astype(jnp.float32)
                  + jnp.moveaxis(rel_tab[rel_bucket(dist)], -1, 1))
        pr = masked_softmax(logits, (dist >= 0)[:, None])
        o = jnp.einsum('bhtk,btkhd->bthd', pr.astype(vg.dtype), vg)
        return o.reshape(B, Q_BLOCK, DSA_W)

    out = lax.map(block, jnp.arange(S // Q_BLOCK))
    return out.transpose(1, 0, 2, 3).reshape(B, S, DSA_W)

def moe_ffn(h, w_r, b_r, w1, b1, w2, b2):
    B, S, D = h.shape
    N = B * S
    hf = h.reshape(N, D)
    logits = (hf @ w_r + b_r).astype(jnp.float32)
    top_val, top_idx = lax.top_k(logits, TOP_K)
    top_w = jax.nn.softmax(top_val, axis=-1)
    e_flat = top_idx.reshape(-1)
    tok_flat = jnp.repeat(jnp.arange(N, dtype=jnp.int32), TOP_K)
    w_flat = top_w.reshape(-1)
    order = jnp.argsort(e_flat)
    e_sorted, tok_sorted, w_sorted = e_flat[order], tok_flat[order], w_flat[order]
    counts = jnp.bincount(e_flat, length=N_EXPERTS)
    padded = (counts + MOE_ROWS - 1) // MOE_ROWS * MOE_ROWS
    pad_end = jnp.cumsum(padded)
    pad_start = pad_end - padded
    start = jnp.cumsum(counts) - counts
    dest = pad_start[e_sorted] + jnp.arange(N * TOP_K) - start[e_sorted]
    n_chunks = -(-(N * TOP_K) // MOE_ROWS) + N_EXPERTS
    P = n_chunks * MOE_ROWS
    row_tok = jnp.full((P,), N, jnp.int32).at[dest].set(tok_sorted)
    row_w = jnp.zeros((P,), jnp.float32).at[dest].set(w_sorted)
    chunk_e = jnp.minimum(jnp.searchsorted(pad_end, jnp.arange(n_chunks) * MOE_ROWS, side='right'),
                          N_EXPERTS - 1)
    h_pad = jnp.concatenate([hf, jnp.zeros((1, D), hf.dtype)], axis=0)

    def expert_rows(args):
        tok, e = args
        xe = h_pad[tok]
        gu = xe @ w1[e] + b1[e]
        gate = jnp.minimum(gu[:, :D_FF], SWIGLU_LIMIT)
        lin = jnp.clip(gu[:, D_FF:], -SWIGLU_LIMIT, SWIGLU_LIMIT)
        act = (lin + 1) * gate * jax.nn.sigmoid(SWIGLU_ALPHA * gate)
        return act @ w2[e] + b2[e]

    rows = lax.map(expert_rows, (row_tok.reshape(n_chunks, MOE_ROWS), chunk_e))
    rows = rows.reshape(P, D) * row_w[:, None].astype(rows.dtype)
    y = jax.ops.segment_sum(rows, row_tok, num_segments=N + 1)[:N]
    return y.reshape(B, S, D)

def setup_inputs(seed: int = 0) -> dict:
    key = jax.random.key(seed)
    ks = jax.random.split(key, 32)
    f32 = jnp.float32

    def nrm(k, shape, fan_in):
        return jax.random.normal(k, shape, f32) * (fan_in ** -0.5)

    def gain(k, shape):
        return 1.0 + 0.1 * jax.random.normal(k, shape, f32)

    L, dh = DEPTH, HEAD_DIM
    return {
        "x": jax.random.normal(ks[0], (BATCH, SEQ, D_MODEL), f32),
        "p": jax.random.normal(ks[1], (DEPTH, BATCH, SEQ, PLE_DIM), f32),
        "w_in": nrm(ks[2], (L, D_MODEL, D_IN), D_MODEL),
        "g_mix": gain(ks[3], (L, D_MODEL)),
        "g_q_nsa": gain(ks[4], (L, dh)),
        "g_k_nsa": gain(ks[5], (L, dh)),
        "g_q_dsa": gain(ks[6], (L, dh)),
        "g_k_dsa": gain(ks[7], (L, dh)),
        "pe_ck": 0.5 * jax.random.normal(ks[8], (L, NSA_CMP_LEN, dh), f32),
        "w_ck1": nrm(ks[9], (L, NSA_CMP_LEN, dh, dh), NSA_CMP_LEN * dh),
        "w_ck2": nrm(ks[10], (L, dh, dh), dh),
        "pe_cv": 0.5 * jax.random.normal(ks[11], (L, NSA_CMP_LEN, dh), f32),
        "w_cv1": nrm(ks[12], (L, NSA_CMP_LEN, dh, dh), NSA_CMP_LEN * dh),
        "w_cv2": nrm(ks[13], (L, dh, dh), dh),
        "w_branch_a": nrm(ks[14], (L, NSA_W, D_MODEL), NSA_W),
        "w_branch_b": nrm(ks[15], (L, DSA_W, D_MODEL), DSA_W),
        "w_out": nrm(ks[16], (L, D_MODEL, D_MODEL), D_MODEL),
        "rel_bias": 0.5 * jax.random.normal(ks[17], (REL_BUCKETS, NSA_HEADS + DSA_HEADS), f32),
        "g_ffn": gain(ks[18], (L, D_MODEL)),
        "w_router": nrm(ks[19], (L, D_MODEL, N_EXPERTS), D_MODEL),
        "b_router": 0.01 * jax.random.normal(ks[20], (L, N_EXPERTS), f32),
        "w_e1": nrm(ks[21], (L, N_EXPERTS, D_MODEL, 2 * D_FF), D_MODEL),
        "b_e1": 0.01 * jax.random.normal(ks[22], (L, N_EXPERTS, 2 * D_FF), f32),
        "w_e2": nrm(ks[23], (L, N_EXPERTS, D_FF, D_MODEL), D_FF),
        "b_e2": 0.01 * jax.random.normal(ks[24], (L, N_EXPERTS, D_MODEL), f32),
        "g_ple": gain(ks[25], (L, D_MODEL)),
        "w_ple": nrm(ks[26], (L, PLE_DIM, D_MODEL), PLE_DIM),
        "w_ple_gate": nrm(ks[27], (L, D_MODEL, D_MODEL), D_MODEL),
    }

def reference(x, p, w_in, g_mix, g_q_nsa, g_k_nsa, g_q_dsa, g_k_dsa, pe_ck, w_ck1, w_ck2,
              pe_cv, w_cv1, w_cv2, w_branch_a, w_branch_b, w_out, rel_bias, g_ffn, w_router,
              b_router, w_e1, b_e1, w_e2, b_e2, g_ple, w_ple, w_ple_gate):
    rel_nsa = rel_bias[:, :NSA_HEADS]
    rel_dsa = rel_bias[:, NSA_HEADS:]
    for i in range(DEPTH):
        h = rmsnorm(x, g_mix[i])
        z = h @ w_in[i]
        nq, nkv, ngate, dq, dk, dv, iq, ik, iw, ga, gb = split_cols(z, IN_SPLITS)
        o_a = nsa_mixer(nq, nkv, ngate, pe_ck[i], w_ck1[i], w_ck2[i], pe_cv[i], w_cv1[i], w_cv2[i],
                        g_q_nsa[i], g_k_nsa[i], rel_nsa)
        o_b = dsa_mixer(dq, dk, dv, iq, ik, iw, g_q_dsa[i], g_k_dsa[i], rel_dsa)
        merged = (jax.nn.sigmoid(ga) * (o_a @ w_branch_a[i])
                  + jax.nn.sigmoid(gb) * (o_b @ w_branch_b[i]))
        x = x + merged @ w_out[i]
        x = x + moe_ffn(rmsnorm(x, g_ffn[i]), w_router[i], b_router[i],
                        w_e1[i], b_e1[i], w_e2[i], b_e2[i])
        x = x + jax.nn.sigmoid(rmsnorm(x, g_ple[i]) @ w_ple_gate[i]) * (p[i] @ w_ple[i])
    return x


_drawn_inputs = setup_inputs


def setup_inputs(seed=0):
    import zlib

    import numpy as np

    out = dict(_drawn_inputs(seed))
    spreads = {}
    factors = {'b_router': 2.967, 'b_e1': 8.0, 'b_e2': 8.0, 'g_ple': 3.34}
    for name, (base, spread) in spreads.items():
        noise = np.random.default_rng([zlib.crc32(name.encode()), seed]).standard_normal(out[name].shape)
        drawn = base * np.exp(spread * noise) if base else spread * noise
        out[name] = __import__('jax').numpy.asarray(drawn.astype(out[name].dtype))
    for name, factor in factors.items():
        out[name] = (out[name] * factor).astype(out[name].dtype)
    return out
```

```python
import math
from contextlib import ExitStack

import numpy as np
import concourse.bass as bass
from concourse import mybir

F32 = mybir.dt.float32
BF16 = mybir.dt.bfloat16
I32 = mybir.dt.int32
ALU = mybir.AluOpType
ACT = mybir.ActivationFunctionType
AX = mybir.AxisListType

P = 128
SEQ, DM = 256, 1024
TT = SEQ // P
KT = DM // P
DH, HEADS, GROUPS, HPG = 64, 8, 2, 4
CMP_LEN, CMP_STRIDE = 32, 16
NCMP = (SEQ - CMP_LEN) // CMP_STRIDE + 1
CMP_SEEN = [(P * (t + 1) - CMP_LEN) // CMP_STRIDE + 1 for t in range(TT)]
IH, ID = 8, 32
KEEP = 64
BUCKETS, MAX_EXACT, MAX_DIST = 32, 16, 128
NE, TOPK, DFF = 32, 4, 1024
LIMIT, ALPHA = 7.0, 1.702
EPS = 1e-6
NEG = -1e30
BLOCKED, TAKEN = -3e38, -3.4e38
PLE = 256
SLOTS = 64
ROUNDS = SEQ // SLOTS
PIECES = 12
UP = 8

O_NQ, O_KV, O_NG, O_DQ, O_DK, O_DV, O_IQ, O_IK, O_IW, O_GA = 0, 512, 1280, 1304, 1816, 2328, 2840, 3096, 3128, 3136
ZW = O_GA
CHUNKS = [(O_IQ, O_GA - O_IQ), (O_DQ, 512), (O_DK, 512), (O_NQ, 512), (O_KV, 512), (O_KV + 512, O_DQ - O_KV - 512),
          (O_DV, 512), (O_GA, 512), (O_GA + 512, 512), (O_GA + 1024, 512), (O_GA + 1536, 512)]
NZ = len(CHUNKS)
C_IX, C_DQ, C_DK, C_NQ, C_N1, C_N2, C_DV, C_G = range(8)

ORDER = ["T:G", "T:X0", "T:X1", "T:X2", "T:X3", "Z0", "Z1", "T:IX0", "T:IX1", "Z2", "I", "T:DQ0", "T:DQ1", "Z3",
         "T:DK0", "T:DK1", "Z4", "T:NQ0", "T:NQ1", "Z5", "Z6", "T:K0", "T:K1", "T:PE", "Z7", "HID", "Z8", "CMPKV", "Z9",
         "T:KC", "Z10", "CSC"]
TJOBS = [x for x in ORDER if x.startswith("T:")] + ["T:C0", "T:C1"]
NTJ = len(TJOBS)
UNITS = [("dsa", t, j) for t in (0, 1) for j in range(4)] + [(b, t, j) for t in (0, 1) for j in range(4) for b in ("slc", "win")]
NU = len(UNITS)
NITEM = 16


def item_of(u):
    return u if u < 8 else 8 + (u - 8) // 2


def block_kernel(nc, io, out):
    ctx = ExitStack()
    with ctx:
        def sb(name, words):
            return ctx.enter_context(nc.sbuf_tensor(name, [P, words], F32))

        def sem(name):
            return ctx.enter_context(nc.semaphore(name))

        ring = sb("ring", PIECES * 2048)
        wbuf = sb("wbuf", 4 * 4096)
        xres = sb("xres", TT * DM)
        hT = sb("hT", KT * SEQ)
        gat = sb("gat", TT * 2 * DM)
        oT = sb("oT", 2 * 4 * SEQ)
        misc = sb("misc", 2000)
        ps = [ctx.enter_context(nc.psum_tensor(f"ps{b}", [P, 512], F32)) for b in range(8)]

        class Take:
            def __init__(self, t, at=0):
                self.t, self.at = t, at

            def __call__(self, *shape, parts=P, dt=F32):
                n = int(np.prod(shape))
                words = n if dt != BF16 else (n + 1) // 2
                ap = self.t[0:parts, self.at:self.at + words]
                self.at += words
                if dt != F32:
                    ap = ap.bitcast(dt)
                if len(shape) == 2:
                    ap = ap.rearrange("p (a b) -> p a b", a=shape[0])
                if len(shape) == 3:
                    ap = ap.rearrange("p (a b c) -> p a b c", a=shape[0], b=shape[1])
                assert self.at <= self.t.shape[1], (self.at, self.t.shape)
                return ap

        def bc(ap, n):
            return ap.unsqueeze(len(ap.shape)).to_broadcast(list(ap.shape) + [n])

        def bm(ap, n):
            s = list(ap.shape)
            return ap.unsqueeze(1).to_broadcast([s[0], n] + s[1:])

        m = Take(misc)
        ident, tri, ones, iota1 = m(128), m(128), m(128), m(2, 64)
        idmod = m(NE)
        gT = m(24)
        gqk = m(4, DH)
        wr, br = m(KT, NE), m(NE)
        rs, ssx = m(2), m(2)
        half = m(64)
        Mt = m(TT, NE)
        top8, nt, e4, lg = m(TT, 8), m(TT), m(TT, 4), m(TT, NE)
        idx8 = m(TT, 8, dt=mybir.dt.uint32)
        idxf = m(TT, 8)
        sm2, cnt, cmax = m(TT, 2), m(NE), m(1)
        cmaxi = m(1, dt=I32)
        sel = m(SLOTS, parts=96, dt=BF16)
        S = m(TT, SLOTS, dt=BF16)

        w = Take(ring)
        z = w(TT, ZW)
        bias = w(16, SEQ)
        xn = w(TT, DM)
        ikZ, rl = xn[:, 0, :].rearrange("p (a b) -> p a b", a=4), xn[:, 1, :].rearrange("p (a b) -> p a b", a=2)
        qaT, qdT = w(4, SEQ), w(4, SEQ)
        kZs, kZw = w(2, SEQ), w(2, SEQ)
        kZd = w(4, 2, SEQ)
        iqT = w(2, SEQ)
        rawT = w(2, SEQ)
        zb = xn[:, 1, :].rearrange("p (a l c) -> p a l c", a=2, l=CMP_LEN)
        score, selm = w(TT, SEQ), w(TT, SEQ)
        sq, qn = w(TT, 512), w(TT, 512)
        PT = w(2, 4, P)
        Bd = w(2, SEQ)
        work_small = Take(ring, w.at)
        V4 = work_small(2, 4, DH)
        kcZ = work_small(2, 16)
        kcs = work_small(2, DH, parts=16)
        kcq = work_small(2, DH, parts=16)
        hid, hsg = work_small(2, 16), work_small(2, 16)
        hid4 = work_small(4, 32)
        peT = work_small(2, CMP_LEN)
        m8 = work_small(8)
        iwS = work_small(TT, IH)
        gsig = work_small(TT, 24)
        v16 = work_small(TT, 8)
        r16 = work_small(TT, 8)
        mx, nmx, ssum, rcp = (work_small(4, 2) for _ in range(4))
        ckr = work_small(4)
        ck2w = work_small(2, DH)
        g0 = Take(gat)
        pe_in = g0(4, DH, parts=CMP_LEN)
        grow = g0(P, parts=24)
        tab, onehot, erow = g0(16, parts=BUCKETS + 1), g0(384, parts=BUCKETS + 1), g0(384, parts=16)
        ot0 = Take(oT)
        P32 = ot0(TT, 8, 32)
        PcT = sq.rearrange("p t (g c) -> p t g c", g=4)[:, :, 0:2, :]
        cL, cst, ck2 = ot0(8, 16), ot0(4, 8), ot0(2, DH)
        wck1 = wbuf[:, 3 * 4096:4 * 4096].rearrange("p (a l e) -> p a l e", a=2, l=CMP_LEN)
        L = hT[:, :].rearrange("p (b h s) -> p b h s", b=4, h=2)
        hTv = hT[:, :].rearrange("p (k t) -> p k t", k=KT)
        x = xres[:, :].rearrange("p (t d) -> p t d", t=TT)
        gates = gat[:, :].rearrange("p (t n) -> p t n", t=TT)
        oTv = oT[:, :].rearrange("p (m j t) -> p m j t", m=2, j=4)
        wa = wbuf[:, 0:4096].rearrange("p (j n) -> p j n", j=4)
        wb = wbuf[:, 4096:8192].rearrange("p (j n) -> p j n", j=4)
        wo = wbuf[:, 8192:16384].rearrange("p (k n) -> p k n", k=KT)
        merged, mtmp = xn, sq
        wple_g = wbuf[:, 0:8192].rearrange("p (k n) -> p k n", k=KT)
        wple = wbuf[:, 8192:10240].rearrange("p (k n) -> p k n", k=2)
        v = Take(wbuf, 10240)
        xeT = v(KT, SLOTS)
        gc, sg, lin, act, actT, oe = v(512), v(512), v(512), v(512), v(4, P), v(512)
        wS, wST = v(TT, P), v(TT * P)
        selx = v(8)
        rank = v(TT, ROUNDS * NE + 1)
        Wt = v(TT, ROUNDS * NE)
        be2, WT = oT[0:NE, 1024:2048], v(SEQ, parts=NE)
        hp = gat[:, 0:3072].bitcast(BF16).rearrange("p (q t d) -> p q t d", q=3, t=TT)
        b1p = gat[0:96, 3072:4096].bitcast(BF16)
        b1f = oT[0:96, :]
        xh = xn
        pin, pT = oT[:, 0:512].rearrange("p (t d) -> p t d", t=TT), oT[:, 512:1024].rearrange("p (k t) -> p k t", k=2)
        xn3, sgate, xout = xn, sq, x
        ring3 = ring[:, :].rearrange("p (i n) -> p i n", i=PIECES)

        ERW = 384
        er_dram = nc.dram_tensor("rel_rows", [16, ERW], F32).ap()
        er_rep = nc.dram_tensor("rel_rows_repeated", [16, P, ERW], F32).ap()

        ld_const, ld_x, ld_small, ld_tab, ld_ck = sem("ld_const"), sem("ld_x"), sem("ld_small"), sem("ld_tab"), sem("ld_ck")
        ld_w = [sem(f"ld_w{i}") for i in range(3)]
        ld_wab, ld_wo, ld_bias, st_er, st_rep, ld_route, ld_b1, ld_be2, ld_p, ld_ple = (
            sem(n) for n in ("ld_wab", "ld_wo", "ld_bias", "st_er", "st_rep", "ld_route", "ld_b1", "ld_be2", "ld_p", "ld_ple"))
        piece = [sem(f"piece{i}") for i in range(PIECES)]
        zeroed, x_sq, x_rs, xn_ready, t_ps, t_ev, z_ps, z_ev = (
            sem(n) for n in ("zeroed", "x_sq", "x_rs", "xn_ready", "t_ps", "t_ev", "z_ps", "z_ev"))
        ikrep_ready, i_ps, i_rl, i_used, score_cut, selm_ready = (
            sem(n) for n in ("ikrep_ready", "i_ps", "i_rl", "i_used", "score_cut", "selm_ready"))
        n_var, n_rs, qn_ready = sem("n_var"), sem("n_rs"), sem("qn_ready")
        er_ps, er_sb = sem("er_ps"), sem("er_sb")
        zb_ready, h_ps, h_exp, hid_ready, kc_ps, kc_copied, v4_ready, kcn_ready = (
            sem(n) for n in ("zb_ready", "h_ps", "h_exp", "hid_ready", "kc_ps", "kc_copied", "v4_ready", "kcn_ready"))
        c_ps, c_log, c_exp, c_ready = sem("c_ps"), sem("c_log"), sem("c_exp"), sem("c_ready")
        s_ps, s_log, s_exp, s_prob, bd_ready, o_ps, o_ev = (
            sem(n) for n in ("s_ps", "s_log", "s_exp", "s_prob", "bd_ready", "o_ps", "o_ev"))
        pr_ps, pr_used, mg_ready, wo_ps, x2_ready, f_sq, f_rs, xh_ready = (
            sem(n) for n in ("pr_ps", "pr_used", "mg_ready", "wo_ps", "x2_ready", "f_sq", "f_rs", "xh_ready"))
        rt_ps, lg_ready, rt_exp, m_ready, rk_ps, rank_ready, wt_ready, y_init, hp_ready, b1_ready, init0 = (
            sem(n) for n in ("rt_ps", "lg_ready", "rt_exp", "m_ready", "rk_ps", "rank_ready", "wt_ready", "y_init",
                             "hp_ready", "b1_ready", "init0"))
        dve_ch, pool_ch, act_ch = sem("dve_chain"), sem("pool_chain"), sem("act_chain")

        class Chain:
            def __init__(self, eng, s):
                self.eng, self.s, self.n = eng, s, 0

            def __call__(self, ins):
                self.n += 1
                ins.then_inc(self.s, 1)
                self.eng.wait_ge(self.s, self.n)

        NORMS = [("dq", O_DQ, 8, 2, DH ** -0.5), ("dk", O_DK, 8, 3, 1.0), ("nq", O_NQ, 8, 0, DH ** -0.5),
                 ("ks", O_KV + 256, 2, 1, 1.0), ("kw", O_KV + 512, 2, 1, 1.0)]
        NORM_CHUNK = [C_DQ, C_DK, C_NQ, C_N1, C_N2]

        def expert_sems(tag):
            names = ("pieces_used", "s_ready", "sel_ready", "xe_ps", "xe_ready", "gc_ready", "lin_ready", "glu_ready", "sig_ready",
                     "act_ready", "at_ps", "at_ready", "wst_ps", "ws_ready", "wst_ready", "out_ready")
            return {n: sem(f"{n}_{tag}") for n in names}

        y_done = sem("y_done")
        w1 = io["w_e1"][0].rearrange("e (k p) n -> e k p n", p=P)
        w2 = io["w_e2"][0].rearrange("e (q r p) n -> e q p r n", r=2, p=P)
        first = dict(s=expert_sems("a"), piece=piece, col=0, visits=NE)
        rest = dict(s=expert_sems("b"), piece=[sem(f"piece_b{i}") for i in range(PIECES)], col=NE, visits=(ROUNDS - 1) * NE)

        def load(eng, e, i, signal):
            if i < UP:
                eng.dma_start(ring3[:, i, :], w1[e, i]).then_inc(signal[i], 16)
            else:
                eng.dma_start(ring3[:, i, :].rearrange("p (r n) -> p r n", r=2), w2[e, i - UP]).then_inc(signal[i], 16)

        def expert_pe(te, a):
            s, col = a["s"], a["col"]
            mm, tr = nc.tensor.matmul, nc.tensor.transpose
            G, Lb, O, T = ps[0], ps[1], ps[2], ps[3]

            def gather():
                for k in range(KT):
                    for t in range(TT):
                        for q in range(3):
                            l = mm(O[:, k * SLOTS:(k + 1) * SLOTS], hp[:, q, t, k * P:(k + 1) * P], S[:, t, :],
                                   start=t == 0 and q == 0, stop=t == TT - 1 and q == 2)
                l.then_inc(s["xe_ps"], 1)

            def scatter():
                for t in range(TT):
                    for n in range(2):
                        h = slice(n * SLOTS, (n + 1) * SLOTS)
                        l = mm(ps[4 + 2 * t + n][:, :], wST[h, t * P:(t + 1) * P], oe[h, :], start=False, stop=False, skip_group_check=True)
                return l

            te.wait_ge(s["s_ready"], 1)
            gather()
            with te.Fori(0, a["visits"]) as it:
                te.wait_ge(s["sel_ready"], it + 1)
                te.wait_ge(s["xe_ready"], it + 1)
                for n in range(4):
                    mm((G, Lb)[n // 2][(n % 2) * SLOTS:(n % 2 + 1) * SLOTS, :], sel, b1p[:, n * 512:(n + 1) * 512], start=True, stop=False)
                for k in range(UP):
                    te.wait_ge(a["piece"][k], it * 16 + 16)
                    for n in range(4):
                        l = mm((G, Lb)[n // 2][(n % 2) * SLOTS:(n % 2 + 1) * SLOTS, :], xeT[:, k, :], ring3[:, k, n * 512:(n + 1) * 512],
                               start=False, stop=k == UP - 1)
                    l.then_inc(s["pieces_used"], 1)
                te.wait_ge(s["out_ready"], it + 1)
                te.wait_ge(s["wst_ready"], it + 1)
                scatter()
                te.wait_ge(s["ws_ready"], it + 1)
                for t in range(TT):
                    l = tr(T[:, t * P:(t + 1) * P], wS[:, t, :], ident)
                l.then_inc(s["wst_ps"], 1)
                te.wait_ge(s["s_ready"], it + 2)
                gather()
                te.wait_ge(s["wst_ready"], it + 2)
                te.wait_ge(s["act_ready"], it + 1)
                for j in range(4):
                    l = tr(T[:, j * P:(j + 1) * P], act[:, j * P:(j + 1) * P], ident)
                l.then_inc(s["at_ps"], 1)
                te.wait_ge(s["at_ready"], it + 1)
                te.wait_ge(s["xe_ready"], it + 2)
                for i in range(UP, PIECES):
                    te.wait_ge(a["piece"][i], it * 16 + 16)
                    for r in range(2):
                        kt = 2 * (i - UP) + r
                        for n in range(2):
                            l = mm(O[n * SLOTS:(n + 1) * SLOTS, :], actT[:, kt % 4, (kt // 4) * SLOTS:(kt // 4 + 1) * SLOTS],
                                   ring3[:, i, r * DM + n * 512:r * DM + (n + 1) * 512], start=kt == 0, stop=kt == 7)
                    l.then_inc(s["pieces_used"], 1)
            te.wait_ge(s["out_ready"], a["visits"] + 1)
            te.wait_ge(s["wst_ready"], a["visits"] + 1)
            scatter().then_inc(y_done, 1)

        def expert_act(sc, a):
            s = a["s"]
            with sc.Fori(0, a["visits"]) as it:
                sc.wait_ge(s["gc_ready"], it + 1)
                nc.scalar.activation(sg, gc, ACT.Sigmoid, scale=ALPHA).then_inc(s["sig_ready"], 1)
                sc.wait_ge(s["wst_ps"], it + 1)
                nc.scalar.copy(wST, ps[3][:, 0:TT * P]).then_inc(s["wst_ready"], 1)
                sc.wait_ge(s["at_ps"], it + 1)
                nc.scalar.copy(actT.rearrange("p j t -> p (j t)"), ps[3][:, :]).then_inc(s["at_ready"], 1)
                sc.wait_ge(s["pieces_used"], it * PIECES + PIECES)
                nc.scalar.copy(oe, ps[2][:, :]).then_inc(s["out_ready"], 1)

        def expert_dve(ve, a):
            s, col, d = a["s"], a["col"], nc.vector
            i1 = iota1[:, 0, :]

            def one_hot(c):
                for t in range(TT):
                    l = d.tensor_scalar(S[:, t, :], i1, rank[:, t, c], None, ALU.is_equal)
                l.then_inc(s["s_ready"], 1)

            def take_rows():
                d.tensor_tensor(xeT, ps[2][:, :].rearrange("p (k c) -> p k c", k=KT), bc(gT[:, 8:16], SLOTS), ALU.mult).then_inc(s["xe_ready"], 1)

            d.memset(oe, 0.0).then_inc(s["out_ready"], 1)
            d.memset(wST, 0.0).then_inc(s["wst_ready"], 1)
            one_hot(slice(col, col + 1))
            ve.wait_ge(s["xe_ps"], 1)
            take_rows()
            with ve.Fori(0, a["visits"]) as it:
                if a is first:
                    e = bass.ds(it, 1)
                else:
                    e = bass.ds(it % NE, 1)
                d.tensor_copy(sel, idmod[0:96, e].to_broadcast([96, SLOTS])).then_inc(s["sel_ready"], 1)
                one_hot(bass.ds(it + (col + 1), 1))
                for t in range(TT):
                    l = d.tensor_scalar(wS[:, t, :], iota1.rearrange("p a b -> p (a b)"), rank[:, t, bass.ds(it + col, 1)],
                                        Wt[:, t, bass.ds(it + col, 1)], ALU.is_equal, ALU.mult)
                l.then_inc(s["ws_ready"], 1)
                ve.wait_ge(s["pieces_used"], it * PIECES + UP)
                d.tensor_scalar(gc, ps[0][:, :], LIMIT, None, ALU.min).then_inc(s["gc_ready"], 1)
                d.tensor_scalar(lin, ps[1][:, :], LIMIT, -LIMIT, ALU.min, ALU.max).then_inc(s["lin_ready"], 1)
                ve.wait_ge(s["gc_ready"], it + 1)
                ve.wait_ge(s["lin_ready"], it + 1)
                d.scalar_tensor_tensor(lin, lin, 1.0, gc, ALU.add, ALU.mult).then_inc(s["glu_ready"], 1)
                ve.wait_ge(s["glu_ready"], it + 1)
                ve.wait_ge(s["sig_ready"], it + 1)
                d.tensor_tensor(act, lin, sg, ALU.mult).then_inc(s["act_ready"], 1)
                ve.wait_ge(s["xe_ps"], it + 2)
                take_rows()

        with nc.Block() as block:
            @block.sync
            def _(sp):
                sp.dma_start(x[:, :, :], io["x"][0].rearrange("(t p) d -> p t d", p=P)).then_inc(ld_x, 16)
                w_in = io["w_in"][0].rearrange("(k p) n -> p k n", p=P)
                for c, (o, n) in enumerate(CHUNKS):
                    if c >= 3:
                        sp.wait_ge(z_ps, 2 * (c - 2))
                    dst = wbuf[:, (c % 3) * 4096:(c % 3) * 4096 + KT * n].rearrange("p (k n) -> p k n", k=KT)
                    sp.dma_start(dst, w_in[:, :, o:o + n]).then_inc(ld_w[c % 3], 16)
                    if c == 2:
                        for a, name in enumerate(("w_ck1", "w_cv1")):
                            for g in range(2):
                                sp.dma_start(wck1[g * DH:(g + 1) * DH, a], io[name][0].rearrange("l d e -> d l e")).then_inc(ld_ck, 16)
                sp.wait_ge(z_ps, 2 * NZ)
                for g in range(2):
                    sp.dma_start(wa[g * DH:(g + 1) * DH], io["w_branch_a"][0].rearrange("(g j d) n -> g d j n", g=2, j=4)[g]).then_inc(ld_wab, 16)
                sp.dma_start(wb[:, :, :], io["w_branch_b"][0].rearrange("(j p) n -> p j n", p=P)).then_inc(ld_wab, 16)
                sp.wait_ge(h_ps, 1)
                sp.dma_start(wo[:, :, :], io["w_out"][0].rearrange("(k p) n -> p k n", p=P)).then_inc(ld_wo, 16)
                sp.wait_ge(pr_used, 4)
                for q in range(3):
                    sp.dma_start(b1f[q * NE:(q + 1) * NE, :], io["b_e1"][0]).then_inc(ld_b1, 16)
                sp.wait_ge(hp_ready, 1)
                for i in range(PIECES):
                    load(sp, 0, i, piece)
                sp.dma_start(wple_g, io["w_ple_gate"][0].rearrange("(k p) n -> p k n", p=P)).then_inc(ld_ple, 16)
                sp.dma_start(wple, io["w_ple"][0].rearrange("(k p) n -> p k n", p=P)).then_inc(ld_ple, 16)
                sp.wait_ge(b1_ready, 1)
                sp.dma_start(be2, io["b_e2"][0]).then_inc(ld_be2, 16)
                sp.dma_start(pin, io["p"][0, 0].rearrange("(t p) d -> p t d", p=P)).then_inc(ld_p, 16)
                with sp.Fori(1, NE) as e:
                    for i in range(PIECES):
                        sp.wait_ge(first["s"]["pieces_used"], e * PIECES - PIECES + (i + 1))
                        load(sp, e, i, piece)

            @block.gpsimd
            def _(pool):
                ch = Chain(pool, pool_ch)
                g = nc.gpsimd
                ch(g.memset(half, -0.5))
                for a in (kZs, kZw):
                    ch(g.memset(a[0:DH, 1, :], 0.0))
                    ch(g.memset(a[DH:P, 0, :], 0.0))
                ch(g.memset(kZd[0:DH, :, 1, :], 0.0))
                ch(g.memset(kZd[DH:P, :, 0, :], 0.0))
                ch(g.memset(V4, 0.0))
                ch(g.memset(kcZ, 0.0))
                ch(g.memset(hid4, 0.0))
                g.memset(P32, 0.0).then_inc(zeroed, 1)

                def rsqrt(dst, src, scale, done):
                    ch(g.tensor_scalar(dst, src, scale, EPS, ALU.mult, ALU.add))
                    n = src.shape
                    e = half[0:n[0], 0:int(np.prod(n[1:]))]
                    if len(n) == 3:
                        e = e.rearrange("p (a b) -> p a b", a=n[1])
                    g.tensor_tensor(dst, dst, e, ALU.pow).then_inc(done, 1)

                pool.wait_ge(zeroed, 1)
                pool.wait_ge(x_sq, 2)
                rsqrt(rs, ssx, 1.0 / DM, x_rs)
                pool.wait_ge(t_ev, 5)
                g.memset(ikZ, 0.0).then_inc(zeroed, 1)
                for n in range(2):
                    pool.wait_ge(n_var, n + 1)
                    rsqrt(v16, r16, 1.0 / DH, n_rs)
                pool.wait_ge(i_used, 6)
                for t in range(TT):
                    n = P * (t + 1)
                    g.affine_select(out=score[:, t, 0:n], in_=score[:, t, 0:n], compare_op=ALU.is_ge, fill=BLOCKED, base=t * P,
                                    pattern=[[-1, n]], channel_multiplier=1).then_inc(score_cut, 1)
                for n in range(2, 5):
                    pool.wait_ge(n_var, n + 1)
                    h = NORMS[n][2]
                    rsqrt(v16[:, :, 0:h], r16[:, :, 0:h], 1.0 / DH, n_rs)
                pool.wait_ge(n_var, 6)
                rsqrt(ckr[0:NCMP, 0:2], ckr[0:NCMP, 2:4], 1.0 / DH, n_rs)
                pool.wait_ge(ld_bias, 16)
                pool.wait_ge(selm_ready, 2)
                for u in range(8):
                    _, t, j = UNITS[u]
                    n = P * (t + 1)
                    o = P * (1 - t)
                    if u >= 1:
                        pool.wait_ge(s_log, u)
                    g.tensor_tensor(Bd[:, :, 0:n], bias[:, 8 + 2 * j:10 + 2 * j, o:o + n], bm(selm[:, t, 0:n], 2),
                                    ALU.add).then_inc(bd_ready, 1)
                pool.wait_ge(f_sq, 2)
                rsqrt(rs, ssx, 1.0 / DM, f_rs)

            @block.scalar
            def _(sc):
                a = nc.scalar
                cst = io["consts"]
                for dst, src in ((ident, cst[:, 0:128]), (tri, cst[:, 128:256]), (ones, cst[:, 256:384]),
                                 (iota1, cst[:, 384:512].rearrange("p (a b) -> p a b", a=2)), (idmod, cst[:, 512:544])):
                    sc.dma_start(dst, src).then_inc(ld_const, 16)
                for i, n in enumerate(("g_mix", "g_ffn", "g_ple")):
                    sc.dma_start(grow[i * 8:(i + 1) * 8, :], io[n][0].rearrange("(k p) -> k p", p=P)).then_inc(ld_const, 16)
                sc.dma_start(tab[0:BUCKETS, :], io["rel_bias"]).then_inc(ld_tab, 16)
                sc.dma_start(tab[BUCKETS:BUCKETS + 1, :], io["negrow"]).then_inc(ld_tab, 16)
                sc.dma_start(onehot, io["onehot"]).then_inc(ld_tab, 16)
                for i, n in enumerate(("g_q_nsa", "g_k_nsa", "g_q_dsa", "g_k_dsa")):
                    sc.dma_start(gqk[:, i, :], io[n].to_broadcast([P, DH])).then_inc(ld_small, 16)
                for i, n in enumerate(("pe_ck", "pe_cv")):
                    for r in range(2):
                        sc.dma_start(pe_in[:, 2 * i + r, :], io[n][0]).then_inc(ld_small, 16)
                for i, n in enumerate(("w_ck2", "w_cv2")):
                    for r in range(2):
                        sc.dma_start(ck2w[r * DH:(r + 1) * DH, i, :], io[n][0]).then_inc(ld_small, 16)
                sc.dma_start(wr, io["w_router"][0].rearrange("(k p) n -> p k n", p=P)).then_inc(ld_route, 16)
                sc.dma_start(br, io["b_router"].to_broadcast([P, NE])).then_inc(ld_route, 16)

                sc.wait_ge(ld_x, 16)
                for t in range(TT):
                    a.activation(xn[:, t, :], x[:, t, :], ACT.Square, accum_out=ssx[:, t:t + 1]).then_inc(x_sq, 1)

                def tjob(name):
                    n = TJOBS.index(name)
                    b = ps[4 + n % 2]
                    sc.wait_ge(t_ps, n + 1)
                    t = int(name[-1]) if name[-1].isdigit() else 0
                    tc = slice(t * P, (t + 1) * P)
                    kind = name[2:].rstrip("0123456789")
                    if kind == "G":
                        a.copy(gT, b[:, 0:24]).then_inc(t_ev, 1)
                        sc.wait_ge(t_ev, n + 1)
                    elif kind == "X":
                        for i in range(2):
                            k = 2 * t + i
                            l = a.activation(hTv[:, k, :], b[:, i * SEQ:(i + 1) * SEQ], ACT.Copy, scale=gT[:, k:k + 1])
                        l.then_inc(t_ev, 1)
                    elif kind == "IX":
                        sc.wait_ge(zeroed, 2)
                        a.copy(iqT[:, :, tc], b[:, 0:2 * P].rearrange("p (a t) -> p a t", a=2))
                        for i in range(4):
                            l = a.copy(ikZ[32 * i:32 * i + 32, i, tc], b[32 * i:32 * i + 32, 2 * P:3 * P])
                        l.then_inc(t_ev, 1)
                    elif kind in ("DQ", "NQ"):
                        q = qdT if kind == "DQ" else qaT
                        a.copy(q[:, :, tc], b[:, :].rearrange("p (j t) -> p j t", j=4)).then_inc(t_ev, 1)
                    elif kind == "DK":
                        v4 = b[:, :].rearrange("p (j t) -> p j t", j=4)
                        a.copy(kZd[0:DH, :, 0, tc], v4[0:DH])
                        a.copy(kZd[DH:P, :, 1, tc], v4[DH:P]).then_inc(t_ev, 1)
                    elif kind == "K":
                        for i, kz in enumerate((kZs, kZw)):
                            for g in range(2):
                                a.copy(kz[g * DH:(g + 1) * DH, g, tc], b[g * DH:(g + 1) * DH, i * P:(i + 1) * P])
                        a.copy(rawT[:, :, tc], b[:, 2 * P:4 * P].rearrange("p (a t) -> p a t", a=2)).then_inc(t_ev, 1)
                    elif kind == "PE":
                        a.copy(peT, b[:, 0:64].rearrange("p (a l) -> p a l", a=2)).then_inc(t_ev, 1)
                    elif kind == "KC":
                        for g in range(2):
                            l = a.copy(kcZ[g * DH:(g + 1) * DH, g, 0:NCMP], b[g * DH:(g + 1) * DH, 0:NCMP])
                        l.then_inc(t_ev, 1)
                    elif kind == "C":
                        a.copy(PcT[:, t], b[:, 0:2 * P].rearrange("p (a t) -> p a t", a=2)).then_inc(t_ev, 1)

                for stage in ORDER:
                    if stage.startswith("T:"):
                        tjob(stage)
                    elif stage[0] == "Z":
                        c = int(stage[1:])
                        o, n = CHUNKS[c]
                        for t in range(TT):
                            sc.wait_ge(z_ps, 2 * c + t + 1)
                            src = ps[2 * (c % 2) + t][:, 0:n]
                            if o < O_GA:
                                a.copy(z[:, t, o:o + n], src).then_inc(z_ev, 1)
                            else:
                                if c == C_G and t == 0:
                                    sc.wait_ge(st_er, 16)
                                a.activation(gates[:, t, o - O_GA:o - O_GA + n], src, ACT.Sigmoid).then_inc(z_ev, 1)
                        if c == C_G:
                            a.activation(gsig, z[:, :, O_NG:O_NG + 24], ACT.Sigmoid)
                    elif stage == "I":
                        if True:
                            sc.wait_ge(er_ps, 1)
                            a.copy(erow, ps[6][0:16, 0:384]).then_inc(er_sb, 1)
                            sc.wait_ge(er_sb, 1)
                            sc.dma_start(er_dram, erow).then_inc(st_er, 16)
                            sc.wait_ge(st_er, 16)
                            sc.dma_start(er_rep, er_dram.unsqueeze(1).to_broadcast([16, P, ERW])).then_inc(st_rep, 16)
                            sc.wait_ge(st_rep, 16)
                            src = bass.AP(tensor=er_rep.tensor, offset=P - 1, ap=[[ERW - 1, P], [P * ERW, 16], [1, SEQ]])
                            sc.dma_start(bias, src).then_inc(ld_bias, 16)
                        for i in range(6):
                            sc.wait_ge(i_ps, i + 1)
                            if i >= 2:
                                sc.wait_ge(i_used, i - 1)
                            a.activation(rl[:, i % 2, :], ps[7 - i % 2][:, :], ACT.Relu).then_inc(i_rl, 1)
                    elif stage == "HID":
                        sc.wait_ge(h_ps, 1)
                        for g in range(2):
                            l = a.activation(hsg[g * DH:(g + 1) * DH], ps[6 + g][g * DH:(g + 1) * DH, 0:32].rearrange("p (a c) -> p a c", a=2), ACT.Exp, scale=-1.0)
                        l.then_inc(h_exp, 1)
                    elif stage == "CMPKV":
                        sc.wait_ge(kc_copied, 1)
                        sc.wait_ge(zeroed, 1)
                        for g in range(2):
                            for j in range(4):
                                l = a.copy(V4[32 * j:32 * j + 32, g, j, :], ps[6 + g][32 * j:32 * j + 32, DH:2 * DH])
                        l.then_inc(v4_ready, 1)
                    elif stage == "CSC":
                        for t in range(TT):
                            n = CMP_SEEN[t]
                            sc.wait_ge(c_log, t + 1)
                            a.activation(cL[:, :, 0:n], cL[:, :, 0:n], ACT.Exp).then_inc(c_exp, 1)

                def exps(u):
                    n = P * (UNITS[u][1] + 1)
                    sc.wait_ge(s_log, u + 1)
                    for h in range(2):
                        l = a.activation(L[:, u % 4, h, 0:n], L[:, u % 4, h, 0:n], ACT.Exp, bias=nmx[:, u % 4, h:h + 1], accum_out=ssum[:, u % 4, h:h + 1])
                    l.then_inc(s_exp, 1)

                def evac_p(u):
                    nb = UNITS[u][1] + 1
                    n = NTJ + u
                    sc.wait_ge(t_ps, n + 1)
                    if u >= 2:
                        sc.wait_ge(o_ps, u - 1)
                    a.copy(PT[:, u % 2, 0:2 * nb, :], ps[4 + n % 2][:, 0:2 * nb * P].rearrange("p (a t) -> p a t", t=P)).then_inc(t_ev, 1)

                def evac_o(u):
                    if u >= 8 and (u - 8) % 2 == 0:
                        return
                    i = item_of(u)
                    kind, t, j = UNITS[u]
                    sc.wait_ge(o_ps, u + 1)
                    a.copy(oTv[:, 1 if i < 8 else 0, j, t * P:(t + 1) * P], ps[6 + i % 2][:, 0:P]).then_inc(o_ev, 1)

                tjob("T:C0")
                tjob("T:C1")
                for u in range(NU + 3):
                    if u < NU:
                        exps(u)
                    if 2 <= u < NU + 2:
                        evac_p(u - 2)
                    if u >= 3:
                        evac_o(u - 3)
                for n in range(4):
                    k = NTJ + NU + n
                    sc.wait_ge(t_ps, k + 1)
                    a.copy(hTv[:, 2 * n:2 * n + 2, :], ps[4 + k % 2][:, :].rearrange("p (k t) -> p k t", k=2)).then_inc(t_ev, 1)
                for t in range(TT):
                    sc.wait_ge(x2_ready, 2 * t + 2)
                    a.activation(xh[:, t, :], x[:, t, :], ACT.Square, accum_out=ssx[:, t:t + 1]).then_inc(f_sq, 1)
                for n in range(4):
                    k = NTJ + NU + 4 + n
                    sc.wait_ge(t_ps, k + 1)
                    for i in range(2):
                        kk = 2 * n + i
                        l = a.activation(hTv[:, kk, :], ps[4 + k % 2][:, i * SEQ:(i + 1) * SEQ], ACT.Copy, scale=gT[:, 8 + kk:9 + kk])
                    l.then_inc(t_ev, 1)
                for t in range(TT):
                    sc.wait_ge(lg_ready, t + 1)
                    a.activation(e4[:, t, :], top8[:, t, 0:4], ACT.Exp, bias=nt[:, t:t + 1], accum_out=sm2[:, t, 0:1]).then_inc(rt_exp, 1)
                k = NTJ + NU + 8
                sc.wait_ge(t_ps, k + 1)
                a.copy(WT, ps[4 + k % 2][0:NE, 0:SEQ]).then_inc(t_ev, 1)
                expert_act(sc, first)

            @block.vector
            def _(ve):
                d = nc.vector
                ch = Chain(ve, dve_ch)
                ve.wait_ge(x_rs, 1)
                for t in range(TT):
                    l = d.tensor_scalar(xn[:, t, :], x[:, t, :], rs[:, t:t + 1], None, ALU.mult)
                l.then_inc(xn_ready, 1)

                def norm_sq(n):
                    _, o, h, _, _ = NORMS[n]
                    ve.wait_ge(z_ev, 2 * (NORM_CHUNK[n] + 1))
                    src = z[:, :, o:o + h * DH]
                    ch(d.tensor_tensor(sq[:, :, 0:h * DH], src, src, ALU.mult))
                    d.tensor_reduce(r16[:, :, 0:h], sq[:, :, 0:h * DH].rearrange("p t (h e) -> p t h e", h=h), AX.X, ALU.add).then_inc(n_var, 1)

                def norm_mul(n, at):
                    name, o, h, g, s = NORMS[n]
                    ve.wait_ge(n_rs, n + 1)
                    if s != 1.0:
                        ch(d.tensor_scalar(v16[:, :, 0:h], v16[:, :, 0:h], s, None, ALU.mult))
                    for t in range(TT):
                        src = z[:, t, o:o + h * DH].rearrange("p (h e) -> p h e", h=h)
                        ch(d.tensor_tensor(sq[:, t, 0:h * DH].rearrange("p (h e) -> p h e", h=h), src, bc(v16[:, t, 0:h], DH), ALU.mult))
                    for t in range(TT):
                        dst = qn[:, t, at:at + h * DH]
                        if name == "nq":
                            dst = dst.rearrange("p (j g e) -> p g j e", j=4, g=2)
                            src = sq[:, t, :].rearrange("p (g j e) -> p g j e", g=2, j=4)
                            for g2 in range(2):
                                l = d.tensor_tensor(dst[:, g2], src[:, g2], bm(gqk[:, g, :], 4), ALU.mult)
                        else:
                            l = d.tensor_tensor(dst.rearrange("p (h e) -> p h e", h=h), sq[:, t, 0:h * DH].rearrange("p (h e) -> p h e", h=h),
                                                bm(gqk[:, g, :], h), ALU.mult)
                    ch_sig(l)

                def ch_sig(l):
                    qn_n[0] += 1
                    l.then_inc(qn_ready, 1)
                    ve.wait_ge(qn_ready, qn_n[0])
                qn_n = [0]

                ve.wait_ge(z_ev, 2)
                for t in range(TT):
                    d.tensor_copy(qn[:, t, 0:P].rearrange("p (r e) -> p r e", r=4), bm(z[:, t, O_IK:O_IK + ID], 4))
                ch(d.tensor_scalar(iwS, z[:, :, O_IW:O_IW + IH], ID ** -0.5 * IH ** -0.5, None, ALU.mult))
                ch(d.memset(score, 0.0))
                d.memset(m8, 0.0).then_inc(ikrep_ready, 1)
                ve.wait_ge(ld_small, 16 * 12)
                norm_sq(0)
                ve.wait_ge(t_ps, TJOBS.index("T:IX1") + 1)
                norm_mul(0, 0)
                for i in range(6):
                    ve.wait_ge(i_rl, i + 1)
                    if i < 4:
                        parts = [(1, 4 * (i // 2) + 2 * (i % 2) + r, rl[:, i % 2, r * SEQ:(r + 1) * SEQ], SEQ) for r in range(2)]
                    else:
                        parts = [(0, 4 * (i - 4) + r, rl[:, i % 2, r * P:(r + 1) * P], P) for r in range(4)]
                    for q, (t, h, src, n) in enumerate(parts):
                        l = d.scalar_tensor_tensor(score[:, t, 0:n], src, iwS[:, t, h:h + 1], score[:, t, 0:n], ALU.mult, ALU.add)
                        if q < len(parts) - 1:
                            ch(l)
                    l.then_inc(i_used, 1)
                    ve.wait_ge(i_used, i + 1)
                norm_sq(1)
                ve.wait_ge(t_ps, TJOBS.index("T:DQ1") + 1)
                norm_mul(1, 0)

                def topk(t):
                    ve.wait_ge(score_cut, t + 1)
                    n = P * (t + 1)
                    for r in range(KEEP // 8):
                        ch(d.max(m8, score[:, t, 0:n]))
                        ch(d.match_replace(score[:, t, 0:n], m8, score[:, t, 0:n], TAKEN))
                    d.tensor_scalar(selm[:, t, 0:n], score[:, t, 0:n], (BLOCKED + TAKEN) / 2, NEG, ALU.is_gt, ALU.mult).then_inc(selm_ready, 1)

                topk(0)
                norm_sq(2)
                ve.wait_ge(t_ps, TJOBS.index("T:DK1") + 1)
                norm_mul(2, 0)
                topk(1)
                norm_sq(3)
                ve.wait_ge(t_ps, TJOBS.index("T:NQ1") + 1)
                norm_mul(3, 0)
                norm_sq(4)
                norm_mul(4, P)
                ve.wait_ge(t_ev, TJOBS.index("T:PE") + 1)
                for kv in range(2):
                    for hf in range(2):
                        src = rawT[:, kv, :].rearrange("p (c i) -> p i c", i=CMP_STRIDE)[:, :, hf:hf + NCMP]
                        l = d.tensor_tensor(zb[:, kv, hf * 16:(hf + 1) * 16, 0:NCMP], src, bc(peT[:, kv, hf * 16:(hf + 1) * 16], NCMP), ALU.add)
                l.then_inc(zb_ready, 1)
                ve.wait_ge(h_exp, 1)
                ch(d.tensor_scalar(hsg[:, :, 0:NCMP], hsg[:, :, 0:NCMP], 1.0, None, ALU.add))
                ch(d.reciprocal(hsg[:, :, 0:NCMP], hsg[:, :, 0:NCMP]))
                for g in range(2):
                    l = d.tensor_tensor(hid[g * DH:(g + 1) * DH, :, 0:NCMP], hsg[g * DH:(g + 1) * DH, :, 0:NCMP],
                                        ps[6 + g][g * DH:(g + 1) * DH, 0:32].rearrange("p (a c) -> p a c", a=2)[:, :, 0:NCMP], ALU.mult)
                ch(l)
                ve.wait_ge(zeroed, 1)
                d.tensor_copy(hid4[:, :, 0:NCMP], bm(hid[:, 1, 0:NCMP], 4)).then_inc(hid_ready, 1)
                ve.wait_ge(kc_ps, 1)
                for g in range(2):
                    l = d.tensor_copy(kcs[0:NCMP, g, :], ps[6 + g][0:NCMP, 0:DH])
                l.then_inc(kc_copied, 1)
                ve.wait_ge(kc_copied, 1)
                kc = kcs[0:NCMP]
                ch(d.tensor_tensor(kcq[0:NCMP], kc, kc, ALU.mult))
                d.tensor_reduce(ckr[0:NCMP, 2:4], kcq[0:NCMP], AX.X, ALU.add).then_inc(n_var, 1)
                ve.wait_ge(n_rs, 6)
                ch(d.tensor_tensor(kcq[0:NCMP], kc, bc(ckr[0:NCMP, 0:2], DH), ALU.mult))
                d.tensor_tensor(kcs[0:NCMP], kcq[0:NCMP], bm(gqk[0:NCMP, 1, :], 2), ALU.mult).then_inc(kcn_ready, 1)
                ve.wait_ge(ld_bias, 16)
                for t in range(TT):
                    n = CMP_SEEN[t]
                    o = P * (1 - t) + CMP_LEN - 1
                    ve.wait_ge(c_ps, t + 1)
                    lv = cL[:, :, 0:n]
                    for g in range(2):
                        src = ps[6 + t][:, 0:P].rearrange("p (j g c) -> p g j c", j=4, g=2)[:, g, :, 0:n]
                        bv = bias[:, 4 * g:4 * g + 4, o:o + (n - 1) * CMP_STRIDE + 1:CMP_STRIDE]
                        l = d.tensor_tensor(cL[:, 4 * g:4 * g + 4, 0:n], src, bv, ALU.add)
                    ch(l)
                    ch(d.tensor_reduce(cst[:, 0, :], lv, AX.X, ALU.max))
                    ch(d.tensor_scalar(cst[:, 1, :], cst[:, 0, :], NEG / 10, None, ALU.max))
                    d.tensor_tensor(lv, lv, bc(cst[:, 1, :], n), ALU.subtract).then_inc(c_log, 1)
                    ve.wait_ge(c_exp, t + 1)
                    ch(d.tensor_reduce(cst[:, 2, :], lv, AX.X, ALU.add))
                    ch(d.tensor_scalar(cst[:, 2, :], cst[:, 2, :], 1e-30, None, ALU.max))
                    ch(d.reciprocal(cst[:, 3, :], cst[:, 2, :]))
                    ch(d.tensor_tensor(cst[:, 3, :], cst[:, 3, :], gsig[:, t, 0:24:3], ALU.mult))
                    d.tensor_tensor(P32[:, t, :, 0:n], lv, bc(cst[:, 3, :], n), ALU.mult).then_inc(c_ready, 1)
                    ve.wait_ge(c_ready, t + 1)

                def logits(u):
                    kind, t, j = UNITS[u]
                    n = P * (t + 1)
                    o = P * (1 - t)
                    ve.wait_ge(s_ps, u + 1)
                    if kind == "dsa":
                        ve.wait_ge(bd_ready, u + 1)
                    if u >= 4:
                        ve.wait_ge(t_ps, NTJ + u - 3)
                    for h in range(2):
                        if kind == "dsa":
                            b = Bd[:, h, 0:n]
                        else:
                            b = bias[:, 4 * h + j, o:o + n]
                        l = d.tensor_tensor_reduce(out=L[:, u % 4, h, 0:n], in0=ps[u % 4][:, h * n:(h + 1) * n], in1=b, scale=1.0, scalar=NEG * 10,
                                                   op0=ALU.add, op1=ALU.max, accum_out=mx[:, u % 4, h:h + 1])
                        ch(l)
                    d.tensor_scalar(nmx[:, u % 4, :], mx[:, u % 4, :], -1.0, None, ALU.mult).then_inc(s_log, 1)
                    ve.wait_ge(s_log, u + 1)

                def probs(u):
                    kind, t, j = UNITS[u]
                    n = P * (t + 1)
                    ve.wait_ge(s_exp, u + 1)
                    r = rcp[:, u % 4, :]
                    ch(d.tensor_scalar(r, ssum[:, u % 4, :], 1e-30, None, ALU.max))
                    ch(d.reciprocal(r, r))
                    if kind != "dsa":
                        b = 1 if kind == "slc" else 2
                        ch(d.tensor_tensor(r, r, gsig[:, t, 3 * j + b:3 * j + b + 13:12], ALU.mult))
                    for h in range(2):
                        l = d.tensor_scalar(L[:, u % 4, h, 0:n], L[:, u % 4, h, 0:n], r[:, h:h + 1], None, ALU.mult)
                    l.then_inc(s_prob, 1)
                    ve.wait_ge(s_prob, u + 1)

                for u in range(NU + 1):
                    if u < NU:
                        logits(u)
                    if u >= 1:
                        probs(u - 1)

                for i in range(4):
                    t, n = i // 2, (i % 2) * 512
                    ve.wait_ge(pr_ps, i + 1)
                    ch(d.tensor_tensor(mtmp[:, 0, :], ps[2 * (i % 2)][:, :], gates[:, t, n:n + 512], ALU.mult))
                    ch(d.tensor_tensor(mtmp[:, 1, :], ps[2 * (i % 2) + 1][:, :], gates[:, t, DM + n:DM + n + 512], ALU.mult))
                    d.tensor_tensor(merged[:, t, n:n + 512], mtmp[:, 0, :], mtmp[:, 1, :], ALU.add).then_inc(pr_used, 1)
                    ve.wait_ge(pr_used, i + 1)
                for i in range(4):
                    t, n = i // 2, (i % 2) * 512
                    ve.wait_ge(wo_ps, i + 1)
                    d.tensor_tensor(x[:, t, n:n + 512], ps[i][:, :], x[:, t, n:n + 512], ALU.add).then_inc(x2_ready, 1)
                ve.wait_ge(f_rs, 1)
                for t in range(TT):
                    l = d.tensor_scalar(xh[:, t, :], x[:, t, :], rs[:, t:t + 1], None, ALU.mult)
                l.then_inc(xh_ready, 1)
                ve.wait_ge(xh_ready, 1)
                ve.wait_ge(t_ps, NTJ + NU + 8)
                for q in range(2):
                    ch(d.tensor_copy(hp[:, q], xh))
                    ch(d.tensor_tensor(xh, xh, hp[:, q], ALU.subtract))
                d.tensor_copy(hp[:, 2], xh).then_inc(hp_ready, 1)
                ve.wait_ge(hp_ready, 1)
                ve.wait_ge(ld_b1, 48)
                ch(d.tensor_copy(b1p, b1f))
                for lo in (NE, 2 * NE, 2 * NE):
                    hi = lo + NE
                    ch(d.tensor_tensor(b1f[lo:hi], b1f[lo:hi], b1p[lo:hi], ALU.subtract))
                    l = d.tensor_copy(b1p[lo:hi], b1f[lo:hi])
                    ch(l)
                d.memset(oe, 0.0).then_inc(b1_ready, 1)
                ve.wait_ge(rt_ps, 1)
                ve.wait_ge(ld_route, 32)
                for t in range(TT):
                    ch(d.tensor_tensor(lg[:, t, :], ps[6][:, t * NE:(t + 1) * NE], br, ALU.add))
                    ch(d.max(top8[:, t, :], lg[:, t, :]))
                    ch(d.max_index(idx8[:, t, :], top8[:, t, :], lg[:, t, :]))
                    ch(d.tensor_copy(idxf[:, t, :], idx8[:, t, :]))
                    d.tensor_scalar(nt[:, t:t + 1], top8[:, t, 0:1], -1.0, None, ALU.mult).then_inc(lg_ready, 1)
                    ve.wait_ge(rt_exp, t + 1)
                    ch(d.reciprocal(sm2[:, t, 1:2], sm2[:, t, 0:1]))
                    ch(d.tensor_scalar(e4[:, t, :], e4[:, t, :], sm2[:, t, 1:2], None, ALU.mult))
                    ch(d.memset(Wt[:, t, :], 0.0))
                    ch(d.memset(Mt[:, t, :], 0.0))
                    for k in range(TOPK):
                        ch(d.tensor_scalar(lg[:, t, :], iota1[:, 0, 0:NE], -1.0, idxf[:, t, k:k + 1], ALU.add, ALU.is_equal))
                        ch(d.scalar_tensor_tensor(Wt[:, t, 0:NE], lg[:, t, :], e4[:, t, k:k + 1], Wt[:, t, 0:NE], ALU.mult, ALU.add))
                        l = d.tensor_tensor(Mt[:, t, :], Mt[:, t, :], lg[:, t, :], ALU.add)
                        if k < TOPK - 1:
                            ch(l)
                    l.then_inc(m_ready, 1)
                    ve.wait_ge(m_ready, t + 1)
                ve.wait_ge(rk_ps, 1)
                for t in range(TT):
                    ch(d.scalar_tensor_tensor(rank[:, t, 0:NE], ps[7][:, t * NE:(t + 1) * NE], 1.0, Mt[:, t, :], ALU.add, ALU.mult))
                    for r in range(1, ROUNDS):
                        d.tensor_scalar(rank[:, t, r * NE:(r + 1) * NE], rank[:, t, 0:NE], float(-SLOTS * r), None, ALU.add)
                        d.tensor_copy(Wt[:, t, r * NE:(r + 1) * NE], Wt[:, t, 0:NE])
                ch(d.tensor_reduce(cmax, ps[7][:, 2 * NE:3 * NE], AX.X, ALU.max))
                ch(d.tensor_copy(cmaxi, cmax))
                d.memset(selx, 0.0).then_inc(init0, 1)
                expert_dve(ve, first)

            @block.tensor
            def _(te):
                mm, tr = nc.tensor.matmul, nc.tensor.transpose
                te.wait_ge(ld_const, 16 * 8)

                def tbank(n):
                    if n >= 2:
                        te.wait_ge(t_ev, n - 1)
                    return ps[4 + n % 2]

                def tjob(name):
                    n = TJOBS.index(name)
                    b = tbank(n)
                    t = int(name[-1]) if name[-1].isdigit() else 0
                    kind = name[2:].rstrip("0123456789")
                    if kind == "G":
                        l = tr(b[:, 0:24], grow, ident[0:24, 0:24])
                    elif kind == "X":
                        te.wait_ge(xn_ready, 1)
                        for i in range(2):
                            for q in range(TT):
                                l = tr(b[:, i * SEQ + q * P:i * SEQ + (q + 1) * P], xn[:, q, (2 * t + i) * P:(2 * t + i + 1) * P], ident)
                    elif kind == "IX":
                        te.wait_ge(ikrep_ready, 1)
                        for i in range(2):
                            tr(b[:, i * P:(i + 1) * P], z[:, t, O_IQ + i * P:O_IQ + (i + 1) * P], ident)
                        l = tr(b[:, 2 * P:3 * P], qn[:, t, 0:P], ident)
                    elif kind in ("DQ", "DK", "NQ"):
                        te.wait_ge(qn_ready, {"DQ": 1, "DK": 2, "NQ": 3}[kind])
                        for j in range(4):
                            l = tr(b[:, j * P:(j + 1) * P], qn[:, t, j * P:(j + 1) * P], ident)
                    elif kind == "K":
                        te.wait_ge(qn_ready, 5)
                        for i in range(2):
                            tr(b[:, i * P:(i + 1) * P], qn[:, t, i * P:(i + 1) * P], ident)
                        for i in range(2):
                            l = tr(b[:, (2 + i) * P:(3 + i) * P], z[:, t, O_KV + i * P:O_KV + (i + 1) * P], ident)
                    elif kind == "PE":
                        te.wait_ge(ld_small, 16 * 12)
                        for i in range(2):
                            l = tr(b[:, i * 32:(i + 1) * 32], pe_in[:, 2 * i:2 * i + 2, :].rearrange("l a d -> l (a d)"), ident[0:32, 0:32])
                    elif kind == "KC":
                        te.wait_ge(kcn_ready, 1)
                        l = tr(b[:, 0:NCMP], kcs[0:NCMP].rearrange("c g d -> c (g d)"), ident[0:NCMP, 0:NCMP])
                    elif kind == "C":
                        te.wait_ge(c_ready, t + 1)
                        for g in range(2):
                            l = tr(b[:, g * P:(g + 1) * P], P32[:, t, 4 * g:4 * g + 4, :].rearrange("p j c -> p (j c)"), ident)
                    l.then_inc(t_ps, 1)

                for stage in ORDER:
                    if stage.startswith("T:"):
                        tjob(stage)
                    elif stage[0] == "Z":
                        c = int(stage[1:])
                        o, n = CHUNKS[c]
                        te.wait_ge(ld_w[c % 3], 16 * (c // 3 + 1))
                        te.wait_ge(t_ev, 5)
                        if c >= 2:
                            te.wait_ge(z_ev, 2 * (c - 1))
                        wv = wbuf[:, (c % 3) * 4096:(c % 3) * 4096 + KT * n].rearrange("p (k n) -> p k n", k=KT)
                        for t in range(TT):
                            for k in range(KT):
                                l = mm(ps[2 * (c % 2) + t][:, 0:n], hTv[:, k, t * P:(t + 1) * P], wv[:, k, :], start=k == 0, stop=k == KT - 1)
                            l.then_inc(z_ps, 1)
                    elif stage == "I":
                        te.wait_ge(ld_tab, 48)
                        mm(ps[6][0:16, 0:384], tab, onehot, start=True, stop=True).then_inc(er_ps, 1)
                        te.wait_ge(t_ev, TJOBS.index("T:IX1") + 1)
                        for i in range(6):
                            if i == 1:
                                te.wait_ge(er_sb, 1)
                            if i >= 2:
                                te.wait_ge(i_rl, i - 1)
                            if i < 4:
                                lhs, rhs = iqT[:, i // 2, P:2 * P], ikZ[:, 2 * (i % 2):2 * (i % 2) + 2, :]
                            else:
                                lhs, rhs = iqT[:, i - 4, 0:P], ikZ[:, :, 0:P]
                            mm(ps[7 - i % 2][:, :], lhs, rhs, start=True, stop=True).then_inc(i_ps, 1)
                    elif stage == "HID":
                        te.wait_ge(ld_ck, 64)
                        te.wait_ge(zb_ready, 1)
                        te.wait_ge(i_rl, 6)
                        for kv in range(2):
                            for l_ in range(CMP_LEN):
                                for g in range(2):
                                    h = slice(g * DH, (g + 1) * DH)
                                    l = mm(ps[6 + g][h, kv * 16:kv * 16 + NCMP], wck1[h, kv, l_, :], zb[h, kv, l_, 0:NCMP],
                                           start=l_ == 0, stop=l_ == CMP_LEN - 1)
                        l.then_inc(h_ps, 1)
                    elif stage == "CMPKV":
                        te.wait_ge(hid_ready, 1)
                        for g in range(2):
                            h = slice(g * DH, (g + 1) * DH)
                            mm(ps[6 + g][0:NCMP, 0:DH], hid[h, 0, 0:NCMP], ck2w[h, 0, :], start=True, stop=True)
                        for g in range(2):
                            h = slice(g * DH, (g + 1) * DH)
                            l = mm(ps[6 + g][:, DH:2 * DH], hid4[h].rearrange("p j c -> p (j c)"), ck2w[h, 1, :], start=True, stop=True)
                        l.then_inc(kc_ps, 1)
                    elif stage == "CSC":
                        te.wait_ge(t_ev, TJOBS.index("T:KC") + 1)
                        te.wait_ge(v4_ready, 1)
                        for t in range(TT):
                            for j in range(4):
                                l = mm(ps[6 + t][:, j * 32:(j + 1) * 32], qaT[:, j, t * P:(t + 1) * P],
                                       kcZ.rearrange("p g c -> p (g c)"), start=True, stop=True)
                            l.then_inc(c_ps, 1)

                def scores(u):
                    kind, t, j = UNITS[u]
                    n = P * (t + 1)
                    if u == 0:
                        te.wait_ge(z_ev, 2 * NZ)
                    if u >= 4:
                        te.wait_ge(s_log, u - 3)
                    q, k = {"dsa": (qdT, kZd[:, j]), "slc": (qaT, kZs), "win": (qaT, kZw)}[kind]
                    mm(ps[u % 4][:, 0:2 * n], q[:, j, t * P:(t + 1) * P], k[:, :, 0:n], start=True, stop=True).then_inc(s_ps, 1)

                def flip(u):
                    t = UNITS[u][1]
                    b = tbank(NTJ + u)
                    te.wait_ge(s_prob, u + 1)
                    for h in range(2):
                        for s in range(t + 1):
                            l = tr(b[:, (h * (t + 1) + s) * P:(h * (t + 1) + s + 1) * P], L[:, u % 4, h, s * P:(s + 1) * P], ident)
                    l.then_inc(t_ps, 1)

                def values(u):
                    kind, t, j = UNITS[u]
                    i = item_of(u)
                    te.wait_ge(t_ev, NTJ + u + 1)
                    if i >= 2:
                        te.wait_ge(o_ev, i - 1)
                    for h in range(2):
                        dst = ps[6 + i % 2][h * DH:(h + 1) * DH, 0:P]
                        o = {"dsa": O_DV + (2 * j + h) * DH, "slc": O_KV + 3 * P + h * DH, "win": O_KV + 5 * P + h * DH}[kind]
                        if kind == "slc":
                            mm(dst, V4[:, h, j, :], PcT[:, t, h, :], start=True, stop=False)
                        for s in range(t + 1):
                            l = mm(dst, z[:, s, o:o + DH], PT[:, u % 2, h * (t + 1) + s, :], start=kind == "dsa" and s == 0,
                                   stop=kind != "slc" and s == t)
                    l.then_inc(o_ps, 1)

                tjob("T:C0")
                tjob("T:C1")
                for u in range(NU + 3):
                    if u < NU:
                        scores(u)
                    if 2 <= u < NU + 2:
                        flip(u - 2)
                    if u >= 3:
                        values(u - 3)
                te.wait_ge(ld_wab, 48)
                te.wait_ge(o_ev, NITEM)
                for i in range(4):
                    t, n = i // 2, (i % 2) * 512
                    if i >= 2:
                        te.wait_ge(pr_used, i - 1)
                    for m_ in range(2):
                        for j in range(4):
                            l = mm(ps[2 * (i % 2) + m_][:, :], oTv[:, m_, j, t * P:(t + 1) * P], (wa, wb)[m_][:, j, n:n + 512], start=j == 0, stop=j == 3)
                    l.then_inc(pr_ps, 1)
                te.wait_ge(pr_used, 4)
                for n in range(4):
                    b = tbank(NTJ + NU + n)
                    for i in range(2):
                        for t in range(TT):
                            l = tr(b[:, i * SEQ + t * P:i * SEQ + (t + 1) * P], merged[:, t, (2 * n + i) * P:(2 * n + i + 1) * P], ident)
                    l.then_inc(t_ps, 1)
                te.wait_ge(ld_wo, 16)
                te.wait_ge(t_ev, NTJ + NU + 4)
                for i in range(4):
                    t, n = i // 2, (i % 2) * 512
                    for k in range(KT):
                        l = mm(ps[i][:, :], hTv[:, k, t * P:(t + 1) * P], wo[:, k, n:n + 512], start=k == 0, stop=k == KT - 1)
                    l.then_inc(wo_ps, 1)
                te.wait_ge(xh_ready, 1)
                for n in range(4):
                    b = tbank(NTJ + NU + 4 + n)
                    for i in range(2):
                        for t in range(TT):
                            l = tr(b[:, i * SEQ + t * P:i * SEQ + (t + 1) * P], xh[:, t, (2 * n + i) * P:(2 * n + i + 1) * P], ident)
                    l.then_inc(t_ps, 1)
                te.wait_ge(t_ev, NTJ + NU + 8)
                te.wait_ge(ld_route, 32)
                for t in range(TT):
                    for k in range(KT):
                        l = mm(ps[6][:, t * NE:(t + 1) * NE], hTv[:, k, t * P:(t + 1) * P], wr[:, k, :], start=k == 0, stop=k == KT - 1)
                l.then_inc(rt_ps, 1)
                te.wait_ge(m_ready, 2)
                mm(ps[7][:, 0:NE], tri, Mt[:, 0, :], start=True, stop=True)
                mm(ps[7][:, NE:2 * NE], ones, Mt[:, 0, :], start=True, stop=False)
                mm(ps[7][:, NE:2 * NE], tri, Mt[:, 1, :], start=False, stop=True)
                mm(ps[7][:, 2 * NE:3 * NE], ones, Mt[:, 0, :], start=True, stop=False)
                mm(ps[7][:, 2 * NE:3 * NE], ones, Mt[:, 1, :], start=False, stop=True).then_inc(rk_ps, 1)
                b = tbank(NTJ + NU + 8)
                for t in range(TT):
                    l = tr(b[0:NE, t * P:(t + 1) * P], Wt[:, t, 0:NE], ident)
                l.then_inc(t_ps, 1)
                te.wait_ge(t_ev, NTJ + NU + 9)
                te.wait_ge(ld_be2, 16)
                te.wait_ge(init0, 1)
                for t in range(TT):
                    for n in range(2):
                        mm(ps[4 + 2 * t + n][:, :], WT[:, t * P:(t + 1) * P], be2[:, n * 512:(n + 1) * 512], start=True, stop=False, skip_group_check=True)
                expert_pe(te, first)

        with nc.Block() as block:
            def some(eng):
                return eng.If(eng.value_load(cmaxi[0:1, 0:1], min_val=0, max_val=SEQ) > SLOTS)

            @block.sync
            def _(sp):
                with some(sp):
                    for i in range(PIECES):
                        load(sp, 0, i, rest["piece"])
                    with sp.Fori(1, rest["visits"]) as it:
                        for i in range(PIECES):
                            sp.wait_ge(rest["s"]["pieces_used"], it * PIECES - PIECES + (i + 1))
                            load(sp, it % NE, i, rest["piece"])

            @block.scalar
            def _(sc):
                with some(sc):
                    expert_act(sc, rest)

            @block.vector
            def _(ve):
                with some(ve):
                    expert_dve(ve, rest)

            @block.tensor
            def _(te):
                with some(te):
                    expert_pe(te, rest)

        x3_ready, p_sq, p_rs, xn3_ready, p_ps, p_ev, g_ps, g_sig, g_used, pl_ps, o_ready, st_out = (
            sem(n) for n in ("x3_ready", "p_sq", "p_rs", "xn3_ready", "p_ps", "p_ev", "g_ps", "g_sig", "g_used", "pl_ps", "o_ready", "st_out"))
        with nc.Block() as block:
            @block.gpsimd
            def _(pool):
                g = nc.gpsimd
                pool.wait_ge(p_sq, 2)
                g.tensor_scalar(rs, ssx, 1.0 / DM, EPS, ALU.mult, ALU.add).then_inc(p_rs, 1)
                pool.wait_ge(p_rs, 1)
                g.tensor_tensor(rs, rs, half[:, 0:2], ALU.pow).then_inc(p_rs, 1)

            @block.scalar
            def _(sc):
                a = nc.scalar
                sc.wait_ge(p_ps, 1)
                a.copy(pT, ps[0][:, :].rearrange("p (k t) -> p k t", k=2)).then_inc(p_ev, 1)
                for t in range(TT):
                    sc.wait_ge(x3_ready, 2 * t + 2)
                    a.activation(xn3[:, t, :], x[:, t, :], ACT.Square, accum_out=ssx[:, t:t + 1]).then_inc(p_sq, 1)
                for n in range(4):
                    sc.wait_ge(p_ps, n + 2)
                    for i in range(2):
                        kk = 2 * n + i
                        l = a.activation(hTv[:, kk, :], ps[n % 2][:, i * SEQ:(i + 1) * SEQ], ACT.Copy, scale=gT[:, 16 + kk:17 + kk])
                    l.then_inc(p_ev, 1)
                for i in range(4):
                    sc.wait_ge(g_ps, i + 1)
                    if i >= 2:
                        sc.wait_ge(o_ready, i - 1)
                    a.activation(sgate[:, i % 2, :], ps[i % 4][:, :], ACT.Sigmoid).then_inc(g_sig, 1)

            @block.vector
            def _(ve):
                d = nc.vector
                for i in range(4):
                    t, n = i // 2, (i % 2) * 512
                    d.tensor_tensor(x[:, t, n:n + 512], x[:, t, n:n + 512], ps[4 + i][:, :], ALU.add).then_inc(x3_ready, 1)
                ve.wait_ge(x3_ready, 4)
                ve.wait_ge(p_rs, 2)
                for t in range(TT):
                    l = d.tensor_scalar(xn3[:, t, :], x[:, t, :], rs[:, t:t + 1], None, ALU.mult)
                l.then_inc(xn3_ready, 1)
                for i in range(4):
                    t, n = i // 2, (i % 2) * 512
                    ve.wait_ge(g_sig, i + 1)
                    ve.wait_ge(pl_ps, i + 1)
                    d.tensor_tensor(sgate[:, i % 2, :], sgate[:, i % 2, :], ps[4 + i][:, :], ALU.mult).then_inc(g_used, 1)
                    ve.wait_ge(g_used, i + 1)
                    d.tensor_tensor(x[:, t, n:n + 512], x[:, t, n:n + 512], sgate[:, i % 2, :], ALU.add).then_inc(o_ready, 1)

            @block.tensor
            def _(te):
                mm, tr = nc.tensor.matmul, nc.tensor.transpose
                te.wait_ge(ld_p, 16)
                for k in range(2):
                    for t in range(TT):
                        l = tr(ps[0][:, k * SEQ + t * P:k * SEQ + (t + 1) * P], pin[:, t, k * P:(k + 1) * P], ident)
                l.then_inc(p_ps, 1)
                te.wait_ge(ld_ple, 32)
                te.wait_ge(p_ev, 1)
                for i in range(4):
                    t, n = i // 2, (i % 2) * 512
                    te.wait_ge(x3_ready, i + 1)
                    for k in range(2):
                        l = mm(ps[4 + i][:, :], pT[:, k, t * P:(t + 1) * P], wple[:, k, n:n + 512], start=k == 0, stop=k == 1)
                    l.then_inc(pl_ps, 1)
                te.wait_ge(xn3_ready, 1)
                for n in range(4):
                    if n >= 2:
                        te.wait_ge(p_ev, n)
                    for i in range(2):
                        for t in range(TT):
                            l = tr(ps[n % 2][:, i * SEQ + t * P:i * SEQ + (t + 1) * P], xn3[:, t, (2 * n + i) * P:(2 * n + i + 1) * P], ident)
                    l.then_inc(p_ps, 1)
                te.wait_ge(p_ev, 5)
                for i in range(4):
                    t, n = i // 2, (i % 2) * 512
                    for k in range(KT):
                        l = mm(ps[i][:, :], hTv[:, k, t * P:(t + 1) * P], wple_g[:, k, n:n + 512], start=k == 0, stop=k == KT - 1)
                    l.then_inc(g_ps, 1)

            @block.sync
            def _(sp):
                for i in range(4):
                    t, n = i // 2, (i % 2) * 512
                    sp.wait_ge(o_ready, i + 1)
                    sp.dma_start(out[0, t * P:(t + 1) * P, n:n + 512], x[:, t, n:n + 512]).then_inc(st_out, 16)
                sp.wait_ge(st_out, 64)


def constants():
    c = np.zeros((P, 544), np.float32)
    c[:, 0:P] = np.eye(P)
    c[:, P:2 * P] = np.triu(np.ones((P, P)), 1)
    c[:, 2 * P:3 * P] = 1.0
    c[:, 3 * P:4 * P] = np.arange(P) % SLOTS + 1
    c[:, 4 * P:4 * P + NE] = (np.arange(P)[:, None] % NE) == np.arange(NE)[None, :]
    onehot = np.zeros((BUCKETS + 1, 384), np.float32)
    for j in range(384):
        n = 255 - j
        if n < 0:
            b = BUCKETS
        elif n < MAX_EXACT:
            b = n
        else:
            big = np.log(np.float32(n) / np.float32(MAX_EXACT)) / np.float32(math.log(MAX_DIST / MAX_EXACT))
            b = min(MAX_EXACT + int(big * np.float32(BUCKETS - MAX_EXACT)), BUCKETS - 1)
        onehot[b, j] = 1.0
    return {"consts": c, "onehot": onehot, "negrow": np.full((1, 16), NEG, np.float32)}


INS = ["x", "p", "w_in", "g_mix", "g_q_nsa", "g_k_nsa", "g_q_dsa", "g_k_dsa", "pe_ck", "w_ck1", "w_ck2", "pe_cv", "w_cv1", "w_cv2",
       "w_branch_a", "w_branch_b", "w_out", "rel_bias", "g_ffn", "w_router", "b_router", "w_e1", "b_e1", "w_e2", "b_e2", "g_ple",
       "w_ple", "w_ple_gate"]


def kernel(**inputs):
    import concourse.bacc as bacc
    from concourse.bass_utils import run_bass_kernel_spmd

    nc = bacc.Bacc("TRN2", target_bir_lowering=False, num_devices=1)
    arrays = {n: np.ascontiguousarray(inputs[n]) for n in INS}
    arrays.update(constants())
    io = {n: nc.dram_tensor(f"in_{n}", a.shape, mybir.dt.from_np(a.dtype), kind="ExternalInput").ap() for n, a in arrays.items()}
    out = nc.dram_tensor("out_0", (1, SEQ, DM), F32, kind="ExternalOutput").ap()
    block_kernel(nc, io, out)
    r = run_bass_kernel_spmd(nc, [{f"in_{n}": a for n, a in arrays.items()}], core_ids=[0])
    return r.results[0]["out_0"]
```

```python
import math
from contextlib import ExitStack

import numpy as np
import concourse.bass as bass
from concourse import mybir

F32 = mybir.dt.float32
BF16 = mybir.dt.bfloat16
I32 = mybir.dt.int32
ALU = mybir.AluOpType
ACT = mybir.ActivationFunctionType
AX = mybir.AxisListType

P = 128
SEQ, DM = 256, 1024
TT = SEQ // P
KT = DM // P
DH, HEADS, GROUPS, HPG = 64, 8, 2, 4
CMP_LEN, CMP_STRIDE = 32, 16
NCMP = (SEQ - CMP_LEN) // CMP_STRIDE + 1
CMP_SEEN = [(P * (t + 1) - CMP_LEN) // CMP_STRIDE + 1 for t in range(TT)]
IH, ID = 8, 32
KEEP = 64
BUCKETS, MAX_EXACT, MAX_DIST = 32, 16, 128
NE, TOPK, DFF = 32, 4, 1024
LIMIT, ALPHA = 7.0, 1.702
EPS = 1e-6
NEG = -1e30
BLOCKED, TAKEN = -3e38, -3.4e38
PLE = 256
SLOTS = 64
ROUNDS = SEQ // SLOTS
PIECES = 12
UP = 8

O_NQ, O_KV, O_NG, O_DQ, O_DK, O_DV, O_IQ, O_IK, O_IW, O_GA = 0, 512, 1280, 1304, 1816, 2328, 2840, 3096, 3128, 3136
ZW = O_GA
CHUNKS = [(O_IQ, O_GA - O_IQ), (O_DQ, 512), (O_DK, 512), (O_NQ, 512), (O_KV, 512), (O_KV + 512, O_DQ - O_KV - 512),
          (O_DV, 512), (O_GA, 512), (O_GA + 512, 512), (O_GA + 1024, 512), (O_GA + 1536, 512)]
NZ = len(CHUNKS)
C_IX, C_DQ, C_DK, C_NQ, C_N1, C_N2, C_DV, C_G = range(8)

ORDER = ["ER", "T:G", "T:X0", "T:X1", "T:X2", "T:X3", "Z0", "Z1", "T:IX0", "T:IX1", "Z2", "I", "T:DQ0", "T:DQ1", "Z3",
         "T:DK0", "T:DK1", "Z4", "T:NQ0", "T:NQ1", "Z5", "Z6", "T:K0", "T:K1", "T:R0", "T:R1", "T:PE", "Z7", "HID", "Z8", "CMPKV", "Z9",
         "T:KC", "Z10", "T:CS"]
UNITS = [("dsa", t, j) for t in (0, 1) for j in range(4)] + [(b, t, j) for t in (0, 1) for j in range(4) for b in ("slc", "win")]
NU = len(UNITS)
C_SOFT = 2
C_AFTER = 4
TJOBS = [x for x in ORDER if x.startswith("T:")]
for _u in range(NU):
    TJOBS += [f"U{_u}"] + (["T:C0", "T:C1"] if _u == C_AFTER else [])
NT = len(TJOBS)
NITEM = 16


def item_of(u):
    return u if u < 8 else 8 + (u - 8) // 2


def block_kernel(nc, io, out):
    ctx = ExitStack()
    with ctx:
        def sb(name, words):
            return ctx.enter_context(nc.sbuf_tensor(name, [P, words], F32))

        def sem(name):
            return ctx.enter_context(nc.semaphore(name))

        ring = sb("ring", PIECES * 2048)
        wbuf = sb("wbuf", 4 * 4096)
        xres = sb("xres", TT * DM)
        hT = sb("hT", KT * SEQ)
        gat = sb("gat", TT * 2 * DM)
        oT = sb("oT", 2 * 4 * SEQ)
        misc = sb("misc", 2000)
        ps = [ctx.enter_context(nc.psum_tensor(f"ps{b}", [P, 512], F32)) for b in range(8)]

        class Take:
            def __init__(self, t, at=0):
                self.t, self.at = t, at

            def __call__(self, *shape, parts=P, dt=F32):
                n = int(np.prod(shape))
                words = n if dt != BF16 else (n + 1) // 2
                ap = self.t[0:parts, self.at:self.at + words]
                self.at += words
                if dt != F32:
                    ap = ap.bitcast(dt)
                if len(shape) == 2:
                    ap = ap.rearrange("p (a b) -> p a b", a=shape[0])
                if len(shape) == 3:
                    ap = ap.rearrange("p (a b c) -> p a b c", a=shape[0], b=shape[1])
                assert self.at <= self.t.shape[1], (self.at, self.t.shape)
                return ap

        def bc(ap, n):
            return ap.unsqueeze(len(ap.shape)).to_broadcast(list(ap.shape) + [n])

        def bm(ap, n):
            s = list(ap.shape)
            return ap.unsqueeze(1).to_broadcast([s[0], n] + s[1:])

        m = Take(misc)
        const_all = misc[:, 0:544]
        ident, tri, ones, iota1 = m(128), m(128), m(128), m(2, 64)
        idmod = m(NE)
        gT = m(24)
        gqk = m(4, DH)
        wr, br = m(KT, NE), m(NE)
        rs, ssx, ssx2 = m(2), m(2), m(2)
        half = m(64)
        Mt = m(TT, NE)
        top8, e4, lg, eq = m(TT, 8), m(TT, TOPK), m(TT, NE), m(TT, TOPK, NE)
        idx8 = m(TT, 8, dt=mybir.dt.uint32)
        idxf = m(TT, 8)
        sm2, cnt, cmax = m(TT, 2), m(NE), m(1)
        cmaxi = m(1, dt=I32)
        sel = m(SLOTS, parts=96, dt=BF16)
        S = m(TT, SLOTS, dt=BF16)

        w = Take(ring)
        z = w(TT, ZW)
        bias = w(16, SEQ)
        xn = ring[:, 22528:24576].rearrange("p (t d) -> p t d", t=TT)
        sq = ring[:, 21504:22528].rearrange("p (t d) -> p t d", t=TT)
        ikZ, rl = xn[:, 0, :].rearrange("p (a b) -> p a b", a=4), xn[:, 1, :].rearrange("p (a b) -> p a b", a=2)
        qaT, qdT = w(4, SEQ), w(4, SEQ)
        kZs, kZw = w(2, SEQ), w(2, SEQ)
        kZd = w(4, 2, SEQ)
        iqT = w(2, SEQ)
        zb = xn[:, 1, 0:2 * 16 * 30].rearrange("p (a l n) -> p a l n", a=2, l=16)
        score, selm = w(TT, SEQ), w(TT, SEQ)
        qn = w(TT, 512)
        PT = w(2, 4, P)
        rawT = PT.rearrange("p b a t -> p (b a t)").rearrange("p (a g t) -> p a g t", a=2, g=2)
        Bd = w(2, SEQ)
        work_small = Take(ring[:, 0:21504], w.at)
        V4 = work_small(2, 4, DH)
        kcZ = work_small(2, 16)
        kcs = work_small(2, DH, parts=16)
        kcq = work_small(2, DH, parts=16)
        hid, hsg = work_small(2, 30, parts=DH), work_small(2, 30, parts=DH)
        hid4 = work_small(2, 4, 32, parts=DH)
        peT = work_small(2, 16)
        m8 = work_small(8)
        iwS = work_small(TT, IH)
        gsig = work_small(TT, 24)
        v16 = work_small(TT, 8)
        r16 = work_small(TT, 8)
        mx, nmx, ssum, rcp = (work_small(4, 2) for _ in range(4))
        ckr = work_small(4)
        ck2w = work_small(2, DH, parts=DH)
        g0 = Take(gat)
        pe_in = g0(2, P, parts=16)
        grow = g0(P, parts=24)
        tab, onehot, erow = g0(16, parts=BUCKETS + 1), g0(384, parts=BUCKETS + 1), g0(384, parts=16)
        ot0 = Take(oT)
        P32 = ot0(TT, 8, 32)
        PcT = sq.rearrange("p t (g c) -> p t g c", g=4)[:, :, 0:2, :]
        cL, cst, csb = ot0(TT, 8, 16), ot0(TT, 4, 8), ot0(TT, P)
        wck1 = wbuf[:, 3 * 4096:3 * 4096 + 2048].rearrange("p (a l e) -> p a l e", a=2, l=16)
        L = hT[:, :].rearrange("p (b h s) -> p b h s", b=4, h=2)
        hTv = hT[:, :].rearrange("p (k t) -> p k t", k=KT)
        x = xres[:, :].rearrange("p (t d) -> p t d", t=TT)
        gates = gat[:, :].rearrange("p (t n) -> p t n", t=TT)
        oTv = oT[:, :].rearrange("p (m j t) -> p m j t", m=2, j=4)
        wa = wbuf[:, 0:4096].rearrange("p (j n) -> p j n", j=4)
        wb = wbuf[:, 4096:8192].rearrange("p (j n) -> p j n", j=4)
        wo = wbuf[:, 8192:16384].rearrange("p (k n) -> p k n", k=KT)
        merged, mtmp = xn, sq
        wple_g = wbuf[:, 0:8192].rearrange("p (k n) -> p k n", k=KT)
        wple = wbuf[:, 8192:10240].rearrange("p (k n) -> p k n", k=2)
        v = Take(wbuf, 10240)
        xeT = v(KT, SLOTS)
        gc, sg, lin, act, actT, oe = v(512), v(512), v(512), v(512), v(4, P), v(512)
        wS, wST = v(TT, P), v(TT * P)
        selx = v(8)
        rank = v(TT, ROUNDS * NE + 1)
        Wt = v(TT, ROUNDS * NE)
        be2, WT = oT[0:NE, 1024:2048], v(SEQ, parts=NE)
        hp = gat[:, 0:3072].bitcast(BF16).rearrange("p (q t d) -> p q t d", q=3, t=TT)
        b1p = gat[0:96, 3072:4096].bitcast(BF16)
        b1f = oT[0:96, :]
        xh = wbuf[:, 10240:12288].rearrange("p (t d) -> p t d", t=TT)
        xr = wbuf[:, 12288:14336].rearrange("p (t d) -> p t d", t=TT)
        pin, pT = oT[:, 0:512].rearrange("p (t d) -> p t d", t=TT), oT[:, 512:1024].rearrange("p (k t) -> p k t", k=2)
        xn3, sgate, xout = xn, sq, x
        ring3 = ring[:, :].rearrange("p (i n) -> p i n", i=PIECES)

        ERW = 384
        er_dram = nc.dram_tensor("rel_rows", [16, ERW], F32).ap()
        er_rep = nc.dram_tensor("rel_rows_repeated", [16, P, ERW], F32).ap()

        ld_const, ld_x, ld_small, ld_tab, ld_ck = sem("ld_const"), sem("ld_x"), sem("ld_small"), sem("ld_tab"), sem("ld_ck")
        ld_w = [sem(f"ld_w{i}") for i in range(3)]
        ld_wab, ld_wo, ld_bias, st_er, st_rep, ld_route, ld_b1, ld_be2, ld_p, ld_ple = (
            sem(n) for n in ("ld_wab", "ld_wo", "ld_bias", "st_er", "st_rep", "ld_route", "ld_b1", "ld_be2", "ld_p", "ld_ple"))
        piece = [sem(f"piece{i}") for i in range(PIECES)]
        zeroed, x_sq, x_rs, t_ps, t_ev, z_ps, z_ev = (
            sem(n) for n in ("zeroed", "x_sq", "x_rs", "t_ps", "t_ev", "z_ps", "z_ev"))
        ikrep_ready, i_ps, i_rl, i_used, score_cut, selm_ready = (
            sem(n) for n in ("ikrep_ready", "i_ps", "i_rl", "i_used", "score_cut", "selm_ready"))
        n_var, n_rs, qn_ready = sem("n_var"), sem("n_rs"), sem("qn_ready")
        er_ps, er_sb = sem("er_ps"), sem("er_sb")
        zb_ready, h_ps, h_exp, hid_ready, kc_ps, kc_copied, v4_ready, kcn_ready = (
            sem(n) for n in ("zb_ready", "h_ps", "h_exp", "hid_ready", "kc_ps", "kc_copied", "v4_ready", "kcn_ready"))
        c_log, c_exp, c_ready = sem("c_log"), sem("c_exp"), sem("c_ready")
        s_ps, s_log, s_exp, s_prob, bd_ready, o_ps, o_ev = (
            sem(n) for n in ("s_ps", "s_log", "s_exp", "s_prob", "bd_ready", "o_ps", "o_ev"))
        pr_ps, pr_used, mg_ready, wo_ps, x2_ready, f_sq, f_rs, xh_ready = (
            sem(n) for n in ("pr_ps", "pr_used", "mg_ready", "wo_ps", "x2_ready", "f_sq", "f_rs", "xh_ready"))
        rt_ps, lg_ready, rt_exp, m_ready, rk_ps, rank_ready, wt_ready, y_init, hp_ready, b1_ready, init0, xr_ready, dup_ready = (
            sem(n) for n in ("rt_ps", "lg_ready", "rt_exp", "m_ready", "rk_ps", "rank_ready", "wt_ready", "y_init",
                             "hp_ready", "b1_ready", "init0", "xr_ready", "dup_ready"))
        dve_ch, pool_ch, act_ch = sem("dve_chain"), sem("pool_chain"), sem("act_chain")

        class Chain:
            def __init__(self, eng, s):
                self.eng, self.s, self.n = eng, s, 0

            def __call__(self, ins):
                self.n += 1
                ins.then_inc(self.s, 1)
                self.eng.wait_ge(self.s, self.n)

        NORMS = [("dq", O_DQ, 8, 2, DH ** -0.5), ("dk", O_DK, 8, 3, 1.0), ("nq", O_NQ, 8, 0, DH ** -0.5),
                 ("ks", O_KV + 256, 2, 1, 1.0), ("kw", O_KV + 512, 2, 1, 1.0)]
        NORM_CHUNK = [C_DQ, C_DK, C_NQ, C_N1, C_N2]

        def expert_sems(tag):
            names = ("pieces_used", "s_ready", "sel_ready", "xe_ps", "xe_ready", "gc_ready", "lin_ready", "glu_ready", "sig_ready",
                     "act_ready", "at_ps", "at_ready", "wst_ps", "ws_ready", "wst_ready", "out_ready")
            return {n: sem(f"{n}_{tag}") for n in names}

        y_done = sem("y_done")
        w1 = io["w_e1"][0].rearrange("e (k p) n -> e k p n", p=P)
        w2 = io["w_e2"][0].rearrange("e (q r p) n -> e q p r n", r=2, p=P)
        first = dict(s=expert_sems("a"), piece=piece, col=0, visits=NE)
        rest = dict(s=expert_sems("b"), piece=[sem(f"piece_b{i}") for i in range(PIECES)], col=NE, visits=(ROUNDS - 1) * NE)

        def load(eng, e, i, signal):
            if i < UP:
                eng.dma_start(ring3[:, i, :], w1[e, i]).then_inc(signal[i], 16)
            else:
                eng.dma_start(ring3[:, i, :].rearrange("p (r n) -> p r n", r=2), w2[e, i - UP]).then_inc(signal[i], 16)

        def expert_pe(te, a):
            s, col = a["s"], a["col"]
            mm, tr = nc.tensor.matmul, nc.tensor.transpose
            G, Lb, O, T = ps[0], ps[1], ps[2], ps[3]

            def gather():
                for k in range(KT):
                    for t in range(TT):
                        for q in range(3):
                            l = mm(O[:, k * SLOTS:(k + 1) * SLOTS], hp[:, q, t, k * P:(k + 1) * P], S[:, t, :],
                                   start=t == 0 and q == 0, stop=t == TT - 1 and q == 2)
                l.then_inc(s["xe_ps"], 1)

            def scatter():
                for t in range(TT):
                    for n in range(2):
                        h = slice(n * SLOTS, (n + 1) * SLOTS)
                        l = mm(ps[4 + 2 * t + n][:, :], wST[h, t * P:(t + 1) * P], oe[h, :], start=False, stop=False, skip_group_check=True)
                return l

            te.wait_ge(s["s_ready"], 1)
            gather()
            with te.Fori(0, a["visits"]) as it:
                te.wait_ge(s["sel_ready"], it + 1)
                te.wait_ge(s["xe_ready"], it + 1)
                for n in range(4):
                    mm((G, Lb)[n // 2][(n % 2) * SLOTS:(n % 2 + 1) * SLOTS, :], sel, b1p[:, n * 512:(n + 1) * 512], start=True, stop=False)
                for k in range(UP):
                    te.wait_ge(a["piece"][k], it * 16 + 16)
                    for n in range(4):
                        l = mm((G, Lb)[n // 2][(n % 2) * SLOTS:(n % 2 + 1) * SLOTS, :], xeT[:, k, :], ring3[:, k, n * 512:(n + 1) * 512],
                               start=False, stop=k == UP - 1)
                    l.then_inc(s["pieces_used"], 1)
                te.wait_ge(s["out_ready"], it + 1)
                te.wait_ge(s["wst_ready"], it + 1)
                scatter()
                te.wait_ge(s["ws_ready"], it + 1)
                for t in range(TT):
                    l = tr(T[:, t * P:(t + 1) * P], wS[:, t, :], ident)
                l.then_inc(s["wst_ps"], 1)
                te.wait_ge(s["s_ready"], it + 2)
                gather()
                te.wait_ge(s["wst_ready"], it + 2)
                te.wait_ge(s["act_ready"], it + 1)
                for j in range(4):
                    l = tr(T[:, j * P:(j + 1) * P], act[:, j * P:(j + 1) * P], ident)
                l.then_inc(s["at_ps"], 1)
                te.wait_ge(s["at_ready"], it + 1)
                te.wait_ge(s["xe_ready"], it + 2)
                for i in range(UP, PIECES):
                    te.wait_ge(a["piece"][i], it * 16 + 16)
                    for r in range(2):
                        kt = 2 * (i - UP) + r
                        for n in range(2):
                            l = mm(O[n * SLOTS:(n + 1) * SLOTS, :], actT[:, kt % 4, (kt // 4) * SLOTS:(kt // 4 + 1) * SLOTS],
                                   ring3[:, i, r * DM + n * 512:r * DM + (n + 1) * 512], start=kt == 0, stop=kt == 7)
                    l.then_inc(s["pieces_used"], 1)
            te.wait_ge(s["out_ready"], a["visits"] + 1)
            te.wait_ge(s["wst_ready"], a["visits"] + 1)
            scatter().then_inc(y_done, 1)

        def expert_act(sc, a):
            s = a["s"]
            with sc.Fori(0, a["visits"]) as it:
                sc.wait_ge(s["gc_ready"], it + 1)
                nc.scalar.activation(sg, gc, ACT.Sigmoid, scale=ALPHA).then_inc(s["sig_ready"], 1)
                sc.wait_ge(s["wst_ps"], it + 1)
                nc.scalar.copy(wST, ps[3][:, 0:TT * P]).then_inc(s["wst_ready"], 1)
                sc.wait_ge(s["at_ps"], it + 1)
                nc.scalar.copy(actT.rearrange("p j t -> p (j t)"), ps[3][:, :]).then_inc(s["at_ready"], 1)
                sc.wait_ge(s["pieces_used"], it * PIECES + PIECES)
                nc.scalar.copy(oe, ps[2][:, :]).then_inc(s["out_ready"], 1)

        def expert_dve(ve, a):
            s, col, d = a["s"], a["col"], nc.vector
            i1 = iota1[:, 0, :]

            def one_hot(c):
                for t in range(TT):
                    l = d.tensor_scalar(S[:, t, :], i1, rank[:, t, c], None, ALU.is_equal)
                l.then_inc(s["s_ready"], 1)

            def take_rows():
                d.tensor_tensor(xeT, ps[2][:, :].rearrange("p (k c) -> p k c", k=KT), bc(gT[:, 8:16], SLOTS), ALU.mult).then_inc(s["xe_ready"], 1)

            ve.wait_ge(hp_ready, 2)
            d.memset(oe, 0.0).then_inc(s["out_ready"], 1)
            d.memset(wST, 0.0).then_inc(s["wst_ready"], 1)
            one_hot(slice(col, col + 1))
            ve.wait_ge(s["xe_ps"], 1)
            take_rows()
            with ve.Fori(0, a["visits"]) as it:
                if a is first:
                    e = bass.ds(it, 1)
                else:
                    e = bass.ds(it % NE, 1)
                d.tensor_copy(sel, idmod[0:96, e].to_broadcast([96, SLOTS])).then_inc(s["sel_ready"], 1)
                one_hot(bass.ds(it + (col + 1), 1))
                for t in range(TT):
                    l = d.tensor_scalar(wS[:, t, :], iota1.rearrange("p a b -> p (a b)"), rank[:, t, bass.ds(it + col, 1)],
                                        Wt[:, t, bass.ds(it + col, 1)], ALU.is_equal, ALU.mult)
                l.then_inc(s["ws_ready"], 1)
                ve.wait_ge(s["pieces_used"], it * PIECES + UP)
                d.tensor_scalar(gc, ps[0][:, :], LIMIT, None, ALU.min).then_inc(s["gc_ready"], 1)
                d.tensor_scalar(lin, ps[1][:, :], LIMIT, -LIMIT, ALU.min, ALU.max).then_inc(s["lin_ready"], 1)
                ve.wait_ge(s["gc_ready"], it + 1)
                ve.wait_ge(s["lin_ready"], it + 1)
                d.scalar_tensor_tensor(lin, lin, 1.0, gc, ALU.add, ALU.mult).then_inc(s["glu_ready"], 1)
                ve.wait_ge(s["glu_ready"], it + 1)
                ve.wait_ge(s["sig_ready"], it + 1)
                d.tensor_tensor(act, lin, sg, ALU.mult).then_inc(s["act_ready"], 1)
                ve.wait_ge(s["xe_ps"], it + 2)
                take_rows()

        with nc.Block() as block:
            @block.sync
            def _(sp):
                sp.dma_start(x[:, :, :], io["x"][0].rearrange("(t p) d -> p t d", p=P)).then_inc(ld_x, 16)
                sp.wait_ge(ld_x, 16)
                w_in = io["w_in"][0].rearrange("(k p) n -> p k n", p=P)
                for c, (o, n) in enumerate(CHUNKS):
                    if c >= 3:
                        sp.wait_ge(z_ps, 2 * (c - 2))
                    dst = wbuf[:, (c % 3) * 4096:(c % 3) * 4096 + KT * n].rearrange("p (k n) -> p k n", k=KT)
                    sp.dma_start(dst, w_in[:, :, o:o + n]).then_inc(ld_w[c % 3], 16)
                    if c == 2:
                        for a, name in enumerate(("w_ck1", "w_cv1")):
                            sp.dma_start(wck1[:, a], io[name][0].rearrange("(l q) d e -> (q d) l e", q=2)).then_inc(ld_ck, 16)
                sp.wait_ge(z_ps, 2 * NZ)
                for g in range(2):
                    sp.dma_start(wa[g * DH:(g + 1) * DH], io["w_branch_a"][0].rearrange("(g j d) n -> g d j n", g=2, j=4)[g]).then_inc(ld_wab, 16)
                sp.dma_start(wb[:, :, :], io["w_branch_b"][0].rearrange("(j p) n -> p j n", p=P)).then_inc(ld_wab, 16)
                sp.wait_ge(h_ps, 1)
                sp.dma_start(wo[:, :, :], io["w_out"][0].rearrange("(k p) n -> p k n", p=P)).then_inc(ld_wo, 16)
                sp.wait_ge(o_ev, NITEM)
                for i in range(10):
                    load(sp, 0, i, piece)
                sp.wait_ge(pr_used, 4)
                for q in range(3):
                    sp.dma_start(b1f[q * NE:(q + 1) * NE, :], io["b_e1"][0]).then_inc(ld_b1, 16)
                sp.dma_start(wple_g, io["w_ple_gate"][0].rearrange("(k p) n -> p k n", p=P)).then_inc(ld_ple, 16)
                sp.wait_ge(t_ev, NT + 4)
                for i in range(10, PIECES):
                    load(sp, 0, i, piece)
                sp.wait_ge(b1_ready, 1)
                sp.dma_start(be2, io["b_e2"][0]).then_inc(ld_be2, 16)
                sp.dma_start(pin, io["p"][0, 0].rearrange("(t p) d -> p t d", p=P)).then_inc(ld_p, 16)
                sp.wait_ge(wo_ps, 4)
                sp.dma_start(wple, io["w_ple"][0].rearrange("(k p) n -> p k n", p=P)).then_inc(ld_ple, 16)
                with sp.Fori(1, NE) as e:
                    for i in range(PIECES):
                        sp.wait_ge(first["s"]["pieces_used"], e * PIECES - PIECES + (i + 1))
                        load(sp, e, i, piece)

            @block.gpsimd
            def _(pool):
                ch = Chain(pool, pool_ch)
                g = nc.gpsimd
                ch(g.memset(half, -0.5))
                for a in (kZs, kZw):
                    ch(g.memset(a[0:DH, 1, :], 0.0))
                    ch(g.memset(a[DH:P, 0, :], 0.0))
                ch(g.memset(kZd[0:DH, :, 1, :], 0.0))
                ch(g.memset(kZd[DH:P, :, 0, :], 0.0))
                ch(g.memset(V4, 0.0))
                ch(g.memset(kcZ, 0.0))
                ch(g.memset(hid4, 0.0))
                g.memset(P32, 0.0).then_inc(zeroed, 1)

                def rsqrt(dst, src, scale, done):
                    ch(g.tensor_scalar(dst, src, scale, EPS, ALU.mult, ALU.add))
                    n = src.shape
                    e = half[0:n[0], 0:int(np.prod(n[1:]))]
                    if len(n) == 3:
                        e = e.rearrange("p (a b) -> p a b", a=n[1])
                    g.tensor_tensor(dst, dst, e, ALU.pow).then_inc(done, 1)

                pool.wait_ge(zeroed, 1)
                pool.wait_ge(x_sq, 1)
                rsqrt(rs, ssx, 1.0 / DM, x_rs)
                pool.wait_ge(er_sb, 1)
                pool.dma_start(er_dram, erow).then_inc(st_er, 16)
                pool.wait_ge(st_er, 16)
                pool.dma_start(er_rep, er_dram.unsqueeze(1).to_broadcast([16, P, ERW])).then_inc(st_rep, 16)
                pool.wait_ge(st_rep, 16)
                pool.dma_start(bias, bass.AP(tensor=er_rep.tensor, offset=P - 1, ap=[[ERW - 1, P], [P * ERW, 16], [1, SEQ]])).then_inc(ld_bias, 16)
                g.memset(ikZ, 0.0).then_inc(zeroed, 1)
                for n in range(2):
                    pool.wait_ge(n_var, n + 1)
                    rsqrt(v16, r16, 1.0 / DH, n_rs)
                pool.wait_ge(i_used, 6)
                for t in range(TT):
                    n = P * (t + 1)
                    g.affine_select(out=score[:, t, 0:n], in_=score[:, t, 0:n], compare_op=ALU.is_ge, fill=BLOCKED, base=t * P,
                                    pattern=[[-1, n]], channel_multiplier=1).then_inc(score_cut, 1)
                for n in range(2, 5):
                    pool.wait_ge(n_var, n + 1)
                    h = NORMS[n][2]
                    rsqrt(v16[:, :, 0:h], r16[:, :, 0:h], 1.0 / DH, n_rs)
                pool.wait_ge(n_var, 6)
                rsqrt(ckr[0:NCMP, 0:2], ckr[0:NCMP, 2:4], 1.0 / DH, n_rs)
                pool.wait_ge(ld_bias, 16)
                pool.wait_ge(selm_ready, 2)
                for u in range(8):
                    _, t, j = UNITS[u]
                    n = P * (t + 1)
                    o = P * (1 - t)
                    if u >= 1:
                        pool.wait_ge(s_log, u)
                    g.tensor_tensor(Bd[:, :, 0:n], bias[:, 8 + 2 * j:10 + 2 * j, o:o + n], bm(selm[:, t, 0:n], 2),
                                    ALU.add).then_inc(bd_ready, 1)
                pool.wait_ge(f_sq, 1)
                rsqrt(rs, ssx, 1.0 / DM, f_rs)

            @block.scalar
            def _(sc):
                a = nc.scalar
                cst = io["consts"]
                sc.dma_start(const_all, cst).then_inc(ld_const, 16)
                for i, n in enumerate(("g_mix", "g_ffn", "g_ple")):
                    sc.dma_start(grow[i * 8:(i + 1) * 8, :], io[n][0].rearrange("(k p) -> k p", p=P)).then_inc(ld_const, 16)
                sc.dma_start(tab[0:BUCKETS, :], io["rel_bias"]).then_inc(ld_tab, 16)
                sc.dma_start(tab[BUCKETS:BUCKETS + 1, :], io["negrow"]).then_inc(ld_tab, 16)
                sc.dma_start(onehot, io["onehot"]).then_inc(ld_tab, 16)
                for i, n in enumerate(("g_q_nsa", "g_k_nsa", "g_q_dsa", "g_k_dsa")):
                    sc.dma_start(gqk[:, i, :], io[n].to_broadcast([P, DH])).then_inc(ld_small, 16)
                for i, n in enumerate(("pe_ck", "pe_cv")):
                    sc.dma_start(pe_in[:, i, :], io[n][0].rearrange("(l q) d -> l (q d)", q=2)).then_inc(ld_small, 16)
                for i, n in enumerate(("w_ck2", "w_cv2")):
                    sc.dma_start(ck2w[:, i, :], io[n][0]).then_inc(ld_small, 16)
                sc.dma_start(wr, io["w_router"][0].rearrange("(k p) n -> p k n", p=P)).then_inc(ld_route, 16)
                sc.dma_start(br, io["b_router"].to_broadcast([P, NE])).then_inc(ld_route, 16)

                def tjob(name):
                    n = TJOBS.index(name)
                    b = ps[4 + n % 2]
                    sc.wait_ge(t_ps, n + 1)
                    t = int(name[-1]) if name[-1].isdigit() else 0
                    tc = slice(t * P, (t + 1) * P)
                    kind = name[2:].rstrip("0123456789")
                    if kind == "G":
                        a.copy(gT, b[:, 0:24]).then_inc(t_ev, 1)
                        sc.wait_ge(t_ev, n + 1)
                    elif kind == "X":
                        for i in range(2):
                            k = 2 * t + i
                            l = a.activation(hTv[:, k, :], b[:, i * SEQ:(i + 1) * SEQ], ACT.Copy, scale=gT[:, k:k + 1])
                        l.then_inc(t_ev, 1)
                    elif kind == "IX":
                        sc.wait_ge(zeroed, 2)
                        a.copy(iqT[:, :, tc], b[:, 0:2 * P].rearrange("p (a t) -> p a t", a=2))
                        for i in range(4):
                            l = a.copy(ikZ[32 * i:32 * i + 32, i, tc], b[32 * i:32 * i + 32, 2 * P:3 * P])
                        l.then_inc(t_ev, 1)
                    elif kind in ("DQ", "NQ"):
                        q = qdT if kind == "DQ" else qaT
                        a.copy(q[:, :, tc], b[:, :].rearrange("p (j t) -> p j t", j=4)).then_inc(t_ev, 1)
                    elif kind == "DK":
                        v4 = b[:, :].rearrange("p (j t) -> p j t", j=4)
                        a.copy(kZd[0:DH, :, 0, tc], v4[0:DH])
                        a.copy(kZd[DH:P, :, 1, tc], v4[DH:P]).then_inc(t_ev, 1)
                    elif kind == "K":
                        for i, kz in enumerate((kZs, kZw)):
                            for g in range(2):
                                l = a.copy(kz[g * DH:(g + 1) * DH, g, tc], b[g * DH:(g + 1) * DH, i * P:(i + 1) * P])
                        l.then_inc(t_ev, 1)
                    elif kind == "R":
                        a.copy(rawT[:, :, :, tc], b[:, :].rearrange("p (a g t) -> p a g t", a=2, g=2)).then_inc(t_ev, 1)
                    elif kind == "PE":
                        a.copy(peT, b[:, 0:32].rearrange("p (a l) -> p a l", a=2)).then_inc(t_ev, 1)
                    elif kind == "KC":
                        for g in range(2):
                            l = a.copy(kcZ[g * DH:(g + 1) * DH, g, 0:NCMP], b[g * DH:(g + 1) * DH, 0:NCMP])
                        l.then_inc(t_ev, 1)
                    elif kind == "CS":
                        a.copy(csb, b[:, 0:2 * P].rearrange("p (t n) -> p t n", t=TT)).then_inc(t_ev, 1)
                    elif kind == "C":
                        a.copy(PcT[:, t], b[:, 0:2 * P].rearrange("p (a t) -> p a t", a=2)).then_inc(t_ev, 1)

                for stage in ORDER:
                    if stage.startswith("T:"):
                        tjob(stage)
                    elif stage == "ER":
                        sc.wait_ge(er_ps, 1)
                        a.copy(erow, ps[6][0:16, 0:384]).then_inc(er_sb, 1)
                    elif stage[0] == "Z":
                        c = int(stage[1:])
                        o, n = CHUNKS[c]
                        for t in range(TT):
                            sc.wait_ge(z_ps, 2 * c + t + 1)
                            src = ps[2 * (c % 2) + t][:, 0:n]
                            if c == 0 and t == 0:
                                sc.wait_ge(x_rs, 1)
                            if o < O_GA:
                                a.activation(z[:, t, o:o + n], src, ACT.Copy, scale=rs[:, t:t + 1]).then_inc(z_ev, 1)
                            else:
                                if c == C_G and t == 0:
                                    sc.wait_ge(st_er, 16)
                                a.activation(gates[:, t, o - O_GA:o - O_GA + n], src, ACT.Sigmoid, scale=rs[:, t:t + 1]).then_inc(z_ev, 1)
                        if c == C_G:
                            a.activation(gsig, z[:, :, O_NG:O_NG + 24], ACT.Sigmoid)
                    elif stage == "I":
                        for i in range(6):
                            sc.wait_ge(i_ps, i + 1)
                            if i >= 2:
                                sc.wait_ge(i_used, i - 1)
                            a.activation(rl[:, i % 2, :], ps[7 - i % 2][:, :], ACT.Relu).then_inc(i_rl, 1)
                    elif stage == "HID":
                        sc.wait_ge(h_ps, 1)
                        a.activation(hsg, ps[7][0:DH, 0:60].rearrange("p (a n) -> p a n", a=2), ACT.Exp, scale=-1.0).then_inc(h_exp, 1)
                    elif stage == "CMPKV":
                        sc.wait_ge(kc_copied, 1)
                        sc.wait_ge(zeroed, 1)
                        for g in range(2):
                            for j in range(4):
                                l = a.copy(V4[32 * j:32 * j + 32, g, j, :], ps[6][32 * j:32 * j + 32, (2 + g) * DH:(3 + g) * DH])
                        l.then_inc(v4_ready, 1)
                def exps(u):
                    n = P * (UNITS[u][1] + 1)
                    sc.wait_ge(s_log, u + 1)
                    for h in range(2):
                        l = a.activation(L[:, u % 4, h, 0:n], L[:, u % 4, h, 0:n], ACT.Exp, bias=nmx[:, u % 4, h:h + 1], accum_out=ssum[:, u % 4, h:h + 1])
                    l.then_inc(s_exp, 1)

                def evac_p(u):
                    nb = UNITS[u][1] + 1
                    n = TJOBS.index(f"U{u}")
                    sc.wait_ge(t_ps, n + 1)
                    if u >= 2:
                        sc.wait_ge(o_ps, u - 1)
                    a.copy(PT[:, u % 2, 0:2 * nb, :], ps[4 + n % 2][:, 0:2 * nb * P].rearrange("p (a t) -> p a t", t=P)).then_inc(t_ev, 1)

                def evac_o(u):
                    if u >= 8 and (u - 8) % 2 == 0:
                        return
                    i = item_of(u)
                    kind, t, j = UNITS[u]
                    sc.wait_ge(o_ps, u + 1)
                    a.copy(oTv[:, 1 if i < 8 else 0, j, t * P:(t + 1) * P], ps[6 + i % 2][:, 0:P]).then_inc(o_ev, 1)

                for u in range(NU + 3):
                    if u < NU:
                        exps(u)
                    if u == C_SOFT:
                        for t in range(TT):
                            n = CMP_SEEN[t]
                            sc.wait_ge(c_log, t + 1)
                            a.activation(cL[:, t, :, 0:n], cL[:, t, :, 0:n], ACT.Exp).then_inc(c_exp, 1)
                    if 2 <= u < NU + 2:
                        evac_p(u - 2)
                        if u - 2 == C_AFTER:
                            tjob("T:C0")
                            tjob("T:C1")
                    if u >= 3:
                        evac_o(u - 3)
                for n in range(4):
                    k = NT + n
                    sc.wait_ge(t_ps, k + 1)
                    a.copy(hTv[:, 2 * n:2 * n + 2, :], ps[4 + k % 2][:, :].rearrange("p (k t) -> p k t", k=2)).then_inc(t_ev, 1)
                for n in range(4):
                    k = NT + 4 + n
                    sc.wait_ge(t_ps, k + 1)
                    for i in range(2):
                        kk = 2 * n + i
                        l = a.activation(hTv[:, kk, :], ps[4 + k % 2][:, i * SEQ:(i + 1) * SEQ], ACT.Copy, scale=gT[:, 8 + kk:9 + kk])
                    l.then_inc(t_ev, 1)
                sc.wait_ge(xr_ready, 1)
                a.copy(hp[:, 1], xr).then_inc(hp_ready, 1)
                sc.wait_ge(lg_ready, 1)
                a.activation(e4, e4, ACT.Exp).then_inc(rt_exp, 1)
                sc.wait_ge(xr_ready, 2)
                a.copy(hp[:, 2], xr).then_inc(hp_ready, 1)
                k = NT + 8
                sc.wait_ge(t_ps, k + 1)
                a.copy(WT, ps[4 + k % 2][0:NE, 0:SEQ]).then_inc(t_ev, 1)
                expert_act(sc, first)

            @block.vector
            def _(ve):
                d = nc.vector
                ch = Chain(ve, dve_ch)
                def squares(junk, done):
                    for t in range(TT):
                        l = d.tensor_tensor_reduce(out=junk[:, t, :], in0=x[:, t, :], in1=x[:, t, :], scale=1.0, scalar=0.0,
                                                   op0=ALU.mult, op1=ALU.add, accum_out=ssx[:, t:t + 1])
                    l.then_inc(done, 1)

                ve.wait_ge(ld_x, 16)
                squares(xn, x_sq)

                def norm_sq(n):
                    _, o, h, _, _ = NORMS[n]
                    ve.wait_ge(z_ev, 2 * (NORM_CHUNK[n] + 1))
                    src = z[:, :, o:o + h * DH]
                    ch(d.tensor_tensor(sq[:, :, 0:h * DH], src, src, ALU.mult))
                    d.tensor_reduce(r16[:, :, 0:h], sq[:, :, 0:h * DH].rearrange("p t (h e) -> p t h e", h=h), AX.X, ALU.add).then_inc(n_var, 1)

                def norm_mul(n, at):
                    name, o, h, g, s = NORMS[n]
                    ve.wait_ge(n_rs, n + 1)
                    if s != 1.0:
                        ch(d.tensor_scalar(v16[:, :, 0:h], v16[:, :, 0:h], s, None, ALU.mult))
                    for t in range(TT):
                        src = z[:, t, o:o + h * DH].rearrange("p (h e) -> p h e", h=h)
                        ch(d.tensor_tensor(sq[:, t, 0:h * DH].rearrange("p (h e) -> p h e", h=h), src, bc(v16[:, t, 0:h], DH), ALU.mult))
                    for t in range(TT):
                        dst = qn[:, t, at:at + h * DH]
                        if name == "nq":
                            dst = dst.rearrange("p (j g e) -> p g j e", j=4, g=2)
                            src = sq[:, t, :].rearrange("p (g j e) -> p g j e", g=2, j=4)
                            for g2 in range(2):
                                l = d.tensor_tensor(dst[:, g2], src[:, g2], bm(gqk[:, g, :], 4), ALU.mult)
                        else:
                            l = d.tensor_tensor(dst.rearrange("p (h e) -> p h e", h=h), sq[:, t, 0:h * DH].rearrange("p (h e) -> p h e", h=h),
                                                bm(gqk[:, g, :], h), ALU.mult)
                    ch_sig(l)

                def ch_sig(l):
                    qn_n[0] += 1
                    l.then_inc(qn_ready, 1)
                    ve.wait_ge(qn_ready, qn_n[0])
                qn_n = [0]

                ve.wait_ge(z_ev, 2)
                for t in range(TT):
                    d.tensor_copy(qn[:, t, 0:P].rearrange("p (r e) -> p r e", r=4), bm(z[:, t, O_IK:O_IK + ID], 4))
                ch(d.tensor_scalar(iwS, z[:, :, O_IW:O_IW + IH], ID ** -0.5 * IH ** -0.5, None, ALU.mult))
                ch(d.memset(score, 0.0))
                d.memset(m8, 0.0).then_inc(ikrep_ready, 1)
                ve.wait_ge(ld_small, 16 * 8)
                norm_sq(0)
                ve.wait_ge(t_ps, TJOBS.index("T:IX1") + 1)
                norm_mul(0, 0)
                for i in range(6):
                    ve.wait_ge(i_rl, i + 1)
                    if i < 4:
                        parts = [(1, 4 * (i // 2) + 2 * (i % 2) + r, rl[:, i % 2, r * SEQ:(r + 1) * SEQ], SEQ) for r in range(2)]
                    else:
                        parts = [(0, 4 * (i - 4) + r, rl[:, i % 2, r * P:(r + 1) * P], P) for r in range(4)]
                    for q, (t, h, src, n) in enumerate(parts):
                        l = d.scalar_tensor_tensor(score[:, t, 0:n], src, iwS[:, t, h:h + 1], score[:, t, 0:n], ALU.mult, ALU.add)
                        if q < len(parts) - 1:
                            ch(l)
                    l.then_inc(i_used, 1)
                    ve.wait_ge(i_used, i + 1)
                norm_sq(1)
                ve.wait_ge(t_ps, TJOBS.index("T:DQ1") + 1)
                norm_mul(1, 0)

                def topk(t):
                    ve.wait_ge(score_cut, t + 1)
                    n = P * (t + 1)
                    for r in range(KEEP // 8):
                        ch(d.max(m8, score[:, t, 0:n]))
                        ch(d.match_replace(score[:, t, 0:n], m8, score[:, t, 0:n], TAKEN))
                    d.tensor_scalar(selm[:, t, 0:n], score[:, t, 0:n], (BLOCKED + TAKEN) / 2, NEG, ALU.is_gt, ALU.mult).then_inc(selm_ready, 1)

                topk(0)
                norm_sq(2)
                ve.wait_ge(t_ps, TJOBS.index("T:DK1") + 1)
                norm_mul(2, 0)
                topk(1)
                norm_sq(3)
                ve.wait_ge(t_ps, TJOBS.index("T:NQ1") + 1)
                norm_mul(3, 0)
                norm_sq(4)
                norm_mul(4, P)
                for t in range(TT):
                    src = z[:, t, O_KV:O_KV + 4 * DH].rearrange("p (i e) -> p i e", i=4).unsqueeze(2).to_broadcast([P, 4, 2, DH])
                    l = d.tensor_copy(sq[:, t, :].rearrange("p (i r e) -> p i r e", i=4, r=2), src)
                l.then_inc(dup_ready, 1)
                ve.wait_ge(t_ev, TJOBS.index("T:PE") + 1)
                for kv in range(2):
                    for q in range(2):
                        for hf in range(2):
                            h = slice(q * DH, (q + 1) * DH)
                            src = rawT[h, kv].rearrange("p g (c l q) -> p l g c q", l=8, q=2)[:, :, :, hf:hf + NCMP, q]
                            pe = peT[h, kv, hf * 8:(hf + 1) * 8].unsqueeze(2).unsqueeze(3).to_broadcast([DH, 8, 2, NCMP])
                            l = d.tensor_tensor(zb[h, kv, hf * 8:(hf + 1) * 8].rearrange("p l (g c) -> p l g c", g=2), src, pe, ALU.add)
                l.then_inc(zb_ready, 1)
                ve.wait_ge(h_exp, 1)
                ch(d.tensor_scalar(hsg, hsg, 1.0, None, ALU.add))
                ch(d.reciprocal(hsg, hsg))
                ch(d.tensor_tensor(hid, hsg, ps[7][0:DH, 0:60].rearrange("p (a n) -> p a n", a=2), ALU.mult))
                ve.wait_ge(zeroed, 1)
                for g in range(2):
                    l = d.tensor_copy(hid4[:, g, :, 0:NCMP], bm(hid[:, 1, g * NCMP:(g + 1) * NCMP], 4))
                l.then_inc(hid_ready, 1)
                ve.wait_ge(kc_ps, 1)
                d.tensor_copy(kcs[0:NCMP], ps[6][0:NCMP, 0:2 * DH].rearrange("p (g e) -> p g e", g=2)).then_inc(kc_copied, 1)
                ve.wait_ge(kc_copied, 1)
                kc = kcs[0:NCMP]
                ch(d.tensor_tensor(kcq[0:NCMP], kc, kc, ALU.mult))
                d.tensor_reduce(ckr[0:NCMP, 2:4], kcq[0:NCMP], AX.X, ALU.add).then_inc(n_var, 1)
                ve.wait_ge(n_rs, 6)
                ch(d.tensor_tensor(kcq[0:NCMP], kc, bc(ckr[0:NCMP, 0:2], DH), ALU.mult))
                d.tensor_tensor(kcs[0:NCMP], kcq[0:NCMP], bm(gqk[0:NCMP, 1, :], 2), ALU.mult).then_inc(kcn_ready, 1)
                def mark(ins):
                    ch.n += 1
                    ins.then_inc(dve_ch, 1)
                    return ch.n

                def compressed():
                    ve.wait_ge(t_ev, TJOBS.index("T:CS") + 1)
                    lv = [cL[:, t, :, 0:CMP_SEEN[t]] for t in range(TT)]
                    for t in range(TT):
                        n, o = CMP_SEEN[t], P * (1 - t) + CMP_LEN - 1
                        for g in range(2):
                            src = csb[:, t, :].rearrange("p (j g c) -> p g j c", j=4, g=2)[:, g, :, 0:n]
                            bv = bias[:, 4 * g:4 * g + 4, o:o + (n - 1) * CMP_STRIDE + 1:CMP_STRIDE]
                            l = mark(d.tensor_tensor(cL[:, t, 4 * g:4 * g + 4, 0:n], src, bv, ALU.add))
                    ve.wait_ge(dve_ch, l)
                    for t in range(TT):
                        l = mark(d.tensor_reduce(cst[:, t, 0, :], lv[t], AX.X, ALU.max))
                    ve.wait_ge(dve_ch, l)
                    ch(d.tensor_scalar(cst[:, :, 1, :], cst[:, :, 0, :], NEG / 10, None, ALU.max))
                    for t in range(TT):
                        d.tensor_tensor(lv[t], lv[t], bc(cst[:, t, 1, :], CMP_SEEN[t]), ALU.subtract).then_inc(c_log, 1)

                def compressed_end():
                    lv = [cL[:, t, :, 0:CMP_SEEN[t]] for t in range(TT)]
                    ve.wait_ge(c_exp, 2)
                    for t in range(TT):
                        l = mark(d.tensor_reduce(cst[:, t, 2, :], lv[t], AX.X, ALU.add))
                    ve.wait_ge(dve_ch, l)
                    ch(d.tensor_scalar(cst[:, :, 2, :], cst[:, :, 2, :], 1e-30, None, ALU.max))
                    ch(d.reciprocal(cst[:, :, 3, :], cst[:, :, 2, :]))
                    ch(d.tensor_tensor(cst[:, :, 3, :], cst[:, :, 3, :], gsig[:, :, 0:24:3], ALU.mult))
                    for t in range(TT):
                        d.tensor_tensor(P32[:, t, :, 0:CMP_SEEN[t]], lv[t], bc(cst[:, t, 3, :], CMP_SEEN[t]), ALU.mult).then_inc(c_ready, 1)

                ve.wait_ge(ld_bias, 16)
                for u in range(NU + 1):
                    if u >= 1:
                        kp, tp, jp = UNITS[u - 1]
                        rp = rcp[:, (u - 1) % 4, :]
                        ve.wait_ge(s_exp, u)
                        last = mark(d.tensor_scalar(rp, ssum[:, (u - 1) % 4, :], 1e-30, None, ALU.max))
                    for h in range(2):
                        if u < NU:
                            kind, t, j = UNITS[u]
                            n, o = P * (t + 1), P * (1 - t)
                            if h == 0:
                                ve.wait_ge(s_ps, u + 1)
                                if kind == "dsa":
                                    ve.wait_ge(bd_ready, u + 1)
                                if u >= 4:
                                    ve.wait_ge(t_ps, TJOBS.index(f"U{u - 4}") + 1)
                            b = Bd[:, h, 0:n] if kind == "dsa" else bias[:, 4 * h + j, o:o + n]
                            top = mark(d.tensor_tensor_reduce(out=L[:, u % 4, h, 0:n], in0=ps[u % 4][:, h * n:(h + 1) * n], in1=b, scale=1.0,
                                                              scalar=NEG * 10, op0=ALU.add, op1=ALU.max, accum_out=mx[:, u % 4, h:h + 1]))
                        if u >= 1 and h == 0:
                            ve.wait_ge(dve_ch, last)
                            last = mark(d.reciprocal(rp, rp))
                    if u >= 1 and kp != "dsa":
                        b = 1 if kp == "slc" else 2
                        ve.wait_ge(dve_ch, last)
                        last = mark(d.tensor_tensor(rp, rp, gsig[:, tp, 3 * jp + b:3 * jp + b + 13:12], ALU.mult))
                    if u < NU:
                        ve.wait_ge(dve_ch, top)
                        d.tensor_scalar(nmx[:, u % 4, :], mx[:, u % 4, :], -1.0, None, ALU.mult).then_inc(s_log, 1)
                    if u >= 1:
                        n = P * (tp + 1)
                        ve.wait_ge(dve_ch, last)
                        for h in range(2):
                            l = d.tensor_scalar(L[:, (u - 1) % 4, h, 0:n], L[:, (u - 1) % 4, h, 0:n], rp[:, h:h + 1], None, ALU.mult)
                        l.then_inc(s_prob, 1)
                    if u == C_SOFT:
                        compressed()
                    if u == C_SOFT + 1:
                        compressed_end()

                for i in range(4):
                    t, n = i // 2, (i % 2) * 512
                    ve.wait_ge(pr_ps, i + 1)
                    ch(d.tensor_tensor(mtmp[:, 0, :], ps[2 * (i % 2)][:, :], gates[:, t, n:n + 512], ALU.mult))
                    ch(d.tensor_tensor(mtmp[:, 1, :], ps[2 * (i % 2) + 1][:, :], gates[:, t, DM + n:DM + n + 512], ALU.mult))
                    d.tensor_tensor(merged[:, t, n:n + 512], mtmp[:, 0, :], mtmp[:, 1, :], ALU.add).then_inc(pr_used, 1)
                    ve.wait_ge(pr_used, i + 1)
                ve.wait_ge(ld_b1, 48)
                ch(d.tensor_copy(b1p, b1f))
                for lo in (NE, 2 * NE, 2 * NE):
                    hi = lo + NE
                    ch(d.tensor_tensor(b1f[lo:hi], b1f[lo:hi], b1p[lo:hi], ALU.subtract))
                    l = d.tensor_copy(b1p[lo:hi], b1f[lo:hi])
                    ch(l)
                d.memset(ssx2, 0.0).then_inc(b1_ready, 1)
                for i in range(4):
                    t, n = i // 2, (i % 2) * 512
                    ve.wait_ge(wo_ps, i + 1)
                    d.tensor_tensor(x[:, t, n:n + 512], ps[i][:, :], x[:, t, n:n + 512], ALU.add).then_inc(x2_ready, 1)
                ve.wait_ge(x2_ready, 4)
                squares(xh, f_sq)
                ve.wait_ge(f_rs, 1)
                for t in range(TT):
                    l = d.tensor_scalar(xh[:, t, :], x[:, t, :], rs[:, t:t + 1], None, ALU.mult)
                l.then_inc(xh_ready, 1)
                ve.wait_ge(xh_ready, 1)
                ch(d.tensor_copy(hp[:, 0], xh))
                d.tensor_tensor(xr, xh, hp[:, 0], ALU.subtract).then_inc(xr_ready, 1)
                ve.wait_ge(rt_ps, 1)
                ve.wait_ge(ld_route, 32)
                for t in range(TT):
                    l = d.scalar_tensor_tensor(lg[:, t, :], ps[6][:, t * NE:(t + 1) * NE], rs[:, t:t + 1], br, ALU.mult, ALU.add)
                ch(l)
                for t in range(TT):
                    ch(d.max(top8[:, t, :], lg[:, t, :]))
                d.tensor_tensor(e4, top8[:, :, 0:TOPK], bc(top8[:, :, 0], TOPK), ALU.subtract).then_inc(lg_ready, 1)
                for t in range(TT):
                    l = d.max_index(idx8[:, t, :], top8[:, t, :], lg[:, t, :])
                ch(l)
                ch(d.tensor_copy(idxf, idx8))
                ch(d.tensor_scalar(idxf, idxf, 1.0, None, ALU.add))
                ch(d.tensor_tensor(eq, iota1[:, 0, 0:NE].unsqueeze(1).unsqueeze(1).to_broadcast([P, TT, TOPK, NE]), bc(idxf[:, :, 0:TOPK], NE), ALU.is_equal))
                d.tensor_reduce(Mt, eq.rearrange("p t k e -> p t e k"), AX.X, ALU.add).then_inc(m_ready, 1)
                ve.wait_ge(rt_exp, 1)
                ch(d.tensor_reduce(sm2[:, :, 0], e4, AX.X, ALU.add))
                ch(d.reciprocal(sm2[:, :, 1], sm2[:, :, 0]))
                ch(d.tensor_tensor(e4, e4, bc(sm2[:, :, 1], TOPK), ALU.mult))
                ch(d.tensor_tensor(eq, eq, bc(e4, NE), ALU.mult))
                d.tensor_reduce(Wt[:, :, 0:NE], eq.rearrange("p t k e -> p t e k"), AX.X, ALU.add).then_inc(wt_ready, 1)
                ve.wait_ge(wt_ready, 1)
                ve.wait_ge(hp_ready, 1)
                d.tensor_tensor(xr, xr, hp[:, 1], ALU.subtract).then_inc(xr_ready, 1)
                ve.wait_ge(rk_ps, 1)
                for t in range(TT):
                    ch(d.scalar_tensor_tensor(rank[:, t, 0:NE], ps[7][:, t * NE:(t + 1) * NE], 1.0, Mt[:, t, :], ALU.add, ALU.mult))
                    for r in range(1, ROUNDS):
                        d.tensor_scalar(rank[:, t, r * NE:(r + 1) * NE], rank[:, t, 0:NE], float(-SLOTS * r), None, ALU.add)
                        d.tensor_copy(Wt[:, t, r * NE:(r + 1) * NE], Wt[:, t, 0:NE])
                ch(d.tensor_reduce(cmax, ps[7][:, 2 * NE:3 * NE], AX.X, ALU.max))
                ch(d.tensor_copy(cmaxi, cmax))
                d.memset(selx, 0.0).then_inc(init0, 1)
                expert_dve(ve, first)

            @block.tensor
            def _(te):
                mm, tr = nc.tensor.matmul, nc.tensor.transpose
                te.wait_ge(ld_const, 16 * 4)

                def tbank(n):
                    if n >= 2:
                        te.wait_ge(t_ev, n - 1)
                    return ps[4 + n % 2]

                def tjob(name):
                    n = TJOBS.index(name)
                    b = tbank(n)
                    t = int(name[-1]) if name[-1].isdigit() else 0
                    kind = name[2:].rstrip("0123456789")
                    if kind == "G":
                        l = tr(b[:, 0:24], grow, ident[0:24, 0:24])
                    elif kind == "X":
                        te.wait_ge(ld_x, 16)
                        for i in range(2):
                            for q in range(TT):
                                l = tr(b[:, i * SEQ + q * P:i * SEQ + (q + 1) * P], x[:, q, (2 * t + i) * P:(2 * t + i + 1) * P], ident)
                    elif kind == "IX":
                        te.wait_ge(ikrep_ready, 1)
                        for i in range(2):
                            tr(b[:, i * P:(i + 1) * P], z[:, t, O_IQ + i * P:O_IQ + (i + 1) * P], ident)
                        l = tr(b[:, 2 * P:3 * P], qn[:, t, 0:P], ident)
                    elif kind in ("DQ", "DK", "NQ"):
                        te.wait_ge(qn_ready, {"DQ": 1, "DK": 2, "NQ": 3}[kind])
                        for j in range(4):
                            l = tr(b[:, j * P:(j + 1) * P], qn[:, t, j * P:(j + 1) * P], ident)
                    elif kind == "K":
                        te.wait_ge(qn_ready, 5)
                        tr(b[:, 0:P], qn[:, t, 0:P], ident)
                        l = tr(b[:, P:2 * P], qn[:, t, P:2 * P], ident)
                    elif kind == "R":
                        te.wait_ge(dup_ready, 1)
                        for i in range(4):
                            l = tr(b[:, i * P:(i + 1) * P], sq[:, t, i * P:(i + 1) * P], ident)
                    elif kind == "PE":
                        te.wait_ge(ld_small, 16 * 8)
                        for i in range(2):
                            l = tr(b[:, i * 16:(i + 1) * 16], pe_in[:, i, :], ident[0:16, 0:16])
                    elif kind == "KC":
                        te.wait_ge(kcn_ready, 1)
                        l = tr(b[:, 0:NCMP], kcs[0:NCMP].rearrange("c g d -> c (g d)"), ident[0:NCMP, 0:NCMP])
                    elif kind == "CS":
                        te.wait_ge(t_ev, TJOBS.index("T:KC") + 1)
                        te.wait_ge(v4_ready, 1)
                        for q in range(TT):
                            for j in range(4):
                                l = mm(b[:, q * P + j * 32:q * P + (j + 1) * 32], qaT[:, j, q * P:(q + 1) * P],
                                       kcZ.rearrange("p g c -> p (g c)"), start=True, stop=True)
                    elif kind == "C":
                        te.wait_ge(c_ready, t + 1)
                        for g in range(2):
                            l = tr(b[:, g * P:(g + 1) * P], P32[:, t, 4 * g:4 * g + 4, :].rearrange("p j c -> p (j c)"), ident)
                    l.then_inc(t_ps, 1)

                for stage in ORDER:
                    if stage.startswith("T:"):
                        tjob(stage)
                    elif stage[0] == "Z":
                        c = int(stage[1:])
                        o, n = CHUNKS[c]
                        te.wait_ge(ld_w[c % 3], 16 * (c // 3 + 1))
                        te.wait_ge(t_ev, 5)
                        if c >= 2:
                            te.wait_ge(z_ev, 2 * (c - 1))
                        wv = wbuf[:, (c % 3) * 4096:(c % 3) * 4096 + KT * n].rearrange("p (k n) -> p k n", k=KT)
                        for t in range(TT):
                            for k in range(KT):
                                l = mm(ps[2 * (c % 2) + t][:, 0:n], hTv[:, k, t * P:(t + 1) * P], wv[:, k, :], start=k == 0, stop=k == KT - 1)
                            l.then_inc(z_ps, 1)
                    elif stage == "ER":
                        te.wait_ge(ld_tab, 48)
                        mm(ps[6][0:16, 0:384], tab, onehot, start=True, stop=True).then_inc(er_ps, 1)
                    elif stage == "I":
                        te.wait_ge(t_ev, TJOBS.index("T:IX1") + 1)
                        for i in range(6):
                            if i == 1:
                                te.wait_ge(er_sb, 1)
                            if i >= 2:
                                te.wait_ge(i_rl, i - 1)
                            if i < 4:
                                lhs, rhs = iqT[:, i // 2, P:2 * P], ikZ[:, 2 * (i % 2):2 * (i % 2) + 2, :]
                            else:
                                lhs, rhs = iqT[:, i - 4, 0:P], ikZ[:, :, 0:P]
                            mm(ps[7 - i % 2][:, :], lhs, rhs, start=True, stop=True).then_inc(i_ps, 1)
                    elif stage == "HID":
                        te.wait_ge(ld_ck, 32)
                        te.wait_ge(zb_ready, 1)
                        te.wait_ge(i_rl, 6)
                        for kv in range(2):
                            for l2 in range(16):
                                l = mm(ps[7][0:DH, kv * 30:(kv + 1) * 30], wck1[:, kv, l2, :], zb[:, kv, l2, :], start=l2 == 0, stop=l2 == 15)
                        l.then_inc(h_ps, 1)
                    elif stage == "CMPKV":
                        te.wait_ge(hid_ready, 1)
                        for g in range(2):
                            mm(ps[6][0:NCMP, g * DH:(g + 1) * DH], hid[:, 0, g * NCMP:(g + 1) * NCMP], ck2w[:, 0, :], start=True, stop=True)
                        for g in range(2):
                            l = mm(ps[6][:, (2 + g) * DH:(3 + g) * DH], hid4[:, g].rearrange("p j c -> p (j c)"), ck2w[:, 1, :], start=True, stop=True)
                        l.then_inc(kc_ps, 1)
                def scores(u):
                    kind, t, j = UNITS[u]
                    n = P * (t + 1)
                    if u == 0:
                        te.wait_ge(z_ev, 2 * NZ)
                    if u >= 4:
                        te.wait_ge(s_log, u - 3)
                    q, k = {"dsa": (qdT, kZd[:, j]), "slc": (qaT, kZs), "win": (qaT, kZw)}[kind]
                    mm(ps[u % 4][:, 0:2 * n], q[:, j, t * P:(t + 1) * P], k[:, :, 0:n], start=True, stop=True).then_inc(s_ps, 1)

                def flip(u):
                    t = UNITS[u][1]
                    b = tbank(TJOBS.index(f"U{u}"))
                    te.wait_ge(s_prob, u + 1)
                    for h in range(2):
                        for s in range(t + 1):
                            l = tr(b[:, (h * (t + 1) + s) * P:(h * (t + 1) + s + 1) * P], L[:, u % 4, h, s * P:(s + 1) * P], ident)
                    l.then_inc(t_ps, 1)

                def values(u):
                    kind, t, j = UNITS[u]
                    i = item_of(u)
                    te.wait_ge(t_ev, TJOBS.index(f"U{u}") + 1)
                    if i >= 2:
                        te.wait_ge(o_ev, i - 1)
                    dst = [ps[6 + i % 2][h * DH:(h + 1) * DH, 0:P] for h in range(2)]
                    if kind == "slc":
                        for h in range(2):
                            mm(dst[h], V4[:, h, j, :], PcT[:, t, h, :], start=True, stop=False)
                    for s_ in range(t + 1):
                        for h in range(2):
                            o = {"dsa": O_DV + (2 * j + h) * DH, "slc": O_KV + 3 * P + h * DH, "win": O_KV + 5 * P + h * DH}[kind]
                            l = mm(dst[h], z[:, s_, o:o + DH], PT[:, u % 2, h * (t + 1) + s_, :], start=kind == "dsa" and s_ == 0,
                                   stop=kind != "slc" and s_ == t)
                    l.then_inc(o_ps, 1)

                for u in range(NU + 3):
                    if u < NU:
                        scores(u)
                    if 2 <= u < NU + 2:
                        flip(u - 2)
                        if u - 2 == C_AFTER:
                            tjob("T:C0")
                            tjob("T:C1")
                    if u >= 3:
                        values(u - 3)
                te.wait_ge(ld_wab, 48)
                te.wait_ge(o_ev, NITEM)
                for i in range(4):
                    t, n = i // 2, (i % 2) * 512
                    if i >= 2:
                        te.wait_ge(pr_used, i - 1)
                    for m_ in range(2):
                        for j in range(4):
                            l = mm(ps[2 * (i % 2) + m_][:, :], oTv[:, m_, j, t * P:(t + 1) * P], (wa, wb)[m_][:, j, n:n + 512], start=j == 0, stop=j == 3)
                    l.then_inc(pr_ps, 1)
                te.wait_ge(pr_used, 4)
                for n in range(4):
                    b = tbank(NT + n)
                    for i in range(2):
                        for t in range(TT):
                            l = tr(b[:, i * SEQ + t * P:i * SEQ + (t + 1) * P], merged[:, t, (2 * n + i) * P:(2 * n + i + 1) * P], ident)
                    l.then_inc(t_ps, 1)
                te.wait_ge(ld_wo, 16)
                te.wait_ge(t_ev, NT + 4)
                for i in range(4):
                    t, n = i // 2, (i % 2) * 512
                    for k in range(KT):
                        l = mm(ps[i][:, :], hTv[:, k, t * P:(t + 1) * P], wo[:, k, n:n + 512], start=k == 0, stop=k == KT - 1)
                    l.then_inc(wo_ps, 1)
                te.wait_ge(x2_ready, 4)
                for n in range(4):
                    b = tbank(NT + 4 + n)
                    for i in range(2):
                        for t in range(TT):
                            l = tr(b[:, i * SEQ + t * P:i * SEQ + (t + 1) * P], x[:, t, (2 * n + i) * P:(2 * n + i + 1) * P], ident)
                    l.then_inc(t_ps, 1)
                te.wait_ge(t_ev, NT + 8)
                te.wait_ge(ld_route, 32)
                for t in range(TT):
                    for k in range(KT):
                        l = mm(ps[6][:, t * NE:(t + 1) * NE], hTv[:, k, t * P:(t + 1) * P], wr[:, k, :], start=k == 0, stop=k == KT - 1)
                l.then_inc(rt_ps, 1)
                te.wait_ge(m_ready, 1)
                mm(ps[7][:, 0:NE], tri, Mt[:, 0, :], start=True, stop=True)
                mm(ps[7][:, NE:2 * NE], ones, Mt[:, 0, :], start=True, stop=False)
                mm(ps[7][:, NE:2 * NE], tri, Mt[:, 1, :], start=False, stop=True)
                mm(ps[7][:, 2 * NE:3 * NE], ones, Mt[:, 0, :], start=True, stop=False)
                mm(ps[7][:, 2 * NE:3 * NE], ones, Mt[:, 1, :], start=False, stop=True).then_inc(rk_ps, 1)
                b = tbank(NT + 8)
                te.wait_ge(wt_ready, 1)
                for t in range(TT):
                    l = tr(b[0:NE, t * P:(t + 1) * P], Wt[:, t, 0:NE], ident)
                l.then_inc(t_ps, 1)
                te.wait_ge(t_ev, NT + 9)
                te.wait_ge(ld_be2, 16)
                te.wait_ge(init0, 1)
                te.wait_ge(hp_ready, 2)
                for t in range(TT):
                    for n in range(2):
                        mm(ps[4 + 2 * t + n][:, :], WT[:, t * P:(t + 1) * P], be2[:, n * 512:(n + 1) * 512], start=True, stop=False, skip_group_check=True)
                expert_pe(te, first)

        with nc.Block() as block:
            def some(eng):
                return eng.If(eng.value_load(cmaxi[0:1, 0:1], min_val=0, max_val=SEQ) > SLOTS)

            @block.sync
            def _(sp):
                with some(sp):
                    for i in range(PIECES):
                        load(sp, 0, i, rest["piece"])
                    with sp.Fori(1, rest["visits"]) as it:
                        for i in range(PIECES):
                            sp.wait_ge(rest["s"]["pieces_used"], it * PIECES - PIECES + (i + 1))
                            load(sp, it % NE, i, rest["piece"])

            @block.scalar
            def _(sc):
                with some(sc):
                    expert_act(sc, rest)

            @block.vector
            def _(ve):
                with some(ve):
                    expert_dve(ve, rest)

            @block.tensor
            def _(te):
                with some(te):
                    expert_pe(te, rest)

        x3_ready, p_sq, p_rs, p_ps, p_ev, g_ps, g_sig, g_used, pl_ps, o_ready, st_out = (
            sem(n) for n in ("x3_ready", "p_sq", "p_rs", "p_ps", "p_ev", "g_ps", "g_sig", "g_used", "pl_ps", "o_ready", "st_out"))
        with nc.Block() as block:
            @block.gpsimd
            def _(pool):
                g = nc.gpsimd
                pool.wait_ge(p_sq, 1)
                g.tensor_scalar(rs, ssx, 1.0 / DM, EPS, ALU.mult, ALU.add).then_inc(p_rs, 1)
                pool.wait_ge(p_rs, 1)
                g.tensor_tensor(rs, rs, half[:, 0:2], ALU.pow).then_inc(p_rs, 1)

            @block.scalar
            def _(sc):
                a = nc.scalar
                sc.wait_ge(p_ps, 1)
                a.copy(pT, ps[0][:, :].rearrange("p (k t) -> p k t", k=2)).then_inc(p_ev, 1)
                for n in range(4):
                    sc.wait_ge(p_ps, n + 2)
                    for i in range(2):
                        kk = 2 * n + i
                        l = a.activation(hTv[:, kk, :], ps[n % 2][:, i * SEQ:(i + 1) * SEQ], ACT.Copy, scale=gT[:, 16 + kk:17 + kk])
                    l.then_inc(p_ev, 1)
                sc.wait_ge(p_rs, 2)
                for i in range(4):
                    sc.wait_ge(g_ps, i + 1)
                    if i >= 2:
                        sc.wait_ge(o_ready, i - 1)
                    a.activation(sgate[:, i % 2, :], ps[i][:, :], ACT.Sigmoid, scale=rs[:, i // 2:i // 2 + 1]).then_inc(g_sig, 1)

            @block.vector
            def _(ve):
                d = nc.vector
                for i in range(4):
                    t, n = i // 2, (i % 2) * 512
                    d.tensor_tensor(x[:, t, n:n + 512], x[:, t, n:n + 512], ps[4 + i][:, :], ALU.add).then_inc(x3_ready, 1)
                ve.wait_ge(x3_ready, 4)
                for t in range(TT):
                    l = d.tensor_tensor_reduce(out=xn3[:, t, :], in0=x[:, t, :], in1=x[:, t, :], scale=1.0, scalar=0.0,
                                               op0=ALU.mult, op1=ALU.add, accum_out=ssx[:, t:t + 1])
                l.then_inc(p_sq, 1)
                for i in range(4):
                    t, n = i // 2, (i % 2) * 512
                    ve.wait_ge(g_sig, i + 1)
                    ve.wait_ge(pl_ps, i + 1)
                    d.tensor_tensor(sgate[:, i % 2, :], sgate[:, i % 2, :], ps[4 + i][:, :], ALU.mult).then_inc(g_used, 1)
                    ve.wait_ge(g_used, i + 1)
                    d.tensor_tensor(x[:, t, n:n + 512], x[:, t, n:n + 512], sgate[:, i % 2, :], ALU.add).then_inc(o_ready, 1)

            @block.tensor
            def _(te):
                mm, tr = nc.tensor.matmul, nc.tensor.transpose
                te.wait_ge(ld_p, 16)
                for k in range(2):
                    for t in range(TT):
                        l = tr(ps[0][:, k * SEQ + t * P:k * SEQ + (t + 1) * P], pin[:, t, k * P:(k + 1) * P], ident)
                l.then_inc(p_ps, 1)
                te.wait_ge(p_ev, 1)
                te.wait_ge(x3_ready, 4)
                for n in range(4):
                    if n >= 2:
                        te.wait_ge(p_ev, n)
                    for i in range(2):
                        for t in range(TT):
                            l = tr(ps[n % 2][:, i * SEQ + t * P:i * SEQ + (t + 1) * P], x[:, t, (2 * n + i) * P:(2 * n + i + 1) * P], ident)
                    l.then_inc(p_ps, 1)
                te.wait_ge(ld_ple, 32)
                for i in range(4):
                    t, n = i // 2, (i % 2) * 512
                    te.wait_ge(x3_ready, i + 1)
                    for k in range(2):
                        l = mm(ps[4 + i][:, :], pT[:, k, t * P:(t + 1) * P], wple[:, k, n:n + 512], start=k == 0, stop=k == 1)
                    l.then_inc(pl_ps, 1)
                te.wait_ge(p_ev, 5)
                for i in range(4):
                    t, n = i // 2, (i % 2) * 512
                    for k in range(KT):
                        l = mm(ps[i][:, :], hTv[:, k, t * P:(t + 1) * P], wple_g[:, k, n:n + 512], start=k == 0, stop=k == KT - 1)
                    l.then_inc(g_ps, 1)

            @block.sync
            def _(sp):
                for i in range(4):
                    t, n = i // 2, (i % 2) * 512
                    sp.wait_ge(o_ready, i + 1)
                    sp.dma_start(out[0, t * P:(t + 1) * P, n:n + 512], x[:, t, n:n + 512]).then_inc(st_out, 16)
                sp.wait_ge(st_out, 64)


def constants():
    c = np.zeros((P, 544), np.float32)
    c[:, 0:P] = np.eye(P)
    c[:, P:2 * P] = np.triu(np.ones((P, P)), 1)
    c[:, 2 * P:3 * P] = 1.0
    c[:, 3 * P:4 * P] = np.arange(P) % SLOTS + 1
    c[:, 4 * P:4 * P + NE] = (np.arange(P)[:, None] % NE) == np.arange(NE)[None, :]
    onehot = np.zeros((BUCKETS + 1, 384), np.float32)
    for j in range(384):
        n = 255 - j
        if n < 0:
            b = BUCKETS
        elif n < MAX_EXACT:
            b = n
        else:
            big = np.log(np.float32(n) / np.float32(MAX_EXACT)) / np.float32(math.log(MAX_DIST / MAX_EXACT))
            b = min(MAX_EXACT + int(big * np.float32(BUCKETS - MAX_EXACT)), BUCKETS - 1)
        onehot[b, j] = 1.0
    return {"consts": c, "onehot": onehot, "negrow": np.full((1, 16), NEG, np.float32)}


INS = ["x", "p", "w_in", "g_mix", "g_q_nsa", "g_k_nsa", "g_q_dsa", "g_k_dsa", "pe_ck", "w_ck1", "w_ck2", "pe_cv", "w_cv1", "w_cv2",
       "w_branch_a", "w_branch_b", "w_out", "rel_bias", "g_ffn", "w_router", "b_router", "w_e1", "b_e1", "w_e2", "b_e2", "g_ple",
       "w_ple", "w_ple_gate"]


def kernel(**inputs):
    import concourse.bacc as bacc
    from concourse.bass_utils import run_bass_kernel_spmd

    nc = bacc.Bacc("TRN2", target_bir_lowering=False, num_devices=1)
    arrays = {n: np.ascontiguousarray(inputs[n]) for n in INS}
    arrays.update(constants())
    io = {n: nc.dram_tensor(f"in_{n}", a.shape, mybir.dt.from_np(a.dtype), kind="ExternalInput").ap() for n, a in arrays.items()}
    out = nc.dram_tensor("out_0", (1, SEQ, DM), F32, kind="ExternalOutput").ap()
    block_kernel(nc, io, out)
    r = run_bass_kernel_spmd(nc, [{f"in_{n}": a for n, a in arrays.items()}], core_ids=[0])
    return r.results[0]["out_0"]
```

```python
import math
from contextlib import ExitStack

import numpy as np
import concourse.bass as bass
from concourse import mybir

F32 = mybir.dt.float32
BF16 = mybir.dt.bfloat16
I32 = mybir.dt.int32
ALU = mybir.AluOpType
ACT = mybir.ActivationFunctionType
AX = mybir.AxisListType

P = 128
SEQ, DM = 256, 1024
TT = SEQ // P
KT = DM // P
DH, HEADS, GROUPS, HPG = 64, 8, 2, 4
CMP_LEN, CMP_STRIDE = 32, 16
NCMP = (SEQ - CMP_LEN) // CMP_STRIDE + 1
CMP_SEEN = [(P * (t + 1) - CMP_LEN) // CMP_STRIDE + 1 for t in range(TT)]
IH, ID = 8, 32
KEEP = 64
BUCKETS, MAX_EXACT, MAX_DIST = 32, 16, 128
NE, TOPK, DFF = 32, 4, 1024
LIMIT, ALPHA = 7.0, 1.702
EPS = 1e-6
NEG = -1e30
BLOCKED, TAKEN = -3e38, -3.4e38
PLE = 256
SLOTS = 64
ROUNDS = SEQ // SLOTS
PIECES = 12
UP = 8

O_NQ, O_KV, O_NG, O_DQ, O_DK, O_DV, O_IQ, O_IK, O_IW, O_GA = 0, 512, 1280, 1304, 1816, 2328, 2840, 3096, 3128, 3136
ZW = O_GA
CHUNKS = [(O_IQ, O_GA - O_IQ), (O_DQ, 512), (O_DK, 512), (O_NQ, 512), (O_KV, 512), (O_KV + 512, O_DQ - O_KV - 512),
          (O_DV, 512), (O_GA, 512), (O_GA + 512, 512), (O_GA + 1024, 512), (O_GA + 1536, 512)]
NZ = len(CHUNKS)
C_IX, C_DQ, C_DK, C_NQ, C_N1, C_N2, C_DV, C_G = range(8)

ORDER = ["T:G", "T:X0", "T:X1", "T:X2", "T:X3", "Z0", "ER", "Z1", "T:IX0", "T:IX1", "Z2", "I", "T:DQ0", "T:DQ1", "Z3",
         "T:DK0", "T:DK1", "Z4", "T:NQ0", "T:NQ1", "Z5", "Z6", "T:K0", "T:K1", "T:R0", "T:R1", "T:PE"]
UNITS = [("dsa", t, j) for t in (0, 1) for j in range(4)] + [(b, t, j) for t in (0, 1) for j in range(4) for b in ("slc", "win")]
NU = len(UNITS)
STEPS = NU + 4
STAGE_AT = {1: "HID", 5: "CMPKV", 7: "T:KC", 8: "T:CS"}
HIDDEN_AT, KEYS_AT, NORMED_AT, C_SOFT = 3, 5, 6, 9
C_AFTER = 8
TJOBS = [x for x in ORDER if x.startswith("T:")]
for _u in range(STEPS):
    if STAGE_AT.get(_u, "").startswith("T:"):
        TJOBS.append(STAGE_AT[_u])
    if 3 <= _u < NU + 3:
        TJOBS += [f"U{_u - 3}"] + (["T:C0", "T:C1"] if _u - 3 == C_AFTER else [])
NT = len(TJOBS)
LATE = [(c, t, k) for c in range(C_G, NZ) for t in range(TT) for k in range(KT)]
LATE_OF = []
for _u in range(STEPS):
    _n = 3 if _u < 16 else 1 if _u < NU else 2
    LATE_OF.append(LATE[:_n])
    LATE = LATE[_n:]
assert not LATE
WBUF = [0, 1, 2, 0, 1, 2, 0, 1, 0, 2, 3]
NITEM = 16


def item_of(u):
    return u if u < 8 else 8 + (u - 8) // 2


def block_kernel(nc, io, out):
    ctx = ExitStack()
    with ctx:
        def sb(name, words):
            return ctx.enter_context(nc.sbuf_tensor(name, [P, words], F32))

        def sem(name):
            return ctx.enter_context(nc.semaphore(name))

        ring = sb("ring", PIECES * 2048)
        wbuf = sb("wbuf", 4 * 4096)
        xres = sb("xres", TT * DM)
        hT = sb("hT", KT * SEQ)
        gat = sb("gat", TT * 2 * DM)
        oT = sb("oT", 2 * 4 * SEQ)
        misc = sb("misc", 2000)
        ps = [ctx.enter_context(nc.psum_tensor(f"ps{b}", [P, 512], F32)) for b in range(8)]

        class Take:
            def __init__(self, t, at=0):
                self.t, self.at = t, at

            def __call__(self, *shape, parts=P, dt=F32):
                n = int(np.prod(shape))
                words = n if dt != BF16 else (n + 1) // 2
                ap = self.t[0:parts, self.at:self.at + words]
                self.at += words
                if dt != F32:
                    ap = ap.bitcast(dt)
                if len(shape) == 2:
                    ap = ap.rearrange("p (a b) -> p a b", a=shape[0])
                if len(shape) == 3:
                    ap = ap.rearrange("p (a b c) -> p a b c", a=shape[0], b=shape[1])
                assert self.at <= self.t.shape[1], (self.at, self.t.shape)
                return ap

        def bc(ap, n):
            return ap.unsqueeze(len(ap.shape)).to_broadcast(list(ap.shape) + [n])

        def bm(ap, n):
            s = list(ap.shape)
            return ap.unsqueeze(1).to_broadcast([s[0], n] + s[1:])

        m = Take(misc)
        const_all = misc[:, 0:544]
        ident, tri, ones, iota1 = m(128), m(128), m(128), m(2, 64)
        idmod = m(NE)
        gT = m(24)
        gqk = m(4, DH)
        wr, br = m(KT, NE), m(NE)
        rs, ssx = m(2), m(2)
        half = m(64)
        Mt = m(TT, NE)
        top8, e4, lg, eq = m(TT, 8), m(TT, TOPK), m(TT, NE), m(TT, TOPK, NE)
        idx8 = m(TT, 8, dt=mybir.dt.uint32)
        idxf = m(TT, 8)
        sm2, cnt, cmax = m(TT, 2), m(NE), m(1)
        cmaxi = m(1, dt=I32)
        sel = m(SLOTS, parts=96, dt=BF16)
        S = m(TT, SLOTS, dt=BF16)

        w = Take(ring)
        z = w(TT, ZW)
        bias = w(16, SEQ)
        xn = ring[:, 22528:24576].rearrange("p (t d) -> p t d", t=TT)
        sq = ring[:, 21504:22528].rearrange("p (t d) -> p t d", t=TT)
        ikZ, rl = xn[:, 0, :].rearrange("p (a b) -> p a b", a=4), xn[:, 1, :].rearrange("p (a b) -> p a b", a=2)
        qaT, qdT = w(4, SEQ), w(4, SEQ)
        kZs, kZw = w(2, SEQ), w(2, SEQ)
        kZd = w(4, 2, SEQ)
        iqT = w(2, SEQ)
        zb = xn[:, 1, 0:2 * 16 * 30].rearrange("p (a l n) -> p a l n", a=2, l=16)
        score, selm = w(TT, SEQ), w(TT, SEQ)
        qn = w(TT, 512)
        PT = w(2, 4, P)
        rawT = PT.rearrange("p b a t -> p (b a t)").rearrange("p (a g t) -> p a g t", a=2, g=2)
        Bd = [w(2, SEQ), sq[:, :, SEQ:2 * SEQ]]
        work_small = Take(ring[:, 0:21504], w.at)
        V4 = work_small(2, 4, DH)
        kcZ = work_small(2, 16)
        kcs = work_small(2, DH, parts=16)
        kcq = work_small(2, DH, parts=16)
        hid, hsg = work_small(2, 30, parts=DH), work_small(2, 30, parts=DH)
        hid4 = work_small(2, 4, 32, parts=DH)
        peT = work_small(2, 16)
        m8 = work_small(8)
        iwS = work_small(TT, IH)
        gsig = work_small(TT, 24)
        v16 = work_small(TT, 8)
        r16 = work_small(TT, 8)
        mx, nmx, ssum, rcp = (work_small(4, 2) for _ in range(4))
        ckr = work_small(4)
        ck2w = work_small(2, DH, parts=DH)
        g0 = Take(gat)
        pe_in = g0(2, P, parts=16)
        grow = g0(P, parts=24)
        tab, onehot, erow = g0(16, parts=BUCKETS + 1), g0(384, parts=BUCKETS + 1), g0(384, parts=16)
        ot0 = Take(oT)
        P32 = ot0(TT, 8, 32)
        PcT = sq.rearrange("p t (g c) -> p t g c", g=4)[:, :, 0:2, :]
        cL, cst = ot0(TT, 8, 16), ot0(TT, 4, 8)
        csb = score[:, :, 0:P]
        wck1 = wbuf[:, 3 * 4096:3 * 4096 + 2048].rearrange("p (a l e) -> p a l e", a=2, l=16)
        L = ring[:, 22528:24576].rearrange("p (b h s) -> p b h s", b=4, h=2)
        hTv = hT[:, :].rearrange("p (k t) -> p k t", k=KT)
        x = xres[:, :].rearrange("p (t d) -> p t d", t=TT)
        gates = gat[:, :].rearrange("p (t n) -> p t n", t=TT)
        oTv = oT[:, :].rearrange("p (m j t) -> p m j t", m=2, j=4)
        wa = wbuf[:, 0:4096].rearrange("p (j n) -> p j n", j=4)
        wb = wbuf[:, 4096:8192].rearrange("p (j n) -> p j n", j=4)
        wo = wbuf[:, 8192:16384].rearrange("p (k n) -> p k n", k=KT)
        merged, mtmp = xn, sq
        wple_g = wbuf[:, 0:8192].rearrange("p (k n) -> p k n", k=KT)
        wple = wbuf[:, 8192:10240].rearrange("p (k n) -> p k n", k=2)
        v = Take(wbuf, 10240)
        xeT = v(KT, SLOTS)
        gc, sg, lin, act, actT, oe = v(512), v(512), v(512), v(512), v(4, P), v(512)
        wS, wST = v(TT, P), v(TT * P)
        rank = v(TT, ROUNDS * NE + 1)
        Wt = v(TT, ROUNDS * NE)
        be2, WT = oT[0:NE, 1024:2048], v(SEQ, parts=NE)
        hp = gat[:, 0:3072].bitcast(BF16).rearrange("p (q t d) -> p q t d", q=3, t=TT)
        b1p = gat[0:96, 3072:4096].bitcast(BF16)
        b1f = oT[0:96, :]
        xh = [wbuf[:, 0:DM], wbuf[:, 11264:12288]]
        xr = [wbuf[:, DM:2 * DM], wbuf[:, 13312:14336]]
        pin, pT = oT[:, 0:512].rearrange("p (t d) -> p t d", t=TT), oT[:, 512:1024].rearrange("p (k t) -> p k t", k=2)
        pl = hT[:, :].rearrange("p (t d) -> p t d", t=TT)
        x3T = ring[:, 0:KT * SEQ].rearrange("p (k t) -> p k t", k=KT)
        xn3, sgate = xn, sq
        ring3 = ring[:, :].rearrange("p (i n) -> p i n", i=PIECES)

        ERW = 384
        er_dram = nc.dram_tensor("rel_rows", [16, ERW], F32).ap()
        er_rep = nc.dram_tensor("rel_rows_repeated", [16, P, ERW], F32).ap()

        ld_const, ld_x, ld_small, ld_tab, ld_ck = sem("ld_const"), sem("ld_x"), sem("ld_small"), sem("ld_tab"), sem("ld_ck")
        ld_w = [sem(f"ld_w{i}") for i in range(4)]
        ld_wab, ld_wo, ld_bias, st_er, st_rep, ld_route, ld_b1, ld_be2, ld_p, ld_ple, ld_ple_gate = (
            sem(n) for n in ("ld_wab", "ld_wo", "ld_bias", "st_er", "st_rep", "ld_route", "ld_b1", "ld_be2", "ld_p", "ld_ple", "ld_ple_gate"))
        piece = [sem(f"piece{i}") for i in range(PIECES)]
        gates_ready, zeroed, x_sq, x_rs, t_ps, t_ev, z_ps, z_ev = (
            sem(n) for n in ("gates_ready", "zeroed", "x_sq", "x_rs", "t_ps", "t_ev", "z_ps", "z_ev"))
        ikrep_ready, i_ps, i_rl, i_used, score_cut, selm_ready = (
            sem(n) for n in ("ikrep_ready", "i_ps", "i_rl", "i_used", "score_cut", "selm_ready"))
        n_var, n_rs, qn_ready = sem("n_var"), sem("n_rs"), sem("qn_ready")
        er_ps, er_sb = sem("er_ps"), sem("er_sb")
        zb_ready, h_ps, h_exp, hid_ready, kc_ps, kc_copied, v4_ready, kcn_ready = (
            sem(n) for n in ("zb_ready", "h_ps", "h_exp", "hid_ready", "kc_ps", "kc_copied", "v4_ready", "kcn_ready"))
        c_log, c_exp, c_ready = sem("c_log"), sem("c_exp"), sem("c_ready")
        s_ps, s_log, s_exp, s_prob, bd_ready, o_ps, o_ev = (
            sem(n) for n in ("s_ps", "s_log", "s_exp", "s_prob", "bd_ready", "o_ps", "o_ev"))
        pr_ps, pr_used, mg_ready, wo_ps, x2_ready, f_sq, f_rs = (
            sem(n) for n in ("pr_ps", "pr_used", "mg_ready", "wo_ps", "x2_ready", "f_sq", "f_rs"))
        rt_ps, lg_ready, rt_exp, m_ready, rk_ps, rank_ready, wt_ready, y_init, hp_ready, b1_ready, ranks_taken, xr_ready, dup_ready = (
            sem(n) for n in ("rt_ps", "lg_ready", "rt_exp", "m_ready", "rk_ps", "rank_ready", "wt_ready", "y_init",
                             "hp_ready", "b1_ready", "ranks_taken", "xr_ready", "dup_ready"))
        dve_ch, pool_ch, act_ch = sem("dve_chain"), sem("pool_chain"), sem("act_chain")

        class Chain:
            def __init__(self, eng, s):
                self.eng, self.s, self.n = eng, s, 0

            def __call__(self, ins):
                self.n += 1
                ins.then_inc(self.s, 1)
                self.eng.wait_ge(self.s, self.n)

        NORMS = [("dq", O_DQ, 8, 2, DH ** -0.5), ("dk", O_DK, 8, 3, 1.0), ("nq", O_NQ, 8, 0, DH ** -0.5),
                 ("ks", O_KV + 256, 2, 1, 1.0), ("kw", O_KV + 512, 2, 1, 1.0)]
        NORM_CHUNK = [C_DQ, C_DK, C_NQ, C_N1, C_N2]

        def expert_sems(tag):
            names = ("pieces_used", "s_ready", "sel_ready", "xe_ps", "xe_ready", "gc_ready", "lin_ready", "glu_ready", "sig_ready",
                     "act_ready", "at_ps", "at_ready", "wst_ps", "ws_ready", "wst_ready", "out_ready")
            return {n: sem(f"{n}_{tag}") for n in names}

        y_done, pl_ps, pl_ev = sem("y_done"), sem("pl_ps"), sem("pl_ev")
        w1 = io["w_e1"][0].rearrange("e (k p) n -> e k p n", p=P)
        w2 = io["w_e2"][0].rearrange("e (q r p) n -> e q p r n", r=2, p=P)
        first = dict(s=expert_sems("a"), piece=piece, col=0, visits=NE)
        rest = dict(s=expert_sems("b"), piece=[sem(f"piece_b{i}") for i in range(PIECES)], col=NE, visits=(ROUNDS - 1) * NE)

        def load(eng, e, i, signal):
            if i < UP:
                eng.dma_start(ring3[:, i, :], w1[e, i]).then_inc(signal[i], 16)
            else:
                eng.dma_start(ring3[:, i, :].rearrange("p (r n) -> p r n", r=2), w2[e, i - UP]).then_inc(signal[i], 16)

        def expert_pe(te, a):
            s, col = a["s"], a["col"]
            mm, tr = nc.tensor.matmul, nc.tensor.transpose
            G, Lb, O, T = ps[0], ps[1], ps[2], ps[3]

            def gather():
                for k in range(KT):
                    for t in range(TT):
                        for q in range(3):
                            l = mm(O[:, k * SLOTS:(k + 1) * SLOTS], hp[:, q, t, k * P:(k + 1) * P], S[:, t, :],
                                   start=t == 0 and q == 0, stop=t == TT - 1 and q == 2)
                l.then_inc(s["xe_ps"], 1)

            def scatter():
                for t in range(TT):
                    for n in range(2):
                        h = slice(n * SLOTS, (n + 1) * SLOTS)
                        l = mm(ps[4 + 2 * t + n][:, :], wST[h, t * P:(t + 1) * P], oe[h, :], start=False, stop=False, skip_group_check=True)
                return l

            te.wait_ge(s["s_ready"], 1)
            gather()
            with te.Fori(0, a["visits"]) as it:
                te.wait_ge(s["sel_ready"], it + 1)
                te.wait_ge(s["xe_ready"], it + 1)
                for n in range(4):
                    mm((G, Lb)[n // 2][(n % 2) * SLOTS:(n % 2 + 1) * SLOTS, :], sel, b1p[:, n * 512:(n + 1) * 512], start=True, stop=False)
                for k in range(UP):
                    te.wait_ge(a["piece"][k], it * 16 + 16)
                    for n in range(4):
                        l = mm((G, Lb)[n // 2][(n % 2) * SLOTS:(n % 2 + 1) * SLOTS, :], xeT[:, k, :], ring3[:, k, n * 512:(n + 1) * 512],
                               start=False, stop=k == UP - 1)
                    l.then_inc(s["pieces_used"], 1)
                te.wait_ge(s["out_ready"], it + 1)
                te.wait_ge(s["wst_ready"], it + 1)
                scatter()
                te.wait_ge(s["ws_ready"], it + 1)
                for t in range(TT):
                    l = tr(T[:, t * P:(t + 1) * P], wS[:, t, :], ident)
                l.then_inc(s["wst_ps"], 1)
                te.wait_ge(s["s_ready"], it + 2)
                gather()
                te.wait_ge(s["wst_ready"], it + 2)
                te.wait_ge(s["act_ready"], it + 1)
                for j in range(4):
                    l = tr(T[:, j * P:(j + 1) * P], act[:, j * P:(j + 1) * P], ident)
                l.then_inc(s["at_ps"], 1)
                te.wait_ge(s["at_ready"], it + 1)
                te.wait_ge(s["xe_ready"], it + 2)
                for i in range(UP, PIECES):
                    te.wait_ge(a["piece"][i], it * 16 + 16)
                    for r in range(2):
                        kt = 2 * (i - UP) + r
                        for n in range(2):
                            l = mm(O[n * SLOTS:(n + 1) * SLOTS, :], actT[:, kt % 4, (kt // 4) * SLOTS:(kt // 4 + 1) * SLOTS],
                                   ring3[:, i, r * DM + n * 512:r * DM + (n + 1) * 512], start=kt == 0, stop=kt == 7)
                    l.then_inc(s["pieces_used"], 1)
            te.wait_ge(s["out_ready"], a["visits"] + 1)
            te.wait_ge(s["wst_ready"], a["visits"] + 1)
            scatter().then_inc(y_done, 1)

        def expert_act(sc, a):
            s = a["s"]
            with sc.Fori(0, a["visits"]) as it:
                sc.wait_ge(s["gc_ready"], it + 1)
                nc.scalar.activation(sg, gc, ACT.Sigmoid, scale=ALPHA).then_inc(s["sig_ready"], 1)
                sc.wait_ge(s["wst_ps"], it + 1)
                nc.scalar.copy(wST, ps[3][:, 0:TT * P]).then_inc(s["wst_ready"], 1)
                sc.wait_ge(s["at_ps"], it + 1)
                nc.scalar.copy(actT.rearrange("p j t -> p (j t)"), ps[3][:, :]).then_inc(s["at_ready"], 1)
                sc.wait_ge(s["pieces_used"], it * PIECES + PIECES)
                nc.scalar.copy(oe, ps[2][:, :]).then_inc(s["out_ready"], 1)

        def expert_dve(ve, a):
            s, col, d = a["s"], a["col"], nc.vector
            i1 = iota1[:, 0, :]

            def one_hot(c):
                for t in range(TT):
                    l = d.tensor_scalar(S[:, t, :], i1, rank[:, t, c], None, ALU.is_equal)
                l.then_inc(s["s_ready"], 1)

            def take_rows():
                d.tensor_tensor(xeT, ps[2][:, :].rearrange("p (k c) -> p k c", k=KT), bc(gT[:, 8:16], SLOTS), ALU.mult).then_inc(s["xe_ready"], 1)

            ve.wait_ge(hp_ready, 4)
            d.memset(oe, 0.0).then_inc(s["out_ready"], 1)
            d.memset(wST, 0.0).then_inc(s["wst_ready"], 1)
            one_hot(slice(col, col + 1))
            ve.wait_ge(s["xe_ps"], 1)
            take_rows()
            with ve.Fori(0, a["visits"]) as it:
                if a is first:
                    e = bass.ds(it, 1)
                else:
                    e = bass.ds(it % NE, 1)
                d.tensor_copy(sel, idmod[0:96, e].to_broadcast([96, SLOTS])).then_inc(s["sel_ready"], 1)
                one_hot(bass.ds(it + (col + 1), 1))
                for t in range(TT):
                    l = d.tensor_scalar(wS[:, t, :], iota1.rearrange("p a b -> p (a b)"), rank[:, t, bass.ds(it + col, 1)],
                                        Wt[:, t, bass.ds(it + col, 1)], ALU.is_equal, ALU.mult)
                l.then_inc(s["ws_ready"], 1)
                ve.wait_ge(s["pieces_used"], it * PIECES + UP)
                d.tensor_scalar(gc, ps[0][:, :], LIMIT, None, ALU.min).then_inc(s["gc_ready"], 1)
                d.tensor_scalar(lin, ps[1][:, :], LIMIT, -LIMIT, ALU.min, ALU.max).then_inc(s["lin_ready"], 1)
                ve.wait_ge(s["gc_ready"], it + 1)
                ve.wait_ge(s["lin_ready"], it + 1)
                d.scalar_tensor_tensor(lin, lin, 1.0, gc, ALU.add, ALU.mult).then_inc(s["glu_ready"], 1)
                ve.wait_ge(s["glu_ready"], it + 1)
                ve.wait_ge(s["sig_ready"], it + 1)
                d.tensor_tensor(act, lin, sg, ALU.mult).then_inc(s["act_ready"], 1)
                ve.wait_ge(s["xe_ps"], it + 2)
                take_rows()

        with nc.Block() as block:
            @block.sync
            def _(sp):
                sp.dma_start(x[:, :, :], io["x"][0].rearrange("(t p) d -> p t d", p=P)).then_inc(ld_x, 16)
                w_in = io["w_in"][0].rearrange("(k p) n -> p k n", p=P)
                for c, (o, n) in enumerate(CHUNKS):
                    if c == 1:
                        sp.wait_ge(ld_x, 16)
                    before = [b for b in range(c) if WBUF[b] == WBUF[c]]
                    if before:
                        sp.wait_ge(z_ps, 2 * (before[-1] + 1))
                    if WBUF[c] == 3:
                        sp.wait_ge(h_ps, 1)
                    dst = wbuf[:, WBUF[c] * 4096:WBUF[c] * 4096 + KT * n].rearrange("p (k n) -> p k n", k=KT)
                    sp.dma_start(dst, w_in[:, :, o:o + n]).then_inc(ld_w[WBUF[c]], 16)
                    if c == 1:
                        sp.dma_start(tab[0:BUCKETS, :], io["rel_bias"]).then_inc(ld_tab, 16)
                        sp.dma_start(tab[BUCKETS:BUCKETS + 1, :], io["negrow"]).then_inc(ld_tab, 16)
                        sp.dma_start(onehot, io["onehot"]).then_inc(ld_tab, 16)
                        for i, n in enumerate(("g_q_nsa", "g_k_nsa", "g_q_dsa", "g_k_dsa")):
                            sp.dma_start(gqk[:, i, :], io[n].to_broadcast([P, DH])).then_inc(ld_small, 16)
                        for i, n in enumerate(("pe_ck", "pe_cv")):
                            sp.dma_start(pe_in[:, i, :], io[n][0].rearrange("(l q) d -> l (q d)", q=2)).then_inc(ld_small, 16)
                        for i, n in enumerate(("w_ck2", "w_cv2")):
                            sp.dma_start(ck2w[:, i, :], io[n][0]).then_inc(ld_small, 16)
                        sp.dma_start(wr, io["w_router"][0].rearrange("(k p) n -> p k n", p=P)).then_inc(ld_route, 16)
                        sp.dma_start(br, io["b_router"].to_broadcast([P, NE])).then_inc(ld_route, 16)
                    if c == 2:
                        for a, name in enumerate(("w_ck1", "w_cv1")):
                            sp.dma_start(wck1[:, a], io[name][0].rearrange("(l q) d e -> (q d) l e", q=2)).then_inc(ld_ck, 16)
                sp.wait_ge(z_ps, 2 * (NZ - 2))
                for g in range(2):
                    sp.dma_start(wa[g * DH:(g + 1) * DH], io["w_branch_a"][0].rearrange("(g j d) n -> g d j n", g=2, j=4)[g]).then_inc(ld_wab, 16)
                sp.dma_start(wb[:, :, :], io["w_branch_b"][0].rearrange("(j p) n -> p j n", p=P)).then_inc(ld_wab, 16)
                sp.wait_ge(z_ps, 2 * NZ)
                sp.dma_start(wo[:, :, :], io["w_out"][0].rearrange("(k p) n -> p k n", p=P)).then_inc(ld_wo, 16)
                sp.wait_ge(o_ev, NITEM)
                for i in range(8):
                    load(sp, 0, i, piece)
                sp.wait_ge(pr_used, 4)
                for q in range(3):
                    sp.dma_start(b1f[q * NE:(q + 1) * NE, :], io["b_e1"][0]).then_inc(ld_b1, 16)
                load(sp, 0, 8, piece)
                load(sp, 0, 9, piece)
                w_gate = io["w_ple_gate"][0].rearrange("(k p) n -> p k n", p=P)
                sp.dma_start(wple_g[:, 2:KT], w_gate[:, 2:KT]).then_inc(ld_ple_gate, 16)
                sp.wait_ge(t_ev, NT + 4)
                for i in range(10, PIECES):
                    load(sp, 0, i, piece)
                sp.wait_ge(b1_ready, 1)
                sp.dma_start(be2, io["b_e2"][0]).then_inc(ld_be2, 16)
                sp.dma_start(pin, io["p"][0, 0].rearrange("(t p) d -> p t d", p=P)).then_inc(ld_p, 16)
                sp.wait_ge(wo_ps, 4)
                sp.dma_start(wple, io["w_ple"][0].rearrange("(k p) n -> p k n", p=P)).then_inc(ld_ple, 16)
                sp.wait_ge(hp_ready, 2)
                sp.dma_start(wple_g[:, 0:2], w_gate[:, 0:2]).then_inc(ld_ple_gate, 16)
                with sp.Fori(1, NE) as e:
                    for i in range(PIECES):
                        sp.wait_ge(first["s"]["pieces_used"], e * PIECES - PIECES + (i + 1))
                        load(sp, e, i, piece)

            @block.gpsimd
            def _(pool):
                ch = Chain(pool, pool_ch)
                g = nc.gpsimd
                ch(g.memset(half, -0.5))
                for a in (kZs, kZw):
                    ch(g.memset(a[0:DH, 1, :], 0.0))
                    ch(g.memset(a[DH:P, 0, :], 0.0))
                ch(g.memset(kZd[0:DH, :, 1, :], 0.0))
                ch(g.memset(kZd[DH:P, :, 0, :], 0.0))
                ch(g.memset(V4, 0.0))
                ch(g.memset(kcZ, 0.0))
                ch(g.memset(hid4, 0.0))
                g.memset(P32, 0.0).then_inc(zeroed, 1)

                def rsqrt(dst, src, scale, done):
                    ch(g.tensor_scalar(dst, src, scale, EPS, ALU.mult, ALU.add))
                    n = src.shape
                    e = half[0:n[0], 0:int(np.prod(n[1:]))]
                    if len(n) == 3:
                        e = e.rearrange("p (a b) -> p a b", a=n[1])
                    g.tensor_tensor(dst, dst, e, ALU.pow).then_inc(done, 1)

                pool.wait_ge(zeroed, 1)
                pool.wait_ge(x_sq, 1)
                rsqrt(rs, ssx, 1.0 / DM, x_rs)
                g.memset(ikZ, 0.0).then_inc(zeroed, 1)
                pool.wait_ge(er_sb, 1)
                pool.dma_start(er_dram, erow).then_inc(st_er, 16)
                pool.wait_ge(st_er, 16)
                pool.dma_start(er_rep, er_dram.unsqueeze(1).to_broadcast([16, P, ERW])).then_inc(st_rep, 16)
                for n in range(2):
                    pool.wait_ge(n_var, n + 1)
                    rsqrt(v16, r16, 1.0 / DH, n_rs)
                    if n == 0:
                        pool.wait_ge(st_rep, 16)
                        pool.dma_start(bias, bass.AP(tensor=er_rep.tensor, offset=P - 1,
                                                     ap=[[ERW - 1, P], [P * ERW, 16], [1, SEQ]])).then_inc(ld_bias, 16)
                pool.wait_ge(i_used, 6)
                for t in range(TT):
                    n = P * (t + 1)
                    g.affine_select(out=score[:, t, 0:n], in_=score[:, t, 0:n], compare_op=ALU.is_ge, fill=BLOCKED, base=t * P,
                                    pattern=[[-1, n]], channel_multiplier=1).then_inc(score_cut, 1)
                for n in range(2, 5):
                    pool.wait_ge(n_var, n + 1)
                    h = NORMS[n][2]
                    rsqrt(v16[:, :, 0:h], r16[:, :, 0:h], 1.0 / DH, n_rs)
                pool.wait_ge(ld_bias, 16)
                pool.wait_ge(selm_ready, 2)
                pool.wait_ge(t_ps, TJOBS.index("T:R1") + 1)
                for u in range(8):
                    _, t, j = UNITS[u]
                    n = P * (t + 1)
                    o = P * (1 - t)
                    if u >= 2:
                        pool.wait_ge(s_log, u - 1)
                    g.tensor_tensor(Bd[u % 2][:, :, 0:n], bias[:, 8 + 2 * j:10 + 2 * j, o:o + n], bm(selm[:, t, 0:n], 2),
                                    ALU.add).then_inc(bd_ready, 1)
                    if u == 7:
                        pool.wait_ge(n_var, 6)
                        rsqrt(ckr[0:NCMP, 0:2], ckr[0:NCMP, 2:4], 1.0 / DH, n_rs)
                for t in range(TT):
                    pool.wait_ge(f_sq, t + 1)
                    rsqrt(rs[:, t:t + 1], ssx[:, t:t + 1], 1.0 / DM, f_rs)

            @block.scalar
            def _(sc):
                a = nc.scalar
                cst = io["consts"]
                sc.dma_start(const_all, cst).then_inc(ld_const, 16)
                for i, n in enumerate(("g_mix", "g_ffn", "g_ple")):
                    sc.dma_start(grow[i * 8:(i + 1) * 8, :], io[n][0].rearrange("(k p) -> k p", p=P)).then_inc(ld_const, 16)
                def tjob(name):
                    n = TJOBS.index(name)
                    b = ps[4 + n % 2]
                    sc.wait_ge(t_ps, n + 1)
                    t = int(name[-1]) if name[-1].isdigit() else 0
                    tc = slice(t * P, (t + 1) * P)
                    kind = name[2:].rstrip("0123456789")
                    if kind == "G":
                        a.copy(gT, b[:, 0:24]).then_inc(t_ev, 1)
                        sc.wait_ge(t_ev, n + 1)
                    elif kind == "X":
                        for i in range(2):
                            k = 2 * t + i
                            l = a.activation(hTv[:, k, :], b[:, i * SEQ:(i + 1) * SEQ], ACT.Copy, scale=gT[:, k:k + 1])
                        l.then_inc(t_ev, 1)
                    elif kind == "IX":
                        sc.wait_ge(zeroed, 2)
                        a.copy(iqT[:, :, tc], b[:, 0:2 * P].rearrange("p (a t) -> p a t", a=2))
                        for i in range(4):
                            l = a.copy(ikZ[32 * i:32 * i + 32, i, tc], b[32 * i:32 * i + 32, 2 * P:3 * P])
                        l.then_inc(t_ev, 1)
                    elif kind in ("DQ", "NQ"):
                        q = qdT if kind == "DQ" else qaT
                        a.copy(q[:, :, tc], b[:, :].rearrange("p (j t) -> p j t", j=4)).then_inc(t_ev, 1)
                    elif kind == "DK":
                        v4 = b[:, :].rearrange("p (j t) -> p j t", j=4)
                        a.copy(kZd[0:DH, :, 0, tc], v4[0:DH])
                        a.copy(kZd[DH:P, :, 1, tc], v4[DH:P]).then_inc(t_ev, 1)
                    elif kind == "K":
                        for i, kz in enumerate((kZs, kZw)):
                            for g in range(2):
                                l = a.copy(kz[g * DH:(g + 1) * DH, g, tc], b[g * DH:(g + 1) * DH, i * P:(i + 1) * P])
                        l.then_inc(t_ev, 1)
                    elif kind == "R":
                        a.copy(rawT[:, :, :, tc], b[:, :].rearrange("p (a g t) -> p a g t", a=2, g=2)).then_inc(t_ev, 1)
                    elif kind == "PE":
                        a.copy(peT, b[:, 0:32].rearrange("p (a l) -> p a l", a=2)).then_inc(t_ev, 1)
                    elif kind == "KC":
                        for g in range(2):
                            l = a.copy(kcZ[g * DH:(g + 1) * DH, g, 0:NCMP], b[g * DH:(g + 1) * DH, 0:NCMP])
                        l.then_inc(t_ev, 1)
                    elif kind == "CS":
                        a.copy(csb, b[:, 0:2 * P].rearrange("p (t n) -> p t n", t=TT)).then_inc(t_ev, 1)
                    elif kind == "C":
                        a.copy(PcT[:, t], b[:, 0:2 * P].rearrange("p (a t) -> p a t", a=2)).then_inc(t_ev, 1)

                def stage_act(stage):
                    if stage.startswith("T:"):
                        tjob(stage)
                    elif stage == "HID":
                        sc.wait_ge(h_ps, 1)
                        a.activation(hsg, ps[7][0:DH, 0:60].rearrange("p (a n) -> p a n", a=2), ACT.Exp, scale=-1.0).then_inc(h_exp, 1)
                    elif stage == "CMPKV":
                        sc.wait_ge(kc_copied, 1)
                        sc.wait_ge(zeroed, 1)
                        for g in range(2):
                            for j in range(4):
                                l = a.copy(V4[32 * j:32 * j + 32, g, j, :], ps[6][32 * j:32 * j + 32, (2 + g) * DH:(3 + g) * DH])
                        l.then_inc(v4_ready, 1)

                for stage in ORDER:
                    if stage.startswith("T:"):
                        tjob(stage)
                    elif stage == "ER":
                        sc.wait_ge(er_ps, 1)
                        a.copy(erow, ps[6][0:16, 0:384]).then_inc(er_sb, 1)
                    elif stage[0] == "Z":
                        c = int(stage[1:])
                        o, n = CHUNKS[c]
                        for t in range(TT):
                            sc.wait_ge(z_ps, 2 * c + t + 1)
                            src = ps[2 * (c % 2) + t][:, 0:n]
                            if c == 0 and t == 0:
                                sc.wait_ge(x_rs, 1)
                            a.activation(z[:, t, o:o + n], src, ACT.Copy, scale=rs[:, t:t + 1]).then_inc(z_ev, 1)
                        if c == C_N2:
                            sc.wait_ge(z_ev, 2 * c + 2)
                            a.activation(gsig, z[:, :, O_NG:O_NG + 24], ACT.Sigmoid)
                    elif stage == "I":
                        for i in range(6):
                            sc.wait_ge(i_ps, i + 1)
                            if i >= 2:
                                sc.wait_ge(i_used, i - 1)
                            a.activation(rl[:, i % 2, :], ps[7 - i % 2][:, :], ACT.Relu).then_inc(i_rl, 1)
                def exps(u):
                    n = P * (UNITS[u][1] + 1)
                    sc.wait_ge(s_log, u + 1)
                    for h in range(2):
                        l = a.activation(L[:, u % 4, h, 0:n], L[:, u % 4, h, 0:n], ACT.Exp, bias=nmx[:, u % 4, h:h + 1], accum_out=ssum[:, u % 4, h:h + 1])
                    l.then_inc(s_exp, 1)

                def evac_p(u):
                    nb = UNITS[u][1] + 1
                    n = TJOBS.index(f"U{u}")
                    sc.wait_ge(t_ps, n + 1)
                    if u >= 2:
                        sc.wait_ge(o_ps, u - 1)
                    a.copy(PT[:, u % 2, 0:2 * nb, :], ps[4 + n % 2][:, 0:2 * nb * P].rearrange("p (a t) -> p a t", t=P)).then_inc(t_ev, 1)

                def evac_o(u):
                    if u >= 8 and (u - 8) % 2 == 0:
                        return
                    i = item_of(u)
                    kind, t, j = UNITS[u]
                    sc.wait_ge(o_ps, u + 1)
                    a.copy(oTv[:, 1 if i < 8 else 0, j, t * P:(t + 1) * P], ps[6 + i % 2][:, 0:P]).then_inc(o_ev, 1)

                def late_copies(u):
                    for c, t, k in LATE_OF[u]:
                        if k == KT - 1:
                            o = CHUNKS[c][0] - O_GA
                            sc.wait_ge(st_er, 16)
                            sc.wait_ge(z_ps, 2 * c + t + 1)
                            a.activation(gates[:, t, o:o + 512], ps[t][:, :], ACT.Copy, scale=rs[:, t:t + 1]).then_inc(z_ev, 1)

                for u in range(STEPS):
                    if u < NU:
                        exps(u)
                    if u in STAGE_AT:
                        stage_act(STAGE_AT[u])
                    if u == C_SOFT:
                        for t in range(TT):
                            n = CMP_SEEN[t]
                            sc.wait_ge(c_log, t + 1)
                            a.activation(cL[:, t, :, 0:n], cL[:, t, :, 0:n], ACT.Exp).then_inc(c_exp, 1)
                    if u >= 1:
                        late_copies(u - 1)
                    if 3 <= u < NU + 3:
                        evac_p(u - 3)
                        if u - 3 == C_AFTER:
                            tjob("T:C0")
                            tjob("T:C1")
                    if u >= 4:
                        evac_o(u - 4)
                late_copies(STEPS - 1)
                sc.wait_ge(z_ev, 2 * NZ)
                for t in range(TT):
                    a.activation(gates[:, t, :], gates[:, t, :], ACT.Sigmoid).then_inc(gates_ready, 1)
                def part(q, t, n):
                    sc.wait_ge(xr_ready, n)
                    a.copy(hp[:, q, t], xr[t]).then_inc(hp_ready, 1)

                for n in range(4):
                    k = NT + n
                    sc.wait_ge(t_ps, k + 1)
                    t, k0 = n // 2, 4 * (n % 2)
                    a.copy(hTv[:, k0:k0 + 4, t * P:(t + 1) * P], ps[4 + k % 2][:, :].rearrange("p (k t) -> p k t", k=4)).then_inc(t_ev, 1)
                part(1, 0, 1)
                part(2, 0, 2)
                for n in range(4):
                    k = NT + 4 + n
                    sc.wait_ge(t_ps, k + 1)
                    if n == 0:
                        sc.wait_ge(wo_ps, 2)
                    if n == 2:
                        sc.wait_ge(wo_ps, 4)
                    t, k0 = n // 2, 4 * (n % 2)
                    for i in range(4):
                        l = a.activation(hTv[:, k0 + i, t * P:(t + 1) * P], ps[4 + k % 2][:, i * P:(i + 1) * P], ACT.Copy,
                                         scale=gT[:, 8 + k0 + i:9 + k0 + i])
                    l.then_inc(t_ev, 1)
                sc.wait_ge(t_ps, NT + 9)
                a.copy(pT, ps[4 + NT % 2][:, :].rearrange("p (k t) -> p k t", k=2)).then_inc(t_ev, 1)
                part(1, 1, 3)
                sc.wait_ge(lg_ready, 1)
                a.activation(e4, e4, ACT.Exp).then_inc(rt_exp, 1)

                def ple_copy(i):
                    sc.wait_ge(pl_ps, i + 1)
                    a.copy(pl[:, i // 2, (i % 2) * 512:(i % 2 + 1) * 512], ps[i][:, :]).then_inc(pl_ev, 1)

                sc.wait_ge(rt_ps, 2)
                ple_copy(0)
                ple_copy(1)
                part(2, 1, 4)
                ple_copy(2)
                ple_copy(3)
                k = NT + 9
                sc.wait_ge(t_ps, k + 1)
                a.copy(WT, ps[4 + k % 2][0:NE, 0:SEQ]).then_inc(t_ev, 1)
                expert_act(sc, first)

            @block.vector
            def _(ve):
                d = nc.vector
                ch = Chain(ve, dve_ch)
                ve.wait_ge(ld_x, 16)
                for t in range(TT):
                    l = d.tensor_tensor_reduce(out=xn[:, t, :], in0=x[:, t, :], in1=x[:, t, :], scale=1.0, scalar=0.0,
                                               op0=ALU.mult, op1=ALU.add, accum_out=ssx[:, t:t + 1])
                l.then_inc(x_sq, 1)

                def norm_sq(n):
                    _, o, h, _, _ = NORMS[n]
                    ve.wait_ge(z_ev, 2 * (NORM_CHUNK[n] + 1))
                    src = z[:, :, o:o + h * DH]
                    ch(d.tensor_tensor(sq[:, :, 0:h * DH], src, src, ALU.mult))
                    d.tensor_reduce(r16[:, :, 0:h], sq[:, :, 0:h * DH].rearrange("p t (h e) -> p t h e", h=h), AX.X, ALU.add).then_inc(n_var, 1)

                def norm_mul(n, at):
                    name, o, h, g, s = NORMS[n]
                    ve.wait_ge(n_rs, n + 1)
                    if s != 1.0:
                        ch(d.tensor_scalar(v16[:, :, 0:h], v16[:, :, 0:h], s, None, ALU.mult))
                    for t in range(TT):
                        src = z[:, t, o:o + h * DH].rearrange("p (h e) -> p h e", h=h)
                        ch(d.tensor_tensor(sq[:, t, 0:h * DH].rearrange("p (h e) -> p h e", h=h), src, bc(v16[:, t, 0:h], DH), ALU.mult))
                    for t in range(TT):
                        dst = qn[:, t, at:at + h * DH]
                        if name == "nq":
                            dst = dst.rearrange("p (j g e) -> p g j e", j=4, g=2)
                            src = sq[:, t, :].rearrange("p (g j e) -> p g j e", g=2, j=4)
                            for g2 in range(2):
                                l = d.tensor_tensor(dst[:, g2], src[:, g2], bm(gqk[:, g, :], 4), ALU.mult)
                        else:
                            l = d.tensor_tensor(dst.rearrange("p (h e) -> p h e", h=h), sq[:, t, 0:h * DH].rearrange("p (h e) -> p h e", h=h),
                                                bm(gqk[:, g, :], h), ALU.mult)
                    ch_sig(l)

                def ch_sig(l):
                    qn_n[0] += 1
                    l.then_inc(qn_ready, 1)
                    ve.wait_ge(qn_ready, qn_n[0])
                qn_n = [0]

                ve.wait_ge(z_ev, 2)
                for t in range(TT):
                    d.tensor_copy(qn[:, t, 0:P].rearrange("p (r e) -> p r e", r=4), bm(z[:, t, O_IK:O_IK + ID], 4))
                ch(d.tensor_scalar(iwS, z[:, :, O_IW:O_IW + IH], ID ** -0.5 * IH ** -0.5, None, ALU.mult))
                ch(d.memset(score, 0.0))
                d.memset(m8, 0.0).then_inc(ikrep_ready, 1)
                ve.wait_ge(ld_small, 16 * 8)
                norm_sq(0)
                ve.wait_ge(t_ps, TJOBS.index("T:IX1") + 1)
                norm_mul(0, 0)
                for i in range(6):
                    ve.wait_ge(i_rl, i + 1)
                    if i < 4:
                        parts = [(1, 4 * (i // 2) + 2 * (i % 2) + r, rl[:, i % 2, r * SEQ:(r + 1) * SEQ], SEQ) for r in range(2)]
                    else:
                        parts = [(0, 4 * (i - 4) + r, rl[:, i % 2, r * P:(r + 1) * P], P) for r in range(4)]
                    for q, (t, h, src, n) in enumerate(parts):
                        l = d.scalar_tensor_tensor(score[:, t, 0:n], src, iwS[:, t, h:h + 1], score[:, t, 0:n], ALU.mult, ALU.add)
                        if q < len(parts) - 1:
                            ch(l)
                    l.then_inc(i_used, 1)
                    ve.wait_ge(i_used, i + 1)
                norm_sq(1)
                ve.wait_ge(t_ps, TJOBS.index("T:DQ1") + 1)
                norm_mul(1, 0)

                def topk(t):
                    ve.wait_ge(score_cut, t + 1)
                    n = P * (t + 1)
                    for r in range(KEEP // 8):
                        ch(d.max(m8, score[:, t, 0:n]))
                        ch(d.match_replace(score[:, t, 0:n], m8, score[:, t, 0:n], TAKEN))
                    d.tensor_scalar(selm[:, t, 0:n], score[:, t, 0:n], (BLOCKED + TAKEN) / 2, NEG, ALU.is_gt, ALU.mult).then_inc(selm_ready, 1)

                topk(0)
                norm_sq(2)
                ve.wait_ge(t_ps, TJOBS.index("T:DK1") + 1)
                norm_mul(2, 0)
                topk(1)
                norm_sq(3)
                ve.wait_ge(t_ps, TJOBS.index("T:NQ1") + 1)
                norm_mul(3, 0)
                norm_sq(4)
                norm_mul(4, P)
                for t in range(TT):
                    src = z[:, t, O_KV:O_KV + 4 * DH].rearrange("p (i e) -> p i e", i=4).unsqueeze(2).to_broadcast([P, 4, 2, DH])
                    l = d.tensor_copy(sq[:, t, :].rearrange("p (i r e) -> p i r e", i=4, r=2), src)
                l.then_inc(dup_ready, 1)
                ve.wait_ge(t_ev, TJOBS.index("T:PE") + 1)
                for kv in range(2):
                    for q in range(2):
                        for hf in range(2):
                            h = slice(q * DH, (q + 1) * DH)
                            src = rawT[h, kv].rearrange("p g (c l q) -> p l g c q", l=8, q=2)[:, :, :, hf:hf + NCMP, q]
                            pe = peT[h, kv, hf * 8:(hf + 1) * 8].unsqueeze(2).unsqueeze(3).to_broadcast([DH, 8, 2, NCMP])
                            l = d.tensor_tensor(zb[h, kv, hf * 8:(hf + 1) * 8].rearrange("p l (g c) -> p l g c", g=2), src, pe, ALU.add)
                l.then_inc(zb_ready, 1)
                def mark(ins):
                    ch.n += 1
                    ins.then_inc(dve_ch, 1)
                    return ch.n

                def compressed():
                    ve.wait_ge(t_ev, TJOBS.index("T:CS") + 1)
                    lv = [cL[:, t, :, 0:CMP_SEEN[t]] for t in range(TT)]
                    for t in range(TT):
                        n, o = CMP_SEEN[t], P * (1 - t) + CMP_LEN - 1
                        for g in range(2):
                            src = csb[:, t, :].rearrange("p (j g c) -> p g j c", j=4, g=2)[:, g, :, 0:n]
                            bv = bias[:, 4 * g:4 * g + 4, o:o + (n - 1) * CMP_STRIDE + 1:CMP_STRIDE]
                            l = mark(d.tensor_tensor(cL[:, t, 4 * g:4 * g + 4, 0:n], src, bv, ALU.add))
                    ve.wait_ge(dve_ch, l)
                    for t in range(TT):
                        l = mark(d.tensor_reduce(cst[:, t, 0, :], lv[t], AX.X, ALU.max))
                    ve.wait_ge(dve_ch, l)
                    ch(d.tensor_scalar(cst[:, :, 1, :], cst[:, :, 0, :], NEG / 10, None, ALU.max))
                    for t in range(TT):
                        d.tensor_tensor(lv[t], lv[t], bc(cst[:, t, 1, :], CMP_SEEN[t]), ALU.subtract).then_inc(c_log, 1)

                def compressed_end():
                    lv = [cL[:, t, :, 0:CMP_SEEN[t]] for t in range(TT)]
                    ve.wait_ge(c_exp, 2)
                    for t in range(TT):
                        l = mark(d.tensor_reduce(cst[:, t, 2, :], lv[t], AX.X, ALU.add))
                    ve.wait_ge(dve_ch, l)
                    ch(d.tensor_scalar(cst[:, :, 2, :], cst[:, :, 2, :], 1e-30, None, ALU.max))
                    ch(d.reciprocal(cst[:, :, 3, :], cst[:, :, 2, :]))
                    ch(d.tensor_tensor(cst[:, :, 3, :], cst[:, :, 3, :], gsig[:, :, 0:24:3], ALU.mult))
                    for t in range(TT):
                        d.tensor_tensor(P32[:, t, :, 0:CMP_SEEN[t]], lv[t], bc(cst[:, t, 3, :], CMP_SEEN[t]), ALU.mult).then_inc(c_ready, 1)

                ve.wait_ge(ld_bias, 16)
                for u in range(NU + 2):
                    v = u - 2
                    if v >= 0:
                        kp, tp, jp = UNITS[v]
                        rp = rcp[:, v % 4, :]
                        ve.wait_ge(s_exp, v + 1)
                        last = mark(d.tensor_scalar(rp, ssum[:, v % 4, :], 1e-30, None, ALU.max))
                    for h in range(2):
                        if u < NU:
                            kind, t, j = UNITS[u]
                            n, o = P * (t + 1), P * (1 - t)
                            if h == 0:
                                ve.wait_ge(s_ps, u + 1)
                                if kind == "dsa":
                                    ve.wait_ge(bd_ready, u + 1)
                                if u == 2:
                                    ve.wait_ge(h_ps, 1)
                                if u >= 4:
                                    ve.wait_ge(t_ps, TJOBS.index(f"U{u - 4}") + 1)
                            b = Bd[u % 2][:, h, 0:n] if kind == "dsa" else bias[:, 4 * h + j, o:o + n]
                            top = mark(d.tensor_tensor_reduce(out=L[:, u % 4, h, 0:n], in0=ps[2 + u % 2][:, h * n:(h + 1) * n], in1=b, scale=1.0,
                                                              scalar=NEG * 10, op0=ALU.add, op1=ALU.max, accum_out=mx[:, u % 4, h:h + 1]))
                        if v >= 0 and h == 0:
                            ve.wait_ge(dve_ch, last)
                            last = mark(d.reciprocal(rp, rp))
                    if v >= 0 and kp != "dsa":
                        b = 1 if kp == "slc" else 2
                        ve.wait_ge(dve_ch, last)
                        last = mark(d.tensor_tensor(rp, rp, gsig[:, tp, 3 * jp + b:3 * jp + b + 13:12], ALU.mult))
                    if u < NU:
                        ve.wait_ge(dve_ch, top)
                        d.tensor_scalar(nmx[:, u % 4, :], mx[:, u % 4, :], -1.0, None, ALU.mult).then_inc(s_log, 1)
                    if v >= 0:
                        n = P * (tp + 1)
                        ve.wait_ge(dve_ch, last)
                        for h in range(2):
                            l = d.tensor_scalar(L[:, v % 4, h, 0:n], L[:, v % 4, h, 0:n], rp[:, h:h + 1], None, ALU.mult)
                        l.then_inc(s_prob, 1)
                    if u == HIDDEN_AT:
                        ve.wait_ge(h_exp, 1)
                        ch(d.tensor_scalar(hsg, hsg, 1.0, None, ALU.add))
                        ch(d.reciprocal(hsg, hsg))
                        ch(d.tensor_tensor(hid, hsg, ps[7][0:DH, 0:60].rearrange("p (a n) -> p a n", a=2), ALU.mult))
                        ve.wait_ge(zeroed, 1)
                        for g in range(2):
                            l = d.tensor_copy(hid4[:, g, :, 0:NCMP], bm(hid[:, 1, g * NCMP:(g + 1) * NCMP], 4))
                        l.then_inc(hid_ready, 1)
                    if u == KEYS_AT:
                        ve.wait_ge(kc_ps, 1)
                        d.tensor_copy(kcs[0:NCMP], ps[6][0:NCMP, 0:2 * DH].rearrange("p (g e) -> p g e", g=2)).then_inc(kc_copied, 1)
                        ve.wait_ge(kc_copied, 1)
                        kc = kcs[0:NCMP]
                        ch(d.tensor_tensor(kcq[0:NCMP], kc, kc, ALU.mult))
                        d.tensor_reduce(ckr[0:NCMP, 2:4], kcq[0:NCMP], AX.X, ALU.add).then_inc(n_var, 1)
                    if u == NORMED_AT:
                        ve.wait_ge(n_rs, 6)
                        ch(d.tensor_tensor(kcq[0:NCMP], kc, bc(ckr[0:NCMP, 0:2], DH), ALU.mult))
                        d.tensor_tensor(kcs[0:NCMP], kcq[0:NCMP], bm(gqk[0:NCMP, 1, :], 2), ALU.mult).then_inc(kcn_ready, 1)
                    if u == C_SOFT:
                        compressed()
                    if u == C_SOFT + 1:
                        compressed_end()

                for i in range(4):
                    t, n = i // 2, (i % 2) * 512
                    ve.wait_ge(pr_ps, i + 1)
                    ve.wait_ge(gates_ready, t + 1)
                    ch(d.tensor_tensor(mtmp[:, 0, :], ps[2 * (i % 2)][:, :], gates[:, t, n:n + 512], ALU.mult))
                    ch(d.tensor_tensor(mtmp[:, 1, :], ps[2 * (i % 2) + 1][:, :], gates[:, t, DM + n:DM + n + 512], ALU.mult))
                    d.tensor_tensor(merged[:, t, n:n + 512], mtmp[:, 0, :], mtmp[:, 1, :], ALU.add).then_inc(pr_used, 1)
                    ve.wait_ge(pr_used, i + 1)
                ve.wait_ge(ld_b1, 48)
                ch(d.tensor_copy(b1p, b1f))
                for i, lo in enumerate((NE, 2 * NE, 2 * NE)):
                    hi = lo + NE
                    ch(d.tensor_tensor(b1f[lo:hi], b1f[lo:hi], b1p[lo:hi], ALU.subtract))
                    l = d.tensor_copy(b1p[lo:hi], b1f[lo:hi])
                    if i < 2:
                        ch(l)
                l.then_inc(b1_ready, 1)
                def ffn_input(t):
                    for n in range(2):
                        ve.wait_ge(wo_ps, 2 * t + n + 1)
                        xs = x[:, t, n * 512:(n + 1) * 512]
                        d.tensor_tensor(xs, ps[2 * t + n][:, :], xs, ALU.add).then_inc(x2_ready, 1)
                    ve.wait_ge(x2_ready, 2 * t + 2)
                    d.tensor_tensor_reduce(out=xh[t], in0=x[:, t, :], in1=x[:, t, :], scale=1.0, scalar=0.0,
                                           op0=ALU.mult, op1=ALU.add, accum_out=ssx[:, t:t + 1]).then_inc(f_sq, 1)
                    ve.wait_ge(f_rs, t + 1)
                    ch(d.tensor_scalar(xh[t], x[:, t, :], rs[:, t:t + 1], None, ALU.mult))
                    ch(d.tensor_copy(hp[:, 0, t], xh[t]))
                    d.tensor_tensor(xr[t], xh[t], hp[:, 0, t], ALU.subtract).then_inc(xr_ready, 1)

                def second_remainder(t):
                    ve.wait_ge(xr_ready, 2 * t + 1)
                    ve.wait_ge(hp_ready, 2 * t + 1)
                    d.tensor_tensor(xr[t], xr[t], hp[:, 1, t], ALU.subtract).then_inc(xr_ready, 1)

                ffn_input(0)
                second_remainder(0)
                ffn_input(1)
                ve.wait_ge(ld_route, 32)
                for t in range(TT):
                    ve.wait_ge(rt_ps, t + 1)
                    ch(d.scalar_tensor_tensor(lg[:, t, :], ps[6 + t][:, 0:NE], rs[:, t:t + 1], br, ALU.mult, ALU.add))
                    ch(d.max(top8[:, t, :], lg[:, t, :]))
                d.tensor_tensor(e4, top8[:, :, 0:TOPK], bc(top8[:, :, 0], TOPK), ALU.subtract).then_inc(lg_ready, 1)
                for t in range(TT):
                    l = d.max_index(idx8[:, t, :], top8[:, t, :], lg[:, t, :])
                ch(l)
                ch(d.tensor_copy(idxf, idx8))
                ch(d.tensor_scalar(idxf, idxf, 1.0, None, ALU.add))
                ch(d.tensor_tensor(eq, iota1[:, 0, 0:NE].unsqueeze(1).unsqueeze(1).to_broadcast([P, TT, TOPK, NE]), bc(idxf[:, :, 0:TOPK], NE), ALU.is_equal))
                d.tensor_reduce(Mt, eq.rearrange("p t k e -> p t e k"), AX.X, ALU.add).then_inc(m_ready, 1)
                ve.wait_ge(rt_exp, 1)
                ch(d.tensor_reduce(sm2[:, :, 0], e4, AX.X, ALU.add))
                ch(d.reciprocal(sm2[:, :, 1], sm2[:, :, 0]))
                ch(d.tensor_tensor(e4, e4, bc(sm2[:, :, 1], TOPK), ALU.mult))
                ch(d.tensor_tensor(eq, eq, bc(e4, NE), ALU.mult))
                d.tensor_reduce(Wt[:, :, 0:NE], eq.rearrange("p t k e -> p t e k"), AX.X, ALU.add).then_inc(wt_ready, 1)
                ve.wait_ge(wt_ready, 1)
                second_remainder(1)
                ve.wait_ge(rk_ps, 1)
                for t in range(TT):
                    ch(d.scalar_tensor_tensor(rank[:, t, 0:NE], ps[7][:, t * NE:(t + 1) * NE], 1.0, Mt[:, t, :], ALU.add, ALU.mult))
                    for r in range(1, ROUNDS):
                        d.tensor_scalar(rank[:, t, r * NE:(r + 1) * NE], rank[:, t, 0:NE], float(-SLOTS * r), None, ALU.add)
                        d.tensor_copy(Wt[:, t, r * NE:(r + 1) * NE], Wt[:, t, 0:NE])
                ch(d.tensor_reduce(cmax, ps[7][:, 2 * NE:3 * NE], AX.X, ALU.max))
                d.tensor_copy(cmaxi, cmax).then_inc(ranks_taken, 1)
                expert_dve(ve, first)

            @block.tensor
            def _(te):
                mm, tr = nc.tensor.matmul, nc.tensor.transpose
                te.wait_ge(ld_const, 16 * 4)

                def tbank(n):
                    if n >= 2:
                        te.wait_ge(t_ev, n - 1)
                    return ps[4 + n % 2]

                def tjob(name):
                    n = TJOBS.index(name)
                    b = tbank(n)
                    t = int(name[-1]) if name[-1].isdigit() else 0
                    kind = name[2:].rstrip("0123456789")
                    if kind == "G":
                        l = tr(b[:, 0:24], grow, ident[0:24, 0:24])
                    elif kind == "X":
                        te.wait_ge(ld_x, 16)
                        for i in range(2):
                            for q in range(TT):
                                l = tr(b[:, i * SEQ + q * P:i * SEQ + (q + 1) * P], x[:, q, (2 * t + i) * P:(2 * t + i + 1) * P], ident)
                    elif kind == "IX":
                        te.wait_ge(ikrep_ready, 1)
                        for i in range(2):
                            tr(b[:, i * P:(i + 1) * P], z[:, t, O_IQ + i * P:O_IQ + (i + 1) * P], ident)
                        l = tr(b[:, 2 * P:3 * P], qn[:, t, 0:P], ident)
                    elif kind in ("DQ", "DK", "NQ"):
                        te.wait_ge(qn_ready, {"DQ": 1, "DK": 2, "NQ": 3}[kind])
                        for j in range(4):
                            l = tr(b[:, j * P:(j + 1) * P], qn[:, t, j * P:(j + 1) * P], ident)
                    elif kind == "K":
                        te.wait_ge(qn_ready, 5)
                        tr(b[:, 0:P], qn[:, t, 0:P], ident)
                        l = tr(b[:, P:2 * P], qn[:, t, P:2 * P], ident)
                    elif kind == "R":
                        te.wait_ge(dup_ready, 1)
                        for i in range(4):
                            l = tr(b[:, i * P:(i + 1) * P], sq[:, t, i * P:(i + 1) * P], ident)
                    elif kind == "PE":
                        te.wait_ge(ld_small, 16 * 8)
                        for i in range(2):
                            l = tr(b[:, i * 16:(i + 1) * 16], pe_in[:, i, :], ident[0:16, 0:16])
                    elif kind == "KC":
                        te.wait_ge(kcn_ready, 1)
                        l = tr(b[:, 0:NCMP], kcs[0:NCMP].rearrange("c g d -> c (g d)"), ident[0:NCMP, 0:NCMP])
                    elif kind == "CS":
                        te.wait_ge(t_ev, TJOBS.index("T:KC") + 1)
                        te.wait_ge(v4_ready, 1)
                        for q in range(TT):
                            for j in range(4):
                                l = mm(b[:, q * P + j * 32:q * P + (j + 1) * 32], qaT[:, j, q * P:(q + 1) * P],
                                       kcZ.rearrange("p g c -> p (g c)"), start=True, stop=True)
                    elif kind == "C":
                        te.wait_ge(c_ready, t + 1)
                        for g in range(2):
                            l = tr(b[:, g * P:(g + 1) * P], P32[:, t, 4 * g:4 * g + 4, :].rearrange("p j c -> p (j c)"), ident)
                    l.then_inc(t_ps, 1)

                for stage in ORDER:
                    if stage.startswith("T:"):
                        tjob(stage)
                    elif stage[0] == "Z":
                        c = int(stage[1:])
                        o, n = CHUNKS[c]
                        te.wait_ge(ld_w[WBUF[c]], 16 * WBUF[0:c + 1].count(WBUF[c]))
                        te.wait_ge(t_ev, 5)
                        if c >= 2:
                            te.wait_ge(z_ev, 2 * (c - 1))
                        wv = wbuf[:, WBUF[c] * 4096:WBUF[c] * 4096 + KT * n].rearrange("p (k n) -> p k n", k=KT)
                        for t in range(TT):
                            for k in range(KT):
                                l = mm(ps[2 * (c % 2) + t][:, 0:n], hTv[:, k, t * P:(t + 1) * P], wv[:, k, :], start=k == 0, stop=k == KT - 1)
                            l.then_inc(z_ps, 1)
                    elif stage == "ER":
                        te.wait_ge(ld_tab, 48)
                        mm(ps[6][0:16, 0:384], tab, onehot, start=True, stop=True).then_inc(er_ps, 1)
                    elif stage == "I":
                        te.wait_ge(t_ev, TJOBS.index("T:IX1") + 1)
                        for i in range(6):
                            if i == 1:
                                te.wait_ge(er_sb, 1)
                            if i >= 2:
                                te.wait_ge(i_rl, i - 1)
                            if i < 4:
                                lhs, rhs = iqT[:, i // 2, P:2 * P], ikZ[:, 2 * (i % 2):2 * (i % 2) + 2, :]
                            else:
                                lhs, rhs = iqT[:, i - 4, 0:P], ikZ[:, :, 0:P]
                            mm(ps[7 - i % 2][:, :], lhs, rhs, start=True, stop=True).then_inc(i_ps, 1)

                def stage_pe(stage):
                    if stage.startswith("T:"):
                        tjob(stage)
                    elif stage == "HID":
                        te.wait_ge(ld_ck, 32)
                        te.wait_ge(zb_ready, 1)
                        te.wait_ge(i_rl, 6)
                        for kv in range(2):
                            for l2 in range(16):
                                l = mm(ps[7][0:DH, kv * 30:(kv + 1) * 30], wck1[:, kv, l2, :], zb[:, kv, l2, :], start=l2 == 0, stop=l2 == 15)
                        l.then_inc(h_ps, 1)
                    elif stage == "CMPKV":
                        te.wait_ge(hid_ready, 1)
                        te.wait_ge(o_ev, 1)
                        for g in range(2):
                            mm(ps[6][0:NCMP, g * DH:(g + 1) * DH], hid[:, 0, g * NCMP:(g + 1) * NCMP], ck2w[:, 0, :], start=True, stop=True)
                        for g in range(2):
                            l = mm(ps[6][:, (2 + g) * DH:(3 + g) * DH], hid4[:, g].rearrange("p j c -> p (j c)"), ck2w[:, 1, :], start=True, stop=True)
                        l.then_inc(kc_ps, 1)

                def scores(u):
                    kind, t, j = UNITS[u]
                    n = P * (t + 1)
                    if u < 2:
                        te.wait_ge(z_ev, 2 * (C_G - 1))
                    else:
                        te.wait_ge(s_log, u - 1)
                    q, k = {"dsa": (qdT, kZd[:, j]), "slc": (qaT, kZs), "win": (qaT, kZw)}[kind]
                    mm(ps[2 + u % 2][:, 0:2 * n], q[:, j, t * P:(t + 1) * P], k[:, :, 0:n], start=True, stop=True).then_inc(s_ps, 1)

                def flip(u):
                    t = UNITS[u][1]
                    b = tbank(TJOBS.index(f"U{u}"))
                    te.wait_ge(s_prob, u + 1)
                    for h in range(2):
                        for s in range(t + 1):
                            l = tr(b[:, (h * (t + 1) + s) * P:(h * (t + 1) + s + 1) * P], L[:, u % 4, h, s * P:(s + 1) * P], ident)
                    l.then_inc(t_ps, 1)

                def values(u):
                    kind, t, j = UNITS[u]
                    i = item_of(u)
                    te.wait_ge(t_ev, TJOBS.index(f"U{u}") + 1)
                    if i >= 2:
                        te.wait_ge(o_ev, i - 1)
                    if u == 2:
                        te.wait_ge(kc_copied, 1)
                        te.wait_ge(v4_ready, 1)
                    dst = [ps[6 + i % 2][h * DH:(h + 1) * DH, 0:P] for h in range(2)]
                    if kind == "slc":
                        for h in range(2):
                            mm(dst[h], V4[:, h, j, :], PcT[:, t, h, :], start=True, stop=False)
                    for s_ in range(t + 1):
                        for h in range(2):
                            o = {"dsa": O_DV + (2 * j + h) * DH, "slc": O_KV + 3 * P + h * DH, "win": O_KV + 5 * P + h * DH}[kind]
                            l = mm(dst[h], z[:, s_, o:o + DH], PT[:, u % 2, h * (t + 1) + s_, :], start=kind == "dsa" and s_ == 0,
                                   stop=kind != "slc" and s_ == t)
                    l.then_inc(o_ps, 1)

                def late(c, t, k):
                    if t == 0 and k == 0:
                        te.wait_ge(ld_w[WBUF[c]], 16 * WBUF[0:c + 1].count(WBUF[c]))
                    if k == 0:
                        te.wait_ge(z_ev, 2 * c + t - 1)
                    l = mm(ps[t][:, :], hTv[:, k, t * P:(t + 1) * P],
                           wbuf[:, WBUF[c] * 4096 + k * 512:WBUF[c] * 4096 + (k + 1) * 512], start=k == 0, stop=k == KT - 1)
                    if k == KT - 1:
                        l.then_inc(z_ps, 1)

                for u in range(STEPS):
                    if u < NU:
                        scores(u)
                    if u in STAGE_AT:
                        stage_pe(STAGE_AT[u])
                    if 3 <= u < NU + 3:
                        flip(u - 3)
                        if u - 3 == C_AFTER:
                            tjob("T:C0")
                            tjob("T:C1")
                    for step in LATE_OF[u]:
                        late(*step)
                    if u >= 4:
                        values(u - 4)
                te.wait_ge(ld_wab, 48)
                te.wait_ge(o_ev, NITEM)
                te.wait_ge(z_ev, 2 * NZ)

                def branch(i):
                    t, n = i // 2, (i % 2) * 512
                    if i >= 2:
                        te.wait_ge(pr_used, i - 1)
                    for m_ in range(2):
                        for j in range(4):
                            l = mm(ps[2 * (i % 2) + m_][:, :], oTv[:, m_, j, t * P:(t + 1) * P], (wa, wb)[m_][:, j, n:n + 512], start=j == 0, stop=j == 3)
                    l.then_inc(pr_ps, 1)

                def half_rows(src, n, at):
                    b = tbank(NT + at)
                    t, k0 = n // 2, 4 * (n % 2)
                    for i in range(4):
                        l = tr(b[:, i * P:(i + 1) * P], src[:, t, (k0 + i) * P:(k0 + i + 1) * P], ident)
                    l.then_inc(t_ps, 1)

                def merged_rows(n):
                    te.wait_ge(pr_used, n + 1)
                    half_rows(merged, n, n)

                def w_out(i):
                    t, n = i // 2, (i % 2) * 512
                    te.wait_ge(t_ev, NT + 2 * t + 2)
                    te.wait_ge(pr_used, 3 + t)
                    for k in range(KT):
                        l = mm(ps[i][:, :], hTv[:, k, t * P:(t + 1) * P], wo[:, k, n:n + 512], start=k == 0, stop=k == KT - 1)
                    l.then_inc(wo_ps, 1)

                def x_rows(n):
                    te.wait_ge(x2_ready, n + 1)
                    half_rows(x, n, 4 + n)

                def router(t):
                    te.wait_ge(t_ev, NT + 6 + 2 * t)
                    for k in range(KT):
                        l = mm(ps[6 + t][:, 0:NE], hTv[:, k, t * P:(t + 1) * P], wr[:, k, :], start=k == 0, stop=k == KT - 1)
                    l.then_inc(rt_ps, 1)

                branch(0)
                branch(1)
                branch(2)
                merged_rows(0)
                merged_rows(1)
                branch(3)
                merged_rows(2)
                te.wait_ge(ld_wo, 16)
                w_out(0)
                merged_rows(3)
                w_out(1)
                w_out(2)
                x_rows(0)
                w_out(3)
                x_rows(1)
                x_rows(2)
                te.wait_ge(ld_route, 32)
                router(0)
                x_rows(3)
                router(1)

                def ple(i):
                    t, n = i // 2, (i % 2) * 512
                    for k in range(2):
                        l = mm(ps[i][:, :], pT[:, k, t * P:(t + 1) * P], wple[:, k, n:n + 512], start=k == 0, stop=k == 1)
                    l.then_inc(pl_ps, 1)

                b = tbank(NT + 8)
                te.wait_ge(ld_p, 16)
                for k in range(2):
                    for t in range(TT):
                        l = tr(b[:, k * SEQ + t * P:k * SEQ + (t + 1) * P], pin[:, t, k * P:(k + 1) * P], ident)
                l.then_inc(t_ps, 1)
                te.wait_ge(t_ev, NT + 9)
                te.wait_ge(ld_ple, 16)
                for i in range(2):
                    ple(i)
                te.wait_ge(m_ready, 1)
                mm(ps[7][:, 0:NE], tri, Mt[:, 0, :], start=True, stop=True)
                mm(ps[7][:, NE:2 * NE], ones, Mt[:, 0, :], start=True, stop=False)
                mm(ps[7][:, NE:2 * NE], tri, Mt[:, 1, :], start=False, stop=True)
                mm(ps[7][:, 2 * NE:3 * NE], ones, Mt[:, 0, :], start=True, stop=False)
                mm(ps[7][:, 2 * NE:3 * NE], ones, Mt[:, 1, :], start=False, stop=True).then_inc(rk_ps, 1)
                for i in range(2, 4):
                    ple(i)
                b = tbank(NT + 9)
                te.wait_ge(wt_ready, 1)
                for t in range(TT):
                    l = tr(b[0:NE, t * P:(t + 1) * P], Wt[:, t, 0:NE], ident)
                l.then_inc(t_ps, 1)
                te.wait_ge(t_ev, NT + 10)
                te.wait_ge(ld_be2, 16)
                te.wait_ge(ranks_taken, 1)
                te.wait_ge(pl_ev, 4)
                te.wait_ge(hp_ready, 4)
                for t in range(TT):
                    for n in range(2):
                        mm(ps[4 + 2 * t + n][:, :], WT[:, t * P:(t + 1) * P], be2[:, n * 512:(n + 1) * 512], start=True, stop=False, skip_group_check=True)
                expert_pe(te, first)

        with nc.Block() as block:
            def some(eng):
                return eng.If(eng.value_load(cmaxi[0:1, 0:1], min_val=0, max_val=SEQ) > SLOTS)

            @block.sync
            def _(sp):
                with some(sp):
                    for i in range(PIECES):
                        load(sp, 0, i, rest["piece"])
                    with sp.Fori(1, rest["visits"]) as it:
                        for i in range(PIECES):
                            sp.wait_ge(rest["s"]["pieces_used"], it * PIECES - PIECES + (i + 1))
                            load(sp, it % NE, i, rest["piece"])

            @block.scalar
            def _(sc):
                with some(sc):
                    expert_act(sc, rest)

            @block.vector
            def _(ve):
                with some(ve):
                    expert_dve(ve, rest)

            @block.tensor
            def _(te):
                with some(te):
                    expert_pe(te, rest)

        x3_ready, p_sq, p_rs, p_ps, p_ev, g_ps, g_sig, g_used, o_ready, st_out = (
            sem(n) for n in ("x3_ready", "p_sq", "p_rs", "p_ps", "p_ev", "g_ps", "g_sig", "g_used", "o_ready", "st_out"))
        with nc.Block() as block:
            @block.gpsimd
            def _(pool):
                g = nc.gpsimd
                pool.wait_ge(p_sq, 1)
                g.tensor_scalar(rs, ssx, 1.0 / DM, EPS, ALU.mult, ALU.add).then_inc(p_rs, 1)
                pool.wait_ge(p_rs, 1)
                g.tensor_tensor(rs, rs, half[:, 0:2], ALU.pow).then_inc(p_rs, 1)

            @block.scalar
            def _(sc):
                a = nc.scalar
                for n in range(4):
                    sc.wait_ge(p_ps, n + 1)
                    for i in range(2):
                        kk = 2 * n + i
                        l = a.activation(x3T[:, kk, :], ps[n % 2][:, i * SEQ:(i + 1) * SEQ], ACT.Copy, scale=gT[:, 16 + kk:17 + kk])
                    l.then_inc(p_ev, 1)
                sc.wait_ge(p_rs, 2)
                for i in range(4):
                    sc.wait_ge(g_ps, i + 1)
                    if i >= 2:
                        sc.wait_ge(o_ready, i - 1)
                    a.activation(sgate[:, i % 2, :], ps[i][:, :], ACT.Sigmoid, scale=rs[:, i // 2:i // 2 + 1]).then_inc(g_sig, 1)

            @block.vector
            def _(ve):
                d = nc.vector
                for i in range(4):
                    t, n = i // 2, (i % 2) * 512
                    d.tensor_tensor(x[:, t, n:n + 512], x[:, t, n:n + 512], ps[4 + i][:, :], ALU.add).then_inc(x3_ready, 1)
                ve.wait_ge(x3_ready, 4)
                for t in range(TT):
                    l = d.tensor_tensor_reduce(out=xn3[:, t, :], in0=x[:, t, :], in1=x[:, t, :], scale=1.0, scalar=0.0,
                                               op0=ALU.mult, op1=ALU.add, accum_out=ssx[:, t:t + 1])
                l.then_inc(p_sq, 1)
                for i in range(4):
                    t, n = i // 2, (i % 2) * 512
                    ve.wait_ge(g_sig, i + 1)
                    d.tensor_tensor(sgate[:, i % 2, :], sgate[:, i % 2, :], pl[:, t, n:n + 512], ALU.mult).then_inc(g_used, 1)
                    ve.wait_ge(g_used, i + 1)
                    d.tensor_tensor(x[:, t, n:n + 512], x[:, t, n:n + 512], sgate[:, i % 2, :], ALU.add).then_inc(o_ready, 1)

            @block.tensor
            def _(te):
                mm, tr = nc.tensor.matmul, nc.tensor.transpose
                te.wait_ge(x3_ready, 4)
                for n in range(4):
                    if n >= 2:
                        te.wait_ge(p_ev, n - 1)
                    for i in range(2):
                        for t in range(TT):
                            l = tr(ps[n % 2][:, i * SEQ + t * P:i * SEQ + (t + 1) * P], x[:, t, (2 * n + i) * P:(2 * n + i + 1) * P], ident)
                    l.then_inc(p_ps, 1)
                te.wait_ge(p_ev, 4)
                te.wait_ge(ld_ple_gate, 32)
                for i in range(4):
                    t, n = i // 2, (i % 2) * 512
                    for k in range(KT):
                        l = mm(ps[i][:, :], x3T[:, k, t * P:(t + 1) * P], wple_g[:, k, n:n + 512], start=k == 0, stop=k == KT - 1)
                    l.then_inc(g_ps, 1)

            @block.sync
            def _(sp):
                for i in range(4):
                    t, n = i // 2, (i % 2) * 512
                    sp.wait_ge(o_ready, i + 1)
                    sp.dma_start(out[0, t * P:(t + 1) * P, n:n + 512], x[:, t, n:n + 512]).then_inc(st_out, 16)
                sp.wait_ge(st_out, 64)


def constants():
    c = np.zeros((P, 544), np.float32)
    c[:, 0:P] = np.eye(P)
    c[:, P:2 * P] = np.triu(np.ones((P, P)), 1)
    c[:, 2 * P:3 * P] = 1.0
    c[:, 3 * P:4 * P] = np.arange(P) % SLOTS + 1
    c[:, 4 * P:4 * P + NE] = (np.arange(P)[:, None] % NE) == np.arange(NE)[None, :]
    onehot = np.zeros((BUCKETS + 1, 384), np.float32)
    for j in range(384):
        n = 255 - j
        if n < 0:
            b = BUCKETS
        elif n < MAX_EXACT:
            b = n
        else:
            big = np.log(np.float32(n) / np.float32(MAX_EXACT)) / np.float32(math.log(MAX_DIST / MAX_EXACT))
            b = min(MAX_EXACT + int(big * np.float32(BUCKETS - MAX_EXACT)), BUCKETS - 1)
        onehot[b, j] = 1.0
    return {"consts": c, "onehot": onehot, "negrow": np.full((1, 16), NEG, np.float32)}


INS = ["x", "p", "w_in", "g_mix", "g_q_nsa", "g_k_nsa", "g_q_dsa", "g_k_dsa", "pe_ck", "w_ck1", "w_ck2", "pe_cv", "w_cv1", "w_cv2",
       "w_branch_a", "w_branch_b", "w_out", "rel_bias", "g_ffn", "w_router", "b_router", "w_e1", "b_e1", "w_e2", "b_e2", "g_ple",
       "w_ple", "w_ple_gate"]


def kernel(**inputs):
    import concourse.bacc as bacc
    from concourse.bass_utils import run_bass_kernel_spmd

    nc = bacc.Bacc("TRN2", target_bir_lowering=False, num_devices=1)
    arrays = {n: np.ascontiguousarray(inputs[n]) for n in INS}
    arrays.update(constants())
    io = {n: nc.dram_tensor(f"in_{n}", a.shape, mybir.dt.from_np(a.dtype), kind="ExternalInput").ap() for n, a in arrays.items()}
    out = nc.dram_tensor("out_0", (1, SEQ, DM), F32, kind="ExternalOutput").ap()
    block_kernel(nc, io, out)
    r = run_bass_kernel_spmd(nc, [{f"in_{n}": a for n, a in arrays.items()}], core_ids=[0])
    return r.results[0]["out_0"]
```
